# Optimizing a Trainium2 kernel written in Bass

```python
import math
import jax, jax.numpy as jnp
from jax import lax
import numpy as np

D_MODEL = 2048
BATCH = 1
SEQ = 256
DEPTH = 1

HEAD_DIM = 128
N_MIX_HEADS = D_MODEL // HEAD_DIM
A_HEADS = N_MIX_HEADS // 4
B_HEADS = (N_MIX_HEADS - A_HEADS) // 2
C_HEADS = N_MIX_HEADS - A_HEADS - B_HEADS
A_DK = HEAD_DIM
A_DV = HEAD_DIM
A_W = A_HEADS * A_DK
B_W = B_HEADS * HEAD_DIM
C_W = C_HEADS * HEAD_DIM
MIX_W = A_W + B_W + C_W
IN_SPLITS = [A_W, A_W, A_W, A_W, B_W, B_W, B_W, B_HEADS, C_W, C_W, C_W]
IN_COLS = sum(IN_SPLITS)
A_CHUNK = 64
B_Q_BLOCK = 128
C_BLOCK = 256
C_TOPK = 3
C_Q_BLOCK = 64
D_FF = 5632
CONV_W = 3
PLE_DIM = 256
EPS = 1e-6
TINY = 1e-30
NEG = -1e30


def rmsnorm(x, g):
    xf = x.astype(jnp.float32)
    y = xf * lax.rsqrt(jnp.mean(xf * xf, axis=-1, keepdims=True) + EPS)
    return (y * g.astype(jnp.float32)).astype(x.dtype)

def heads(t, n):
    b, s, _ = t.shape
    return t.reshape(b, s, n, -1).transpose(0, 2, 1, 3)

def merge_blocks(o):
    nqb, b, h, q, d = o.shape
    return o.transpose(1, 0, 3, 2, 4).reshape(b, nqb * q, h * d)

def alibi_slopes(n):
    return jnp.exp2(-8.0 * jnp.arange(1, n + 1, dtype=jnp.float32) / n)

def hgrn2_lower_bounds(lb_logits):
    sm = jax.nn.softmax(lb_logits.astype(jnp.float32), axis=0)
    return jnp.cumsum(sm, axis=0) - sm[0:1]

def hgrn2_mixer(q, f_logit, i, g, lb, o_norm_g):
    bsz, s, _ = q.shape
    dt = q.dtype
    z = f_logit.astype(jnp.float32)
    lbf = lb.astype(jnp.float32)
    f = lbf + (1.0 - lbf) * jax.nn.sigmoid(z)
    log_f = jnp.log(jnp.maximum(f, TINY))
    k = (1.0 - lbf) * jax.nn.sigmoid(-z)
    qh = heads(jax.nn.silu(q.astype(jnp.float32)), A_HEADS)
    kh = heads(k, A_HEADS)
    gh = heads(log_f, A_HEADS)
    vh = heads(i.astype(jnp.float32), A_HEADS)
    nc = s // A_CHUNK

    def chunks(t):
        return t.reshape(bsz, A_HEADS, nc, A_CHUNK, t.shape[-1]).transpose(2, 0, 1, 3, 4)

    causal = jnp.tril(jnp.ones((A_CHUNK, A_CHUNK), dtype=bool))[:, :, None]

    def step(state, xs):
        qc, kc, gc, vc = xs
        b = jnp.cumsum(gc, axis=2)
        o_inter = jnp.einsum('bhtd,bhde->bhte', qc * jnp.exp(b), state)
        diff = b[:, :, :, None, :] - b[:, :, None, :, :]
        decay = jnp.where(causal, jnp.exp(jnp.where(causal, diff, 0.0)), 0.0)
        attn = jnp.einsum('bhtd,bhsd,bhtsd->bhts', qc, kc, decay)
        o = o_inter + jnp.einsum('bhts,bhse->bhte', attn, vc)
        b_last = b[:, :, -1:, :]
        k_dec = kc * jnp.exp(b_last - b)
        state = jnp.exp(b_last[:, :, 0, :])[..., None] * state + jnp.einsum('bhsd,bhse->bhde', k_dec, vc)
        return state, o

    s0 = jnp.zeros((bsz, A_HEADS, A_DK, A_DV), jnp.float32)
    _, o = lax.scan(step, s0, (chunks(qh), chunks(kh), chunks(gh), chunks(vh)))
    o = o.transpose(1, 2, 0, 3, 4).reshape(bsz, A_HEADS, s, A_DV)
    o = rmsnorm(o, o_norm_g) * jax.nn.silu(heads(g.astype(jnp.float32), A_HEADS))
    return o.transpose(0, 2, 1, 3).reshape(bsz, s, A_W).astype(dt)

def fox_mixer(q, k, v, f_logit, b_f, qn_g, kn_g):
    bsz, s, _ = q.shape
    dt = q.dtype
    qh = rmsnorm(heads(q, B_HEADS), qn_g)
    kh = rmsnorm(heads(k, B_HEADS), kn_g)
    vh = heads(v, B_HEADS)
    log_f = jax.nn.log_sigmoid(f_logit.astype(jnp.float32) + b_f.astype(jnp.float32))
    fcum = jnp.cumsum(log_f, axis=1).transpose(0, 2, 1)
    nqb = s // B_Q_BLOCK
    qb = qh.reshape(bsz, B_HEADS, nqb, B_Q_BLOCK, HEAD_DIM).transpose(2, 0, 1, 3, 4)
    fq = fcum.reshape(bsz, B_HEADS, nqb, B_Q_BLOCK).transpose(2, 0, 1, 3)
    kpos = jnp.arange(s)
    scale = HEAD_DIM ** -0.5

    def block(xs):
        qi, fi, bi = xs
        qpos = bi * B_Q_BLOCK + jnp.arange(B_Q_BLOCK)
        logits = (jnp.einsum('bhqd,bhkd->bhqk', qi, kh).astype(jnp.float32) * scale
                  + fi[..., None] - fcum[:, :, None, :])
        logits = jnp.where(kpos[None, :] <= qpos[:, None], logits, NEG)
        w = jax.nn.softmax(logits, axis=-1).astype(dt)
        return jnp.einsum('bhqk,bhkd->bhqd', w, vh)

    o = lax.map(block, (qb, fq, jnp.arange(nqb)))
    return merge_blocks(o)

def moba_mixer(q, k, v, qn_g, kn_g, slopes):
    bsz, s, _ = q.shape
    dt = q.dtype
    h = C_HEADS
    qh = rmsnorm(heads(q, h), qn_g)
    kh = rmsnorm(heads(k, h), kn_g)
    vh = heads(v, h)
    nb = -(-s // C_BLOCK)
    s_pad = nb * C_BLOCK
    pad = ((0, 0), (0, 0), (0, s_pad - s), (0, 0))
    kp = jnp.pad(kh, pad)
    vp = jnp.pad(vh, pad)
    kblk = kp.reshape(bsz, h, nb, C_BLOCK, HEAD_DIM)
    vblk = vp.reshape(bsz, h, nb, C_BLOCK, HEAD_DIM)
    pos = jnp.arange(s)
    own = pos // C_BLOCK
    topk = min(C_TOPK, nb - 1)
    scale = HEAD_DIM ** -0.5
    kflat = kblk.reshape(bsz * h * nb, C_BLOCK, HEAD_DIM)
    vflat = vblk.reshape(bsz * h * nb, C_BLOCK, HEAD_DIM)
    bh_off = (jnp.arange(bsz * h, dtype=jnp.int32) * nb).reshape(bsz, h, 1, 1)
    blk_off = jnp.arange(C_BLOCK)
    sl = slopes[None, :, None, None]
    nqb = s // C_Q_BLOCK

    def to_blocks(t):
        t = t.reshape((bsz, h, nqb, C_Q_BLOCK) + t.shape[3:])
        return jnp.moveaxis(t, 2, 0)

    if topk > 0:
        kbar = jnp.mean(kblk.astype(jnp.float32), axis=3)
        gate = jnp.einsum('bhsd,bhnd->bhsn', qh.astype(jnp.float32), kbar)
        past = jnp.arange(nb)[None, :] < own[:, None]
        gate = jnp.where(past, gate, NEG)
        gval, gidx = lax.top_k(gate, topk)
        gvalid = gval > NEG / 2
        xs = (to_blocks(qh), jnp.arange(nqb), to_blocks(gidx), to_blocks(gvalid))
    else:
        xs = (to_blocks(qh), jnp.arange(nqb))

    def block(xs):
        qi, bi = xs[0], xs[1]
        qpos = bi * C_Q_BLOCK + jnp.arange(C_Q_BLOCK)
        start = (bi * C_Q_BLOCK // C_BLOCK) * C_BLOCK
        k_own = lax.dynamic_slice_in_dim(kp, start, C_BLOCK, axis=2)
        v_own = lax.dynamic_slice_in_dim(vp, start, C_BLOCK, axis=2)
        dist = (qpos[:, None] - (start + blk_off)[None, :]).astype(jnp.float32)
        s_own = jnp.einsum('bhqd,bhkd->bhqk', qi, k_own).astype(jnp.float32) * scale - sl * dist
        scores = [jnp.where(dist >= 0, s_own, NEG)]
        flats = []
        if topk > 0:
            idx, valid = xs[2], xs[3]
            flat = bh_off + idx
            for j in range(topk):
                fj = flat[..., j]
                flats.append(fj)
                kg = kflat[fj]
                kpos_g = idx[..., j][..., None] * C_BLOCK + blk_off
                dist_g = (qpos[None, None, :, None] - kpos_g).astype(jnp.float32)
                sj = jnp.einsum('bhqd,bhqkd->bhqk', qi, kg).astype(jnp.float32) * scale - sl * dist_g
                scores.append(jnp.where(valid[..., j][..., None], sj, NEG))
        w = jax.nn.softmax(jnp.concatenate(scores, axis=-1), axis=-1).astype(dt)
        out = jnp.einsum('bhqk,bhkd->bhqd', w[..., :C_BLOCK], v_own)
        for j, fj in enumerate(flats):
            vg = vflat[fj]
            wj = w[..., (j + 1) * C_BLOCK:(j + 2) * C_BLOCK]
            out = out + jnp.einsum('bhqk,bhqkd->bhqd', wj, vg)
        return out

    o = lax.map(block, xs)
    return merge_blocks(o)

def conv_ffn(x, w_gate, w_up, conv_w, conv_b, w_down):
    hg = x @ w_gate
    hg = lax.conv_general_dilated(hg, conv_w[:, None, :], window_strides=(1,),
                                  padding=[(CONV_W - 1, 0)],
                                  dimension_numbers=('NWC', 'WIO', 'NWC'),
                                  feature_group_count=hg.shape[-1]) + conv_b
    return (jax.nn.gelu(hg, approximate=True) * (x @ w_up)) @ w_down

def first_inputs(seed: int = 0) -> dict:
    key = jax.random.key(seed)
    ks = jax.random.split(key, 21)
    f32 = jnp.float32

    def nrm(k, shape, scale):
        return jax.random.normal(k, shape, f32) * scale

    return {
        "x": nrm(ks[0], (BATCH, SEQ, D_MODEL), 1.0),
        "p": nrm(ks[1], (DEPTH, BATCH, SEQ, PLE_DIM), 1.0),
        "attn_norm": 1.0 + nrm(ks[2], (DEPTH, D_MODEL), 0.02),
        "w_in": nrm(ks[3], (DEPTH, D_MODEL, IN_COLS), D_MODEL ** -0.5),
        "fox_bf": nrm(ks[4], (DEPTH, B_HEADS), 0.1),
        "lb_logits": nrm(ks[5], (DEPTH, A_W), 0.1),
        "hgrn_onorm": 1.0 + nrm(ks[6], (DEPTH, A_DV), 0.02),
        "fox_qnorm": 1.0 + nrm(ks[7], (DEPTH, HEAD_DIM), 0.02),
        "fox_knorm": 1.0 + nrm(ks[8], (DEPTH, HEAD_DIM), 0.02),
        "moba_qnorm": 1.0 + nrm(ks[9], (DEPTH, HEAD_DIM), 0.02),
        "moba_knorm": 1.0 + nrm(ks[10], (DEPTH, HEAD_DIM), 0.02),
        "w_out": nrm(ks[11], (DEPTH, MIX_W, D_MODEL), MIX_W ** -0.5),
        "ffn_norm": 1.0 + nrm(ks[12], (DEPTH, D_MODEL), 0.02),
        "w_gate": nrm(ks[13], (DEPTH, D_MODEL, D_FF), D_MODEL ** -0.5),
        "w_up": nrm(ks[14], (DEPTH, D_MODEL, D_FF), D_MODEL ** -0.5),
        "conv_w": nrm(ks[15], (DEPTH, CONV_W, D_FF), CONV_W ** -0.5),
        "conv_b": nrm(ks[16], (DEPTH, D_FF), 0.01),
        "w_down": nrm(ks[17], (DEPTH, D_FF, D_MODEL), D_FF ** -0.5),
        "ple_norm": 1.0 + nrm(ks[18], (DEPTH, D_MODEL), 0.02),
        "w_ple_gate": nrm(ks[19], (DEPTH, D_MODEL, D_MODEL), D_MODEL ** -0.5),
        "w_ple_proj": nrm(ks[20], (DEPTH, PLE_DIM, D_MODEL), PLE_DIM ** -0.5),
    }

def first_block(x, p, attn_norm, w_in, fox_bf, lb_logits, hgrn_onorm, fox_qnorm, fox_knorm,
              moba_qnorm, moba_knorm, w_out, ffn_norm, w_gate, w_up, conv_w, conv_b, w_down,
              ple_norm, w_ple_gate, w_ple_proj):
    lbs = hgrn2_lower_bounds(lb_logits)
    slopes = alibi_slopes(C_HEADS)
    split_idx = []
    acc = 0
    for n in IN_SPLITS[:-1]:
        acc += n
        split_idx.append(acc)
    h = x
    for i in range(DEPTH):
        a = rmsnorm(h, attn_norm[i])
        proj = a @ w_in[i]
        aq, af, ai, ag, bq, bk, bv, bf, cq, ck, cv = jnp.split(proj, split_idx, axis=-1)
        oa = hgrn2_mixer(aq, af, ai, ag, lbs[i], hgrn_onorm[i])
        ob = fox_mixer(bq, bk, bv, bf, fox_bf[i], fox_qnorm[i], fox_knorm[i])
        oc = moba_mixer(cq, ck, cv, moba_qnorm[i], moba_knorm[i], slopes)
        h = h + jnp.concatenate([oa, ob, oc], axis=-1) @ w_out[i]
        c = rmsnorm(h, ffn_norm[i])
        h = h + conv_ffn(c, w_gate[i], w_up[i], conv_w[i], conv_b[i], w_down[i])
        e = rmsnorm(h, ple_norm[i])
        h = h + jax.nn.sigmoid(e @ w_ple_gate[i]) * (p[i] @ w_ple_proj[i])
    return h


MIX_WIDTH = D_MODEL
ATTN_HEAD_DIM = 64
ATTN_WIDTH = MIX_WIDTH // 2
ATTN_HEADS = ATTN_WIDTH // ATTN_HEAD_DIM
DILATION_PATTERNS = ((128, 1), (512, 4), (2048, 16))
QBLK = 128
GLA_WIDTH = MIX_WIDTH - ATTN_WIDTH
GLA_HEADS = 4
GLA_KEY_WIDTH = GLA_WIDTH // 2
GLA_HEAD_DK = GLA_KEY_WIDTH // GLA_HEADS
GLA_HEAD_DV = GLA_WIDTH // GLA_HEADS
GLA_GATE_RANK = 16
GLA_GATE_TAU = 16.0
GLA_CHUNK = 64
FFN_HIDDEN = -(-(8 * D_MODEL) // (3 * 256)) * 256
REL_BUCKETS = 32
REL_MAX_DISTANCE = 1024
NORM_EPS = 1e-6
IN_SIZES = (ATTN_WIDTH, ATTN_WIDTH, ATTN_WIDTH,
            GLA_KEY_WIDTH, GLA_KEY_WIDTH, GLA_WIDTH, GLA_WIDTH, 2 * GLA_GATE_RANK)
IN_WIDTH = 3 * ATTN_WIDTH + 2 * GLA_KEY_WIDTH + 2 * GLA_WIDTH + 2 * GLA_GATE_RANK


def rmsnorm_2(x, w):
    x32 = x.astype(jnp.float32)
    y = x32 * lax.rsqrt(jnp.mean(x32 * x32, axis=-1, keepdims=True) + NORM_EPS)
    return y.astype(x.dtype) * w

def _t5_bucket(rel):
    nb = REL_BUCKETS // 2
    ret = np.where(rel > 0, nb, 0)
    n = np.abs(rel)
    max_exact = nb // 2
    large = max_exact + (np.log(np.maximum(n, 1) / max_exact)
                         / math.log(REL_MAX_DISTANCE / max_exact)
                         * (nb - max_exact)).astype(np.int64)
    large = np.minimum(large, nb - 1)
    return (ret + np.where(n < max_exact, n, large)).astype(np.int32)

def _band_layout(L, radius, dilation):
    nb = -(-L // QBLK)
    span = QBLK + 2 * radius
    key_idx = np.arange(nb)[:, None] * QBLK + np.arange(span)[None, :]
    kpos = key_idx - radius
    qpos = np.arange(nb)[:, None] * QBLK + np.arange(QBLK)[None, :]
    off = kpos[:, None, :] - qpos[:, :, None]
    valid = (np.abs(off) <= radius) & (kpos[:, None, :] >= 0) & (kpos[:, None, :] < L)
    bucket = _t5_bucket(off[0] * dilation)
    return nb, key_idx, valid, bucket

def _from_sub(t, L, S):
    B, H, r = t.shape[:3]
    rest = t.shape[5:]
    t = t.reshape((B, H, r, -1) + rest)[:, :, :, :L]
    t = jnp.swapaxes(t, 2, 3)
    return t.reshape((B, H, S) + rest)

def dilated_window_attention(q, k, v, rel_table, window, dilation):
    B, H, S, Dh = q.shape
    L = S // dilation
    R = (window // 2) // dilation
    nb, key_idx, valid, bucket = _band_layout(L, R, dilation)
    Lp = nb * QBLK

    def to_sub(t):
        return t.reshape(B, H, L, dilation, Dh).transpose(0, 1, 3, 2, 4)

    zpad = ((0, 0), (0, 0), (0, 0))
    qs = jnp.pad(to_sub(q), zpad + ((0, Lp - L), (0, 0)))
    ks = jnp.pad(to_sub(k), zpad + ((R, Lp - L + R), (0, 0)))
    vs = jnp.pad(to_sub(v), zpad + ((R, Lp - L + R), (0, 0)))
    qb = qs.reshape(B, H, dilation, nb, QBLK, Dh)
    kb = ks[:, :, :, key_idx]
    vb = vs[:, :, :, key_idx]

    bias = jnp.transpose(rel_table[bucket].astype(jnp.float32), (2, 0, 1))
    logits = (jnp.einsum('bhrnqd,bhrnkd->bhrnqk', qb, kb).astype(jnp.float32)
              * (Dh ** -0.5) + bias[None, :, None, None])
    logits = jnp.where(valid[None, None, None], logits, -1e30)
    m = jnp.max(logits, axis=-1, keepdims=True)
    p = jnp.exp(logits - m)
    s = jnp.sum(p, axis=-1, keepdims=True)
    o = jnp.einsum('bhrnqk,bhrnkd->bhrnqd', p, vb.astype(jnp.float32)) / s
    lse = (m + jnp.log(s))[..., 0]
    return _from_sub(o, L, S), _from_sub(lse, L, S)

def mixture_of_dilations(q, k, v, rel_table):
    outs, lses = [], []
    for window, dilation in DILATION_PATTERNS:
        o, l = dilated_window_attention(q, k, v, rel_table, window, dilation)
        outs.append(o)
        lses.append(l)
    w = jax.nn.softmax(jnp.stack(lses, axis=0), axis=0)
    out = sum(w[i][..., None] * outs[i] for i in range(len(outs)))
    return out

def gla_causal(q, k, v, log_a):
    B, H, S, Dk = q.shape
    Dv = v.shape[-1]
    n = S // GLA_CHUNK
    qc = q.astype(jnp.float32).reshape(B, H, n, GLA_CHUNK, Dk)
    kc = k.astype(jnp.float32).reshape(B, H, n, GLA_CHUNK, Dk)
    vc = v.astype(jnp.float32).reshape(B, H, n, GLA_CHUNK, Dv)
    G = jnp.cumsum(log_a.astype(jnp.float32).reshape(B, H, n, GLA_CHUNK, Dk), axis=-2)
    q_in = qc * jnp.exp(G)
    k_in = kc * jnp.exp(-G)
    tril = jnp.tril(jnp.ones((GLA_CHUNK, GLA_CHUNK), jnp.float32))
    A = jnp.einsum('bhncd,bhnjd->bhncj', q_in, k_in) * tril
    intra = jnp.einsum('bhncj,bhnjv->bhncv', A, vc)
    G_last = G[..., -1:, :]
    k_end = kc * jnp.exp(G_last - G)
    U = jnp.einsum('bhnjd,bhnjv->bhndv', k_end, vc)
    decay = jnp.exp(G_last[..., 0, :])

    def step(state, inp):
        dec, u = inp
        return state * dec[..., None] + u, state

    _, S_prev = lax.scan(step, jnp.zeros((B, H, Dk, Dv), jnp.float32),
                         (jnp.moveaxis(decay, 2, 0), jnp.moveaxis(U, 2, 0)))
    S_prev = jnp.moveaxis(S_prev, 0, 2)
    inter = jnp.einsum('bhncd,bhndv->bhncv', q_in, S_prev)
    return (intra + inter).reshape(B, H, S, Dv)

def _heads(t, n_heads):
    B, S, W = t.shape
    return t.reshape(B, S, n_heads, W // n_heads).transpose(0, 2, 1, 3)

def _merge_heads(t):
    B, H, S, Dh = t.shape
    return t.transpose(0, 2, 1, 3).reshape(B, S, H * Dh)

def second_inputs(seed: int = 0) -> dict:
    key = jax.random.key(seed)
    ks = jax.random.split(key, 16)
    f32 = jnp.float32
    nrm = lambda k, shape, scale: jax.random.normal(k, shape, f32) * scale
    return {
        "x": nrm(ks[0], (BATCH, SEQ, D_MODEL), 1.0),
        "attn_norm_w": 1.0 + nrm(ks[1], (DEPTH, D_MODEL), 0.02),
        "w_in": nrm(ks[2], (DEPTH, D_MODEL, IN_WIDTH), D_MODEL ** -0.5),
        "rel_bias_table": nrm(ks[3], (REL_BUCKETS, ATTN_HEADS), 0.3),
        "gla_gate_w_fwd": nrm(ks[4], (DEPTH, GLA_GATE_RANK, GLA_KEY_WIDTH), GLA_GATE_RANK ** -0.5),
        "gla_gate_b_fwd": nrm(ks[5], (DEPTH, GLA_KEY_WIDTH), 0.1),
        "gla_gate_w_bwd": nrm(ks[6], (DEPTH, GLA_GATE_RANK, GLA_KEY_WIDTH), GLA_GATE_RANK ** -0.5),
        "gla_gate_b_bwd": nrm(ks[7], (DEPTH, GLA_KEY_WIDTH), 0.1),
        "gla_norm_w": 1.0 + nrm(ks[8], (DEPTH, GLA_WIDTH), 0.02),
        "w_out": nrm(ks[9], (DEPTH, MIX_WIDTH, D_MODEL), MIX_WIDTH ** -0.5),
        "ffn_norm_w": 1.0 + nrm(ks[10], (DEPTH, D_MODEL), 0.02),
        "w_gate": nrm(ks[11], (DEPTH, D_MODEL, FFN_HIDDEN), D_MODEL ** -0.5),
        "w_up": nrm(ks[12], (DEPTH, D_MODEL, FFN_HIDDEN), D_MODEL ** -0.5),
        "w_down": nrm(ks[13], (DEPTH, FFN_HIDDEN, D_MODEL), FFN_HIDDEN ** -0.5),
        "final_norm_w": 1.0 + nrm(ks[14], (D_MODEL,), 0.02),
    }

def second_block(x, attn_norm_w, w_in, rel_bias_table, gla_gate_w_fwd, gla_gate_b_fwd,
              gla_gate_w_bwd, gla_gate_b_bwd, gla_norm_w, w_out, ffn_norm_w,
              w_gate, w_up, w_down, final_norm_w):
    split_idx = []
    acc = 0
    for size in IN_SIZES[:-1]:
        acc += size
        split_idx.append(acc)

    for l in range(DEPTH):
        h = rmsnorm_2(x, attn_norm_w[l])
        proj = h @ w_in[l]
        aq, ak, av, gq, gk, gv, gr, glr = jnp.split(proj, split_idx, axis=-1)

        attn = mixture_of_dilations(_heads(aq, ATTN_HEADS), _heads(ak, ATTN_HEADS),
                                    _heads(av, ATTN_HEADS), rel_bias_table)
        attn_out = _merge_heads(attn).astype(x.dtype)

        lr_f, lr_b = glr[..., :GLA_GATE_RANK], glr[..., GLA_GATE_RANK:]
        log_a_f = jax.nn.log_sigmoid((lr_f @ gla_gate_w_fwd[l] + gla_gate_b_fwd[l])
                                     .astype(jnp.float32)) / GLA_GATE_TAU
        log_a_b = jax.nn.log_sigmoid((lr_b @ gla_gate_w_bwd[l] + gla_gate_b_bwd[l])
                                     .astype(jnp.float32)) / GLA_GATE_TAU
        qh = _heads(gq, GLA_HEADS) * (GLA_HEAD_DK ** -0.5)
        kh = _heads(gk, GLA_HEADS)
        vh = _heads(gv, GLA_HEADS)
        fwd = gla_causal(qh, kh, vh, _heads(log_a_f, GLA_HEADS))
        flip = lambda t: jnp.flip(t, axis=2)
        bwd = flip(gla_causal(flip(qh), flip(kh), flip(vh), flip(_heads(log_a_b, GLA_HEADS))))
        o = fwd + bwd
        o = o * lax.rsqrt(jnp.mean(o * o, axis=-1, keepdims=True) + NORM_EPS)
        gla_out = (_merge_heads(o).astype(x.dtype) * gla_norm_w[l]) * jax.nn.silu(gr)

        mixed = jnp.concatenate([attn_out, gla_out], axis=-1) @ w_out[l]
        x = x + mixed

        h = rmsnorm_2(x, ffn_norm_w[l])
        x = x + (jax.nn.silu(h @ w_gate[l]) * (h @ w_up[l])) @ w_down[l]

    return rmsnorm_2(x, final_norm_w)


def setup_inputs(seed=0):
    out = dict(first_inputs(seed))
    for name, value in second_inputs(seed + 1).items():
        if name != "x":
            out[name + "_2"] = value
    return out


def reference(
    x, p, attn_norm, w_in, fox_bf, lb_logits, hgrn_onorm, fox_qnorm, fox_knorm, moba_qnorm,
    moba_knorm, w_out, ffn_norm, w_gate, w_up, conv_w, conv_b, w_down, ple_norm, w_ple_gate,
    w_ple_proj, attn_norm_w_2, w_in_2, rel_bias_table_2, gla_gate_w_fwd_2, gla_gate_b_fwd_2,
    gla_gate_w_bwd_2, gla_gate_b_bwd_2, gla_norm_w_2, w_out_2, ffn_norm_w_2, w_gate_2, w_up_2,
    w_down_2, final_norm_w_2,
):
    x = first_block(
        x, p, attn_norm, w_in, fox_bf, lb_logits, hgrn_onorm, fox_qnorm, fox_knorm, moba_qnorm,
        moba_knorm, w_out, ffn_norm, w_gate, w_up, conv_w, conv_b, w_down, ple_norm, w_ple_gate,
        w_ple_proj,
    )
    return second_block(
        x, attn_norm_w_2, w_in_2, rel_bias_table_2, gla_gate_w_fwd_2, gla_gate_b_fwd_2,
        gla_gate_w_bwd_2, gla_gate_b_bwd_2, gla_norm_w_2, w_out_2, ffn_norm_w_2, w_gate_2,
        w_up_2, w_down_2, final_norm_w_2,
    )


_drawn_inputs = setup_inputs


def setup_inputs(seed=0):
    import zlib

    import numpy as np

    out = dict(_drawn_inputs(seed))
    spreads = {}
    factors = {'attn_norm': 3.324,
     'fox_bf': 3.708,
     'hgrn_onorm': 7.82,
     'fox_qnorm': 8.0,
     'fox_knorm': 8.0,
     'moba_qnorm': 8.0,
     'moba_knorm': 8.0,
     'ffn_norm': 3.572,
     'conv_b': 8.0,
     'ple_norm': 200.0,
     'attn_norm_w_2': 4.369,
     'rel_bias_table_2': 13.458,
     'gla_gate_b_fwd_2': 6.519,
     'gla_gate_b_bwd_2': 6.834,
     'gla_norm_w_2': 22.958,
     'ffn_norm_w_2': 15.415,
     'final_norm_w_2': 22.344}
    for name, (base, spread) in spreads.items():
        noise = np.random.default_rng([zlib.crc32(name.encode()), seed]).standard_normal(out[name].shape)
        drawn = base * np.exp(spread * noise) if base else spread * noise
        out[name] = __import__('jax').numpy.asarray(drawn.astype(out[name].dtype))
    for name, factor in factors.items():
        out[name] = (out[name] * factor).astype(out[name].dtype)
    return out
```

```python
from contextlib import ExitStack
from math import log

import numpy as np

import concourse.bass as bass
from concourse import mybir

ALU = mybir.AluOpType
ACT = mybir.ActivationFunctionType
F32 = mybir.dt.float32
F32R = mybir.dt.float32r
I8 = mybir.dt.int8
AX_X = mybir.AxisListType.X

P = 128
T = 256
TB = T // P
D = 2048
KT = D // P
FF = 5632
W = 512
NG = FF // W
FT = W // P
EPS = 1e-6
NEG = -1e30
FAR = -1e34
LN_TINY = log(1e-30)
RAW = 4
SPL = 4
AHEAD = 3
HEADS_B = HEADS_C = 6
HEADS_2 = 16
LEVELS = (1, 2, 4, 8, 16, 32, 64)
GRP = 24
BUCKETS = 32
ND = 2 * T - 1


def shape_constants():
    i, j = np.arange(P)[:, None], np.arange(P)[None, :]
    cf = np.zeros((P, 3 * P + 768), np.float32)
    cf[:, 0:P] = i == j
    cf[:, P:2 * P] = i <= j
    cf[:, 2 * P:3 * P] = 1.0
    q = np.arange(P)[:, None]
    k0, k1 = np.arange(P)[None, :], np.arange(T)[None, :]
    dist = np.concatenate([k0 - q, k1 - q - P], axis=1)
    cf[:, 3 * P:3 * P + 384] = np.where(dist <= 0, 0.0, NEG)
    cf[:, 3 * P + 384:3 * P + 768] = np.where(dist <= 0, dist, FAR)
    masks = np.zeros((P, 15, P), np.float32)
    masks[:, 0] = i == j
    for n, size in enumerate(LEVELS):
        pair = (i // (2 * size) == j // (2 * size)) & (i // size % 2 == 0) & (j // size % 2 == 1)
        masks[:, 1 + n] = pair
        masks[:, 8 + n] = pair.T
    rel = T - 1 - np.arange(ND)
    nb = BUCKETS // 2
    n = np.abs(rel)
    exact = nb // 2
    large = exact + (np.log(np.maximum(n, 1) / exact) / log(1024 / exact) * (nb - exact)).astype(np.int64)
    bucket = np.where(rel > 0, nb, 0) + np.where(n < exact, n, np.minimum(large, nb - 1))
    times = (n <= 64) * 1 + (rel % 4 == 0) * 1 + (rel % 16 == 0) * 1
    hot = np.zeros((BUCKETS + 1, 512), np.float32)
    hot[bucket, np.arange(ND)] = 1.0
    hot[BUCKETS, :ND] = np.where(times > 0, np.log(np.maximum(times, 1)), NEG)
    return cf, masks.reshape(P, 15 * P), hot


class Panel:

    def __init__(self, weight, col, width, kts, per=2, row0=0, source="x"):
        self.weight, self.col, self.width, self.kts, self.per = weight, col, width, kts, per
        self.row0, self.source = row0, source
        self.chunks = len(kts) // per


def plan():
    full = list(range(KT))
    a0 = 0
    b0 = 4 * W
    c0 = b0 + 3 * HEADS_B * P + HEADS_B
    first = [Panel("w_in", b0 + 3 * HEADS_B * P, HEADS_B, full, per=KT)]
    first += [Panel("w_in", a0 + W * j, W, full) for j in range(4)]
    for base in (b0, c0):
        first += [Panel("w_in", base + HEADS_B * P * m + 384 * half, 384, full)
                  for half in range(2) for m in range(3)]
    out1 = [Panel("w_out", W * j, W, full[:12]) for j in range(4)]
    out1 += [Panel("w_out", W * j, W, full[12:]) for j in range(4)]
    ple = []
    for j in range(4):
        ple += [Panel("w_ple_proj", W * j, W, [0, 1], source="p"), Panel("w_ple_gate", W * j, W, full)]
    second = [Panel("w_in_2", 6144, 32, full, per=KT)]
    second += [Panel("w_in_2", c, W, full) for c in
               (3072, 3584, 4096, 4608, 5120, 5632, 0, 1024, 2048, 512, 1536, 2560)]
    out2 = [Panel("w_out_2", W * j, W, full[8:]) for j in range(4)]
    out2 += [Panel("w_out_2", W * j, W, full[:8]) for j in range(4)]
    return first, out1, ple, second, out2


def build(nc, g, out, const_f, const_m, hot):
    first, out1, ple, second, out2 = plan()
    straight = {}
    ends = {}
    n = q = 0

    def lay(panels):
        nonlocal n, q
        begin = n
        for p in panels:
            for j in range(p.chunks):
                straight[n] = (p, q, j)
                n += 1
            ends[n - 1] = q
            q += 1
        return begin, n

    IN1, IN1_END = lay(first)
    OUT1, OUT1_END = lay(out1)
    FFN1, FFN1_Q = n, q
    n += GRP * NG
    q += 6 * NG
    PLE, PLE_END = lay(ple)
    PLE_Q = straight[PLE][1]
    IN2, IN2_END = lay(second)
    IN2_Q = straight[IN2][1]
    OUT2, OUT2_END = lay(out2)
    OUT1_Q, OUT2_Q = straight[OUT1][1], straight[OUT2][1]
    FFN2, FFN2_Q = n, q
    n += GRP * NG
    TOTAL = n

    x_d = g["x"].rearrange("b (t p) d -> p (b t) d", p=P)
    out_d = out.rearrange("b (t p) d -> p (b t) d", p=P)
    wd = {k: (g[k].rearrange("a r c -> (a r) c")) for k in (
        "w_in", "w_out", "w_gate", "w_up", "w_down", "w_ple_gate", "w_ple_proj", "w_in_2", "w_out_2",
        "w_gate_2", "w_up_2", "w_down_2")}
    VEC_DMAS = 21
    bias_rows = nc.dram_tensor("bias_rows", [HEADS_2, 512], F32, kind="Internal").ap()

    with ExitStack() as ctx:
        def sb(name, shape, dt=F32, stack=ctx):
            return stack.enter_context(nc.sbuf_tensor(name, shape, dt))

        def sem(name):
            return ctx.enter_context(nc.semaphore(name))

        acc = ctx.enter_context(nc.psum_tensor("acc", [P, 4, 512], F32))
        mb = ctx.enter_context(nc.psum_tensor("mb", [P, 4, 512], F32))

        raw = sb("raw", [P, RAW, 2 * W])
        w_hi = sb("w_hi", [P, SPL, 2 * W], F32R)
        w_lo = sb("w_lo", [P, SPL, 2 * W], F32R)
        x_hi = sb("x_hi", [P, KT, T], F32R)
        x_lo = sb("x_lo", [P, KT, T], F32R)
        h = sb("h", [P, TB, D])
        cf = sb("cf", [P, 3 * P])
        ident, upto, ones = cf[:, 0:P], cf[:, P:2 * P], cf[:, 2 * P:3 * P]
        masks = sb("masks", [P, 15, P], I8)
        NV = 5 * KT + 1 + 4 + 8 + 8
        vecs = sb("vecs", [P, NV])
        NORM = [vecs[:, KT * j:KT * (j + 1)] for j in range(5)]
        V0 = 5 * KT
        hgrn_gain = vecs[:, V0:V0 + 1]
        qk_gain = [vecs[:, V0 + 1 + j:V0 + 2 + j] for j in range(4)]
        gate_bias = [vecs[:, V0 + 5 + 4 * d:V0 + 9 + 4 * d] for d in range(2)]
        gla_gain = vecs[:, V0 + 13:V0 + 21]
        conv = sb("conv", [P, 4, 44])
        small = sb("small", [P, 96])
        half = small[:, 0:1]
        ssq = small[:, 2:4]
        rstd = small[:, 4:6]
        hsq, hrs = small[:, 8:16], small[:, 16:24]
        full01 = small[:, 24:32]
        negmax, rowsum, rowinv = small[:, 32:36], small[:, 36:40], small[:, 40:44]
        fbias = small[:, 44:50]
        lf = small[:, 52:64].rearrange("p (t h) -> p t h", t=2)
        nlf = small[:, 64:76].rearrange("p (t h) -> p t h", t=2)
        fcum = small[:, 76:88].rearrange("p (t h) -> p t h", t=2)
        scanm = sb("scanm", [P, T])


        with ExitStack() as s1:
            tail = sb("tail", [P, TB, HEADS_B], F32, s1)
            a_reg = sb("a_reg", [P, 4, 1024], F32, s1)
            bc_reg = sb("bc_reg", [P, 12, 768], F32, s1)
            AT1 = sb("AT1", [P, 4, TB, T], F32, s1)
            X1 = sb("X1", [P, 2, 512], F32, s1)
            LG1 = sb("LG1", [P, 1024], F32, s1)
            B1 = sb("B1", [P, 1024], F32, s1)
            L1 = sb("L1", [P, 2, 512], F32, s1)
            WT1 = sb("WT1", [P, 2, 512], F32, s1)
            causal = sb("causal", [P, 384], F32, s1)
            alibi = sb("alibi", [P, 384], F32, s1)
            stage = sb("stage", [P, 3, P], F32, s1)
            masks_f = sb("masks_f", [P, 15, P], F32, s1)
            table = sb("table", [BUCKETS + 1, HEADS_2], F32, s1)
            hot_sb = sb("hot_sb", [BUCKETS + 1, 512], F32, s1)
            rows_sb = sb("rows_sb", [HEADS_2, 512], F32, s1)
        with ExitStack() as s2:
            h_hi = sb("h_hi", [P, FT, T], F32R, s2)
            h_lo = sb("h_lo", [P, FT, T], F32R, s2)
            gate_n = sb("gate_n", [P, TB, W], F32, s2)
            up_n = sb("up_n", [P, TB, W], F32, s2)
            cv = sb("cv", [P, FT, T], F32, s2)
            pn = sb("pn", [P, TB, W], F32, s2)
            hn = sb("hn", [P, TB, D], F32, s2)
            p_in = sb("p_in", [P, TB, 256], F32, s2)
            p_hi = sb("p_hi", [P, 2, T], F32R, s2)
            p_lo = sb("p_lo", [P, 2, T], F32R, s2)
            fin_g = sb("fin_g", [P, D], F32, s2)
        with ExitStack() as s3:
            tail2 = sb("tail2", [P, TB, 32], F32, s3)
            reg2 = sb("reg2", [P, 12, 1024], F32, s3)
            Z = sb("Z", [P, HEADS_2, 384], F32, s3)
            AT2 = sb("AT2", [P, 4, TB, T], F32, s3)
            X2 = sb("X2", [P, 2, 512], F32, s3)
            BF2 = sb("BF2", [P, 1024], F32, s3)
            BB2 = sb("BB2", [P, 1024], F32, s3)
            L2 = sb("L2", [P, 2, 512], F32, s3)
            WT2 = sb("WT2", [P, 2, 512], F32, s3)
            lr_t = L2[0:16, :, 0:T]
            gate_w = WT2[0:16, :, :]

        raw_in = [sem(f"raw_in{s}") for s in range(RAW)]
        hi_ready = sem("hi_ready")
        lo_ready = sem("lo_ready")
        mm_done = sem("mm_done")
        panel_out = [sem("panel_out_even"), sem("panel_out_odd")]
        x_in, const_in, vec_in = sem("x_in"), sem("const_in"), sem("vec_in")
        pool_set, table_one = sem("pool_set"), sem("table_one")
        vec_turned, vec_out, rows_made, rows_out, rows_kept = (
            sem("vec_turned"), sem("vec_out"), sem("rows_made"), sem("rows_out"), sem("rows_kept"))
        sq_act, sq_dve, h_done = sem("sq_act"), sem("sq_dve"), sem("h_done")
        rstd_ready, hn_act, hn_dve = sem("rstd_ready"), sem("hn_act"), sem("hn_dve")
        hn_turned, xhi_ready, xlo_ready = sem("hn_turned"), sem("xhi_ready"), sem("xlo_ready")
        gate_turned, conv_begun, conv_first, conv_done = (
            sem("gate_turned"), sem("conv_begun"), sem("conv_first"), sem("conv_done"))
        gelu_done, up_turned, prod_done = sem("gelu_done"), sem("up_turned"), sem("prod_done")
        hhi_ready, hlo_ready = sem("hhi_ready"), sem("hlo_ready")
        p_landed, p_turned, phi_ready, plo_ready = (
            sem("p_landed"), sem("p_turned"), sem("phi_ready"), sem("plo_ready"))
        ple_sig_out = sem("ple_added")
        dq_turned, dq_out, dk_turned, dk_out = sem("dq_turned"), sem("dq_out"), sem("dk_turned"), sem("dk_out")
        log1p_out, logf_out, decay_out = sem("log1p_out"), sem("logf_out"), sem("decay_out")
        lr_turned, lr_out, gates_made, gate_w_in = sem("lr_turned"), sem("lr_out"), sem("gates_made"), sem("gate_w_in")
        expo_out, exp_out, x_out, pair_made, pair_kept = (
            sem("expo_out"), sem("exp_out"), sem("x_out"), sem("pair_made"), sem("pair_kept"))
        at_zero, o_made, o_out, og_out, osq_out, orstd, o_scaled, o_turned, o_kept = (
            sem("at_zero"), sem("o_made"), sem("o_out"), sem("og_out"), sem("osq_out"), sem("orstd"),
            sem("o_scaled"), sem("o_turned"), sem("o_kept"))
        forget_exp, forget_out, fcum_made, fcum_out = (
            sem("forget_exp"), sem("forget_out"), sem("fcum_made"), sem("fcum_out"))
        prep_sq, prep_rstd, prep_scaled, prep_turned, prep_out = (
            sem("prep_sq"), sem("prep_rstd"), sem("prep_scaled"), sem("prep_turned"), sem("prep_out"))
        scores_made, logits_out, exps_out, probs_out, probs_turned, probs_kept, head_made, head_out = (
            sem("scores_made"), sem("logits_out"), sem("exps_out"), sem("probs_out"),
            sem("probs_turned"), sem("probs_kept"), sem("head_made"), sem("head_out"))
        z_in = sem("z_in")
        ohi_ready, olo_ready = sem("ohi_ready"), sem("olo_ready")
        fin_in, fin_done, out_stored = sem("fin_in"), sem("fin_done"), sem("out_stored")
        act_link, dve_link, pool_link = sem("act_link"), sem("dve_link"), sem("pool_link")

        HG = dict(turn_q=9, turn_f=17, levels=20, make_o=56)
        PREP1 = {5: 62, 6: 64, 8: 66, 9: 74, 11: 99, 12: 101, 14: 117, 15: 121}
        HEAD1 = [78 + 3 * i for i in range(6)] + [106, 109, 112, 129, 131, 133]
        b = IN2
        PREP2 = {7: b + 76, 8: b + 77, 10: b + 97, 11: b + 98}
        HEAD2 = [b + 79 + 2 * i for i in range(8)] + [b + 100 + i for i in range(8)]
        OSPLIT = {IN1_END - 1: range(0, 6), OUT1 + 22: range(6, 8),
                  IN2_END - 1: range(8, 12), OUT2 + 15: range(12, 16)}
        NORM_AT = {FFN1 - 1: 1, PLE - 1: 2, IN2 - 1: 3, FFN2 - 1: 4}
        LEVELS1 = [(0, hp, lv) for hp in range(2) for lv in range(8)]
        LEVELS2 = [(d, hp, lv) for d in range(2) for hp in range(2) for lv in range(8)]

        def level_slot(block, j):
            return HG["levels"] + 2 * j if block == 0 else IN2 + 19 + 3 * j // 2

        def chunk_of(value, i):
            return value if i is None else i * GRP + value

        def grown(value, i, step):
            return value if i is None else i * step + value

        def cut(buf, slot, per, width):
            return buf[:, slot, 0:per * width].rearrange("p (k n) -> p k n", k=per)

        def shape_of(n):
            if n in straight:
                return straight[n][0].per, straight[n][0].width
            return 2, W

        def panel_in(t, q):
            return acc[:, 2 * (q % 2) + t, :]

        def region(q):
            j = q if q < IN2_Q else q - IN2_Q
            if q < IN2_Q:
                r = a_reg[:, j - 1, :] if j <= 4 else bc_reg[:, j - 5, :]
            else:
                r = reg2[:, j - 1, :]
            wide = 384 if q < IN2_Q and j > 4 else W
            return r.rearrange("p (t n) -> p t n", t=TB), r.rearrange("p (k t) -> p k t", t=T), wide // P

        def o_turned_at(kt, block):
            if block == 0:
                if kt < 4:
                    return a_reg[:, 3, T * kt:T * kt + T]
                hh = kt - 4
                return bc_reg[:, 6 * (hh // 6) + 3 * (hh % 6 // 3), T * (hh % 3):T * (hh % 3) + T]
            if kt >= 8:
                return reg2[:, 4 + (kt - 8) // 4, T * (kt % 4):T * (kt % 4) + T]
            return reg2[:, 6 + 3 * (kt // 4), T * (kt % 4):T * (kt % 4) + T]

        def head(u):
            if u < 12:
                base, s = 6 * (u // 6) + 3 * (u % 6 // 3), T * (u % 3)
                v = bc_reg[:, base + 2, :].rearrange("p (t n) -> p t n", t=TB)[:, :, P * (u % 3):P * (u % 3) + P]
                return bc_reg[:, base, s:s + T], bc_reg[:, base + 1, s:s + T], v, bc_reg[:, base, s:s + T], P
            e = u - 12
            base, s, lo = 6 + 3 * (e // 8), T * (e % 8 // 2), 64 * (e % 2)
            v = reg2[:, base + 2, :].rearrange("p (t n) -> p t n", t=TB)[:, :, 64 * (e % 8):64 * (e % 8) + 64]
            q = reg2[lo:lo + 64, base, s:s + T]
            return q, reg2[lo:lo + 64, base + 1, s:s + T], v, q, 64

        LOGITS = [((0, 128), (128, 256)), ((0, 256), (256, 256))]

        block = ctx.enter_context(nc.Block())

        @block.sync
        def _(sp):
            sp.dma_start(h[:, :, :], x_d).then_inc(x_in, 16)

            def load(n, base, i, src, per, width):
                if i is not None or base >= RAW:
                    sp.wait_ge(lo_ready, n - (RAW - 1))
                sp.dma_start(cut(raw, base % RAW, per, width),
                             src.rearrange("(k p) n -> p k n", p=P)).then_inc(raw_in[base % RAW], 16)

            def load_straight(a, z):
                for n in range(a, z):
                    p, _, j = straight[n]
                    rows = (p.kts[0] + j * p.per) * P
                    load(n, n, None, wd[p.weight][rows:rows + p.per * P, p.col:p.col + p.width], p.per, p.width)

            def load_ffn(base, gate, up, down):
                def group(i, first, last):
                    at = base + (16 if not first else 0)
                    col = 0 if i is None else i * W + W
                    prev = (NG - 1) * W if last else (i * W if i is not None else None)
                    for c in range(16 if first else GRP):
                        if last and c < 16:
                            continue
                        cc = c
                        b0 = at + c
                        if last:
                            b0 = base + 16 + (NG - 1) * GRP + c - 16
                        n = chunk_of(b0, i)
                        if c < 16:
                            wsrc = wd[gate if c < 8 else up]
                            src = wsrc[(cc % 8) * 2 * P:(cc % 8 + 1) * 2 * P, bass.ds(col, W)]
                        else:
                            row = prev + (c % 2) * 2 * P
                            src = wd[down][bass.ds(row, 2 * P), (c - 16) // 2 * W:((c - 16) // 2 + 1) * W]
                        load(n, b0, i, src, 2, W)

                group(None, True, False)
                with sp.Fori(0, NG - 1) as i:
                    group(i, False, False)
                group(None, False, True)

            load_straight(IN1, FFN1)
            load_ffn(FFN1, "w_gate", "w_up", "w_down")
            load_straight(PLE, FFN2)
            load_ffn(FFN2, "w_gate_2", "w_up_2", "w_down_2")
            sp.wait_ge(fin_done, 2)
            sp.dma_start(out_d, hn[:, :, :]).then_inc(out_stored, 16)
            sp.wait_ge(out_stored, 16)

        @block.gpsimd
        def _(pool):
            links = [0]

            def link(ins):
                links[0] += 1
                ins.then_inc(pool_link, 1)
                pool.wait_ge(pool_link, links[0])

            pool.memset(small[:, 0:1], -0.5).then_inc(pool_set, 1)
            pool.memset(scanm[:, :], 1.0).then_inc(pool_set, 1)
            pool.memset(table[:, :], 1.0).then_inc(table_one, 1)
            pool.wait_ge(pool_set, 2)
            pool.memset(scanm[:, 0:T:64], 0.0).then_inc(pool_set, 1)
            pool.memset(AT1[:, :, :, :], 0.0).then_inc(at_zero, 1)

            def inverse_root(to, sums, count, done):
                link(pool.tensor_scalar(to, sums, 1.0 / count, EPS, ALU.mult, ALU.add))
                pool.tensor_tensor(to, to, small[:, 0:1].to_broadcast([P, to.shape[1]]), ALU.pow).then_inc(done, 1)

            def norm(i):
                pool.wait_ge(sq_act, i + 1)
                pool.wait_ge(sq_dve, i + 1)
                inverse_root(rstd, ssq, D, rstd_ready)

            norm(0)
            pool.wait_ge(osq_out, 1)
            inverse_root(hrs, hsq, P, orstd)
            for j in range(len(PREP1)):
                pool.wait_ge(prep_sq, j + 1)
                inverse_root(hrs[:, 0:6], hsq[:, 0:6], P, prep_rstd)
            norm(1)
            norm(2)
            norm(3)
            pool.wait_ge(xlo_ready, 32)
            pool.memset(AT2[:, :, :, :], 0.0).then_inc(at_zero, 1)
            pool.wait_ge(osq_out, 2)
            inverse_root(hrs, hsq, T, orstd)
            norm(4)
            norm(5)

        @block.tensor
        def _(pe):
            def turn(out, in_):
                return pe.transpose(out, in_, ident)

            def multiply(n, base, i, per, width, kts, hi, lo, pair, first, last):
                pe.wait_ge(lo_ready, n + 1)
                wh, wl = cut(w_hi, base % SPL, per, width), cut(w_lo, base % SPL, per, width)
                for k in range(per):
                    for t in range(TB):
                        to = acc[:, 2 * pair + t, 0:width]
                        s = slice(P * t, P * t + P)
                        for m, (xx, ww) in enumerate(((hi, wh), (hi, wl), (lo, wh))):
                            mm = pe.matmul(to, xx[:, kts[k], s], ww[:, k, :], start=first and k == 0 and m == 0,
                                           stop=last and k == per - 1 and m == 2)
                mm.then_inc(mm_done, 1)

            def norm(i):
                pe.wait_ge(hn_act, i + 1)
                pe.wait_ge(hn_dve, i + 1)
                for j in range(KT // 2):
                    if j >= 4:
                        pe.wait_ge(xlo_ready, 8 * i + j - 3)
                    for k in range(2):
                        for t in range(TB):
                            kt = 2 * j + k
                            mm = turn(mb[:, j % 4, T * k + P * t:T * k + P * t + P], hn[:, t, P * kt:P * kt + P])
                    mm.then_inc(hn_turned, 1)

            def turn_panel(src, banks, tiles, done):
                for k in range(tiles):
                    for t in range(TB):
                        at = T * k + P * t
                        mm = turn(mb[:, banks + at // 512, at % 512:at % 512 + P], src[:, t, P * k:P * k + P])
                mm.then_inc(done, 1)

            def pair_levels(block, j):
                steps = LEVELS1 if block == 0 else LEVELS2
                d, hp, lv = steps[j]
                k = j + (16 if block else 0)
                X = (X1 if block == 0 else X2)[:, k % 2, :].rearrange("p (h t) -> p h t", h=2)
                pe.wait_ge(x_out, k + 1)
                if j >= 2:
                    pe.wait_ge(pair_kept, (17 if block else 0) + j)
                for e in range(2):
                    if lv == 7:
                        ks, qs = (0, P) if d == 0 else (P, 0)
                        mm = pe.matmul(mb[:, k % 2, P * e:P * e + P], X[:, e, ks:ks + P], X[:, e, qs:qs + P],
                                       start=True, stop=True)
                    else:
                        for t in range(TB):
                            s = slice(P * t, P * t + P)
                            mm = pe.matmul(mb[:, k % 2, 256 * e + P * t:256 * e + P * t + P], X[:, e, s], X[:, e, s],
                                           start=True, stop=True)
                mm.then_inc(pair_made, 1)

            def diagonal(block):
                q, k = (a_reg[:, 0, :], a_reg[:, 1, :]) if block == 0 else (reg2[:, 0, :], reg2[:, 1, :])
                for e in range(4):
                    for t in range(TB):
                        s = slice(T * e + P * t, T * e + P * t + P)
                        to = mb[:, 2 + e // 2, 256 * (e % 2) + P * t:256 * (e % 2) + P * t + P]
                        for again in range(block + 1):
                            mm = pe.matmul(to, k[:, s], q[:, s], start=again == 0, stop=again == block)
                mm.then_inc(pair_made, 1)

            def make_o(block):
                AT = AT1 if block == 0 else AT2
                dv = P if block == 0 else T
                pe.wait_ge(pair_kept, 17 if block == 0 else 50)
                for t in range(TB):
                    for e in range(4):
                        to = mb[:, t, P * e:P * e + P] if block == 0 else mb[:, 2 * t + e // 2, T * (e % 2):T * (e % 2) + T]
                        srcs = [s for s in range(TB) if block == 1 or s <= t]
                        for s in srcs:
                            if block == 0:
                                v = a_reg[:, 2, :].rearrange("p (t n) -> p t n", t=TB)[:, s, P * e:P * e + P]
                            else:
                                v = reg2[:, 2 + e // 2, :].rearrange("p (t n) -> p t n", t=TB)[:, s, T * (e % 2):T * (e % 2) + T]
                            mm = pe.matmul(to, AT[:, e, s, P * t:P * t + P], v, start=s == srcs[0], stop=s == srcs[-1])
                mm.then_inc(o_made, 1)

            def scores(u):
                q, k, _, _, rows = head(u)
                to = mb[:, u % 2, :]
                if u >= 2:
                    pe.wait_ge(logits_out, u - 1)
                fox = u < HEADS_B
                second = u >= 12
                for t, (c, keys) in enumerate(LOGITS[second]):
                    mm = pe.matmul(to[:, c:c + keys], q[:, P * t:P * t + P], k[:, 0:keys], start=True, stop=not fox)
                    if fox:
                        for s in range(t + 1):
                            row = nlf[:, s, u:u + 1].to_broadcast([P, P])
                            if s < t:
                                pe.matmul(to[:, c + P:c + 2 * P], row, ones, start=False, stop=False)
                            mm = pe.matmul(to[:, c + P * s:c + P * s + P], row, upto, start=False, stop=s == t)
                return mm

            def turn_probs(u):
                second = u >= 12
                L = (L2 if second else L1)[:, u % 2, :]
                pe.wait_ge(probs_out, u + 1)
                if u >= 2:
                    pe.wait_ge(head_out, u - 1)
                to = mb[:, 2 + u % 2, :]
                if second:
                    spots = [(0, 0), (P, T), (T, P), (T + P, T + P)]
                else:
                    spots = [(0, 0), (P, P), (2 * P, T)]
                for src, dst in spots:
                    mm = turn(to[:, dst:dst + P], L[:, src:src + P])
                mm.then_inc(probs_turned, 1)

            def head_values(u):
                _, _, v, _, rows = head(u)
                second = u >= 12
                WT = (WT2 if second else WT1)[:, u % 2, :]
                lo = 64 * (u % 2) if second else 0
                to = mb[lo:lo + rows, 2 + u % 2, :]
                pe.wait_ge(probs_kept, u + 1)
                pe.matmul(to[:, 0:T], v[:, 0, :], WT[:, 0:T], start=True, stop=False)
                if second:
                    mm = pe.matmul(to[:, 0:T], v[:, 1, :], WT[:, T:2 * T], start=False, stop=True)
                else:
                    mm = pe.matmul(to[:, P:T], v[:, 1, :], WT[:, T:T + P], start=False, stop=True)
                mm.then_inc(head_made, 1)

            def head_steps(n, slots, u0):
                for i, s in enumerate(slots):
                    u = u0 + i
                    if n == s:
                        if u == 0:
                            pe.wait_ge(prep_out, 4)
                            pe.wait_ge(fcum_out, 1)
                        if u == 6:
                            pe.wait_ge(prep_out, 6)
                        if u == 9:
                            pe.wait_ge(prep_out, 8)
                        if u == 12:
                            pe.wait_ge(prep_out, 10)
                        if u == 20:
                            pe.wait_ge(prep_out, 12)
                        scores(u).then_inc(scores_made, 1)
                    if n == s + 2:
                        turn_probs(u)
                    if n == s + 3:
                        head_values(u)

            def beside(n):
                if n == 1:
                    pe.wait_ge(forget_out, 1)
                    pe.matmul(mb[:, 3, 0:6], upto, lf[:, 0, :], start=True, stop=True)
                    pe.matmul(mb[:, 3, 6:12], ones, lf[:, 0, :], start=True, stop=False)
                    pe.matmul(mb[:, 3, 6:12], upto, lf[:, 1, :], start=False, stop=True).then_inc(fcum_made, 1)
                if n == HG["turn_q"]:
                    pe.wait_ge(panel_out[1], 1)
                    turn_panel(region(1)[0], 0, 4, dq_turned)
                if n == HG["turn_f"]:
                    pe.wait_ge(panel_out[0], 2)
                    pe.wait_ge(fcum_out, 1)
                    turn_panel(region(2)[0], 2, 4, dk_turned)
                if n == HG["levels"] - 1:
                    pe.wait_ge(dk_out, 1)
                    diagonal(0)
                for j in range(len(LEVELS1)):
                    if n == level_slot(0, j) + 2:
                        pair_levels(0, j)
                if n == HG["make_o"]:
                    make_o(0)
                if n == HG["make_o"] + 4:
                    pe.wait_ge(o_scaled, 1)
                    turn_panel(LG1[:, :].rearrange("p (t n) -> p t n", t=TB), 2, 4, o_turned)
                for j, (panel, s) in enumerate(PREP1.items()):
                    if n == s + 2:
                        pe.wait_ge(prep_scaled, j + 1)
                        if j:
                            pe.wait_ge(prep_out, j)
                        if j in (4, 6):
                            pe.wait_ge(head_out, 6 if j == 4 else 9)
                        turn_panel(region(panel)[0], 0, 3, prep_turned)
                head_steps(n, HEAD1, 0)

                if n == IN2 + 1:
                    for d in range(2):
                        for t in range(TB):
                            if d == 0 and t == 0:
                                pe.wait_ge(panel_out[IN2_Q % 2], IN2_Q // 2 + 1)
                            mm = turn(mb[0:16, 0, T * d + P * t:T * d + P * t + P], tail2[:, t, 16 * d:16 * d + 16])
                    mm.then_inc(lr_turned, 1)
                if n == IN2 + 3:
                    pe.wait_ge(lr_out, 1)
                    pe.wait_ge(gate_w_in, 32)
                    for d in range(2):
                        for e in range(4):
                            mm = pe.matmul(mb[:, 2 * d + e // 2, T * (e % 2):T * (e % 2) + T],
                                           gate_w[:, d, P * e:P * e + P], lr_t[:, d, :], start=True, stop=True)
                    mm.then_inc(gates_made, 1)
                if n == IN2 + 9:
                    pe.wait_ge(panel_out[(IN2_Q + 1) % 2], (IN2_Q + 1) // 2 + 1)
                    pe.wait_ge(log1p_out, 4)
                    turn_panel(region(IN2_Q + 1)[0], 0, 4, dq_turned)
                if n == IN2 + 17:
                    pe.wait_ge(panel_out[(IN2_Q + 2) % 2], (IN2_Q + 2) // 2 + 1)
                    turn_panel(region(IN2_Q + 2)[0], 2, 4, dk_turned)
                if n == IN2 + 18:
                    pe.wait_ge(dk_out, 2)
                    pe.wait_ge(dq_out, 2)
                    diagonal(1)
                for j in range(len(LEVELS2)):
                    if n == level_slot(1, j) + 2:
                        pair_levels(1, j)
                if n == IN2 + 70:
                    make_o(1)
                if n == IN2 + 74:
                    pe.wait_ge(o_scaled, 2)
                    src = reg2[:, 0:2, :].rearrange("p r n -> p (r n)").rearrange("p (t n) -> p t n", t=TB)
                    turn_panel(src, 0, 8, o_turned)
                for j, (panel, s) in enumerate(PREP2.items()):
                    if n == s:
                        pe.wait_ge(panel_out[(IN2_Q + panel) % 2], (IN2_Q + panel) // 2 + 1)
                        if j == 0:
                            pe.wait_ge(o_kept, 2)
                        if j == 2:
                            pe.wait_ge(head_out, 20)
                        turn_panel(region(IN2_Q + panel)[0], 2 * (j % 2), 4, prep_turned)
                head_steps(n, HEAD2, 12)
                if n in NORM_AT:
                    norm(NORM_AT[n])
                if n == PLE - 1:
                    pe.wait_ge(p_landed, 16)
                    pe.wait_ge(xlo_ready, 8 * 3)
                    turn_panel(p_in, 0, 2, p_turned)

            def straight_part(a, z):
                for n in range(a, z):
                    p, q, j = straight[n]
                    if j == 0 and q >= 2:
                        pe.wait_ge(panel_out[q % 2], q // 2)
                    hi, lo, kts = x_hi, x_lo, [k for k in p.kts[j * p.per:(j + 1) * p.per]]
                    if p.source == "p":
                        hi, lo = p_hi, p_lo
                        pe.wait_ge(plo_ready, 1)
                    elif p.weight.startswith("w_out"):
                        done = (kts[0] // 2 if p.weight == "w_out" else 8 + (kts[0] // 2 + 4) % 8) + 1
                        pe.wait_ge(olo_ready, done)
                    elif q in (0, IN2_Q) or q == PLE_Q + 1:
                        first_norm = {0: 0, IN2_Q: 3, PLE_Q + 1: 2}[q]
                        pe.wait_ge(xlo_ready, 8 * first_norm + kts[-1] // 2 + 1)
                    multiply(n, n, None, p.per, p.width, kts, hi, lo, q % 2, j == 0, j == p.chunks - 1)
                    beside(n)

            def ffn_part(which, base, base_q):
                norm_no = 1 if which == 0 else 4
                groups = NG * which

                def group(i, first, last):
                    if not last:
                        at = base if first else base + 16
                        qq = base_q if first else base_q + 2
                    else:
                        at, qq = base + 16 + (NG - 1) * GRP - 16, base_q + 2 + 6 * (NG - 1) - 2
                    number = grown(groups + (0 if first else 1), i, 1)
                    for c in range(16 if last else 0, 16 if first else GRP):
                        par = (qq + (c // 8 if c < 16 else 2 + (c - 16) // 2)) % 2
                        part = c // 8 if c < 16 else 2 + (c - 16) // 2
                        begins = c % 8 == 0 if c < 16 else c % 2 == 0
                        if begins:
                            pe.wait_ge(panel_out[par], grown((qq + part) // 2, i, 3))
                        n = chunk_of(at + c, i)
                        if first and c < 8:
                            pe.wait_ge(xlo_ready, 8 * norm_no + c + 1)
                        if c == 16:
                            pe.wait_ge(hlo_ready, groups + NG if last else grown(groups + 1, i, 1))
                        if c < 16:
                            multiply(n, at + c, i, 2, W, (2 * (c % 8), 2 * (c % 8) + 1), x_hi, x_lo, par,
                                     c % 8 == 0, c % 8 == 7)
                        else:
                            multiply(n, at + c, i, 2, W, (2 * (c % 2), 2 * (c % 2) + 1), h_hi, h_lo, par,
                                     c % 2 == 0, c % 2 == 1)
                        if last:
                            continue
                        if which == 0 and c == 9:
                            pe.wait_ge(panel_out[qq % 2], grown(qq // 2 + 1, i, 3))
                            if not first:
                                pe.wait_ge(conv_done, grown(1, i, 1))
                            turn_panel(gate_n, 0, FT, gate_turned)
                        if c == 15 and first or c == 17:
                            pe.wait_ge(panel_out[(qq + 1) % 2], grown((qq + 1) // 2 + 1, i, 3))
                            if not first:
                                pe.wait_ge(hlo_ready if which else prod_done, number)
                            turn_panel(up_n, 2 if which == 0 else 0, FT, up_turned)

                group(None, True, False)
                with pe.Fori(0, NG - 1) as i:
                    group(i, False, False)
                group(None, False, True)

            pe.wait_ge(const_in, 32)
            pe.wait_ge(vec_in, 16 * VEC_DMAS)
            turn_rows = [(0, NV), (1, 88), (2, 88)]
            for k, (s, rows) in enumerate(turn_rows):
                mm = pe.transpose(mb[:, 0, P * k:P * k + rows], stage[0:rows, s, :], ident[0:rows, 0:rows])
            mm.then_inc(vec_turned, 1)
            pe.matmul(mb[0:HEADS_2, 1, :], table[:, :], hot_sb[:, :], start=True, stop=True).then_inc(rows_made, 1)
            pe.wait_ge(vec_out, 2)
            pe.wait_ge(rows_out, 1)
            norm(0)
            straight_part(IN1, FFN1 - 1 + 1)
            ffn_part(0, FFN1, FFN1_Q)
            beside(PLE - 1)
            straight_part(PLE, FFN2)
            ffn_part(1, FFN2, FFN2_Q)

        @block.scalar
        def _(act):
            links = [0]

            def link(ins):
                links[0] += 1
                ins.then_inc(act_link, 1)
                act.wait_ge(act_link, links[0])

            def split_hi(n, base, i, per, width):
                act.wait_ge(raw_in[base % RAW], grown(16 * (base // RAW + 1), i, 16 * GRP // RAW))
                if i is not None or base >= SPL:
                    act.wait_ge(mm_done, n - (SPL - 1))
                act.activation(cut(w_hi, base % SPL, per, width), cut(raw, base % RAW, per, width),
                               ACT.Copy).then_inc(hi_ready, 1)

            def copy_panel(q, to, func=ACT.Copy):
                width = to.shape[2]
                for t in range(TB):
                    ins = act.activation(to[:, t, :], panel_in(t, q)[:, 0:width], func)
                ins.then_inc(panel_out[q % 2], 1)

            def norm(i):
                if i:
                    act.wait_ge(h_done, i)
                if i == 1:
                    act.dma_start(p_in[:, :, :], g["p"].rearrange("a b (t p) d -> p (a b t) d", p=P)).then_inc(p_landed, 16)
                if i == 4:
                    act.dma_start(fin_g[:, :], g["final_norm_w_2"].rearrange("(a d) -> a d", a=1)
                                  .to_broadcast([P, D])).then_inc(fin_in, 16)
                act.activation(hn[:, 0, :], h[:, 0, :], ACT.Square, accum_out=ssq[:, 0:1]).then_inc(sq_act, 1)
                if i == 5:
                    return
                act.wait_ge(rstd_ready, i + 1)
                act.activation(hn[:, 0, :], h[:, 0, :], ACT.Copy, scale=rstd[:, 0:1]).then_inc(hn_act, 1)
                for j in range(KT // 2):
                    act.wait_ge(hn_turned, 8 * i + j + 1)
                    for k in range(2):
                        kt = 2 * j + k
                        ins = act.activation(x_hi[:, kt, :], mb[:, j % 4, T * k:T * k + T], ACT.Copy,
                                             scale=NORM[i][:, kt:kt + 1])
                    ins.then_inc(xhi_ready, 1)

            def log1p_exp(d, k):
                X = (X1 if k == 0 else X2)[:, :, :].rearrange("p a n -> p (a n)")
                src = mb[:, 2:4, :].rearrange("p a n -> p (a n)") if k == 0 else (BF2 if d == 0 else BB2)[:, :]
                link(act.activation(X, src, ACT.Abs))
                link(act.activation(X, X, ACT.Exp, scale=-1.0))
                act.activation(X, X, ACT.Ln, bias=1.0).then_inc(log1p_out, 1)

            def level_exp(blk, j):
                k = j + 16 * blk
                X = (X1 if blk == 0 else X2)[:, k % 2, :]
                act.wait_ge(expo_out, k + 1)
                act.activation(X, X, ACT.Exp).then_inc(exp_out, 1)

            def head_steps(n, slots, u0):
                for i, s in enumerate(slots):
                    u = u0 + i
                    second = u >= 12
                    L = (L2 if second else L1)[:, u % 2, :]
                    WT = (WT2 if second else WT1)[:, u % 2, :]
                    if n == s + 1:
                        act.wait_ge(logits_out, u + 1)
                        for t, (c, keys) in enumerate(LOGITS[second]):
                            at = 2 * (u % 2) + t
                            ins = act.activation(L[:, c:c + keys], L[:, c:c + keys], ACT.Exp,
                                                 bias=negmax[:, at:at + 1], accum_out=rowsum[:, at:at + 1])
                        ins.then_inc(exps_out, 1)
                    if n == s + 3:
                        act.wait_ge(probs_turned, u + 1)
                        if u >= 2:
                            act.wait_ge(head_made, u - 1)
                        width = 512 if second else 384
                        act.activation(WT[:, 0:width], mb[:, 2 + u % 2, 0:width], ACT.Copy).then_inc(probs_kept, 1)
                    if n == s + 4:
                        _, _, _, o, rows = head(u)
                        lo = 64 * (u % 2) if second else 0
                        act.wait_ge(head_made, u + 1)
                        act.activation(o, mb[lo:lo + rows, 2 + u % 2, 0:T], ACT.Copy).then_inc(head_out, 1)

            def beside(n):
                if n in ends and (n < OUT1 or IN2 <= n < OUT2):
                    q = ends[n]
                    act.wait_ge(mm_done, n + 1)
                    if q == 0:
                        copy_panel(q, tail)
                    elif q == IN2_Q:
                        copy_panel(q, tail2)
                    else:
                        copy_panel(q, region(q)[0])
                if n == 0:
                    act.wait_ge(forget_exp, 1)
                    flat = small[:, 64:76]
                    link(act.activation(flat, flat, ACT.Exp))
                    act.activation(flat, flat, ACT.Ln, bias=1.0).then_inc(log1p_out, 1)
                if n == 2:
                    act.wait_ge(fcum_made, 1)
                    act.activation(small[:, 76:88], mb[:, 3, 0:12], ACT.Copy).then_inc(fcum_out, 1)
                if n == HG["turn_q"] + 1:
                    act.wait_ge(dq_turned, 1)
                    act.activation(a_reg[:, 0, :], mb[:, 0:2, :].rearrange("p a n -> p (a n)"), ACT.Silu).then_inc(dq_out, 1)
                if n == HG["turn_f"] + 1:
                    act.wait_ge(dk_turned, 1)
                    log1p_exp(0, 0)
                if n == HG["turn_f"] + 2:
                    act.wait_ge(logf_out, 1)
                    act.activation(a_reg[:, 1, :], a_reg[:, 1, :], ACT.Exp).then_inc(dk_out, 1)
                for j in range(len(LEVELS1)):
                    if n == level_slot(0, j):
                        level_exp(0, j)
                if n == HG["make_o"] + 1:
                    act.wait_ge(o_made, 1)
                    act.activation(LG1[:, :], mb[:, 0:2, :].rearrange("p a n -> p (a n)"), ACT.Copy).then_inc(o_out, 1)
                    act.wait_ge(panel_out[0], 3)
                    act.activation(a_reg[:, 3, :], a_reg[:, 3, :], ACT.Silu).then_inc(og_out, 1)
                if n == HG["make_o"] + 5:
                    act.wait_ge(o_turned, 1)
                    act.activation(a_reg[:, 3, :], mb[:, 2:4, :].rearrange("p a n -> p (a n)"), ACT.Copy,
                                   scale=hgrn_gain).then_inc(o_kept, 1)
                for j, (panel, s) in enumerate(PREP1.items()):
                    if n == s + 3:
                        act.wait_ge(prep_turned, j + 1)
                        act.activation(bc_reg[:, panel - 5, :], mb[:, 0:2, :].rearrange("p a n -> p (a n)")[:, 0:768],
                                       ACT.Copy, scale=qk_gain[j // 4 * 2 + j % 2]).then_inc(prep_out, 1)
                head_steps(n, HEAD1, 0)

                if n == IN2 + 2:
                    act.wait_ge(lr_turned, 1)
                    act.activation(lr_t, mb[0:16, 0, :].rearrange("p (d t) -> p d t", d=2), ACT.Copy).then_inc(lr_out, 1)
                    act.wait_ge(rows_kept, 16)
                    act.dma_start(Z[:, :, :], bass.AP(bias_rows.tensor, 0, [[1, P], [512, HEADS_2], [1, 384]])).then_inc(z_in, 16)
                if n in (IN2 + 4, IN2 + 6):
                    d = (n - IN2 - 4) // 2
                    B = (BF2, BB2)[d]
                    if d == 0:
                        act.wait_ge(gates_made, 1)
                    else:
                        act.wait_ge(decay_out, 2)
                    for e in range(4):
                        ins = act.activation(B[:, T * e:T * e + T], mb[:, 2 * d + e // 2, T * (e % 2):T * (e % 2) + T],
                                             ACT.Identity, bias=gate_bias[d][:, e:e + 1])
                    link(ins)
                    log1p_exp(d, 1)
                if n == IN2 + 10:
                    act.wait_ge(dq_turned, 2)
                    act.activation(reg2[:, 0, :], mb[:, 0:2, :].rearrange("p a n -> p (a n)"), ACT.Copy,
                                   scale=float(P) ** -0.5).then_inc(dq_out, 1)
                if n == IN2 + 18:
                    act.wait_ge(dk_turned, 2)
                    act.activation(reg2[:, 1, :], mb[:, 2:4, :].rearrange("p a n -> p (a n)"), ACT.Copy).then_inc(dk_out, 1)
                for j in range(len(LEVELS2)):
                    if n == level_slot(1, j):
                        level_exp(1, j)
                if n == IN2 + 50:
                    act.wait_ge(panel_out[(IN2_Q + 6) % 2], (IN2_Q + 6) // 2 + 1)
                    act.wait_ge(panel_out[(IN2_Q + 5) % 2], (IN2_Q + 5) // 2 + 1)
                    gr = reg2[:, 4:6, :].rearrange("p a n -> p (a n)")
                    act.activation(gr, gr, ACT.Silu).then_inc(og_out, 1)
                if n == IN2 + 71:
                    act.wait_ge(o_made, 2)
                    act.activation(reg2[:, 0:2, :].rearrange("p a n -> p (a n)"), mb[:, :, :].rearrange("p a n -> p (a n)"),
                                   ACT.Copy).then_inc(o_out, 1)
                if n == IN2 + 75:
                    act.wait_ge(o_turned, 2)
                    for kt in range(8):
                        ins = act.activation(o_turned_at(8 + kt, 1), mb[:, kt // 2, T * (kt % 2):T * (kt % 2) + T], ACT.Copy,
                                             scale=gla_gain[:, kt:kt + 1])
                    ins.then_inc(o_kept, 1)
                for j, (panel, s) in enumerate(PREP2.items()):
                    if n == s + 1:
                        act.wait_ge(prep_turned, 8 + j + 1)
                        src = mb[:, 2 * (j % 2):2 * (j % 2) + 2, :].rearrange("p a n -> p (a n)")
                        act.activation(reg2[:, panel - 1, :], src, ACT.Copy,
                                       scale=64.0 ** -0.5 if j % 2 == 0 else 1.0).then_inc(prep_out, 1)
                head_steps(n, HEAD2, 12)
                if n in OSPLIT:
                    blk = n >= IN2
                    if n in (IN1_END - 1, IN2_END - 1):
                        act.wait_ge(mm_done, n + 1)
                        act.wait_ge(o_kept, blk + 1)
                    if n != IN2_END - 1:
                        act.wait_ge(head_out, {IN1_END - 1: 9, OUT1 + 22: 12, OUT2 + 15: 28}[n])
                    for s in OSPLIT[n]:
                        pair = s if not blk else (s - 4) % 8
                        for kt in (2 * pair, 2 * pair + 1):
                            ins = act.activation(x_hi[:, kt, :], o_turned_at(kt, int(blk)), ACT.Copy)
                        ins.then_inc(ohi_ready, 1)
                if PLE <= n < PLE_END and n in ends:
                    q = ends[n]
                    j = (q - PLE_Q) // 2
                    act.wait_ge(mm_done, n + 1)
                    if (q - PLE_Q) % 2 == 0:
                        if j:
                            act.wait_ge(ple_sig_out, j)
                        copy_panel(q, pn)
                    else:
                        copy_panel(q, gate_n, ACT.Sigmoid)
                if n in NORM_AT:
                    norm(NORM_AT[n])
                if n == IN2 - 1:
                    for d, name in enumerate(("gla_gate_w_fwd_2", "gla_gate_w_bwd_2")):
                        act.dma_start(gate_w[:, d, :], g[name].rearrange("a r c -> (a r) c")).then_inc(gate_w_in, 16)
                if n == PLE - 1:
                    act.wait_ge(p_turned, 1)
                    act.activation(p_hi[:, :, :].rearrange("p a n -> p (a n)"), mb[:, 0, :], ACT.Copy).then_inc(phi_ready, 1)

            def split_ahead(n):
                m = n + AHEAD
                if m < TOTAL:
                    per, width = shape_of(m)
                    split_hi(m, m, None, per, width)

            def straight_part(a, z):
                for n in range(a, z):
                    split_ahead(n)
                    beside(n)

            def ffn_part(which, base, base_q):
                groups = NG * which

                def group(i, first, last):
                    at = base if first else base + 16
                    qq = base_q if first else base_q + 2
                    if last:
                        at += (NG - 1) * GRP - 16
                    gi = 0 if first else 1

                    def split_hidden(n):
                        act.wait_ge(mm_done, n)
                        if which == 0:
                            act.wait_ge(prod_done, NG if last else grown(1, i, 1))
                            src = cv[:, :, :].rearrange("p a n -> p (a n)")
                        else:
                            act.wait_ge(up_turned, groups + NG if last else grown(groups + 1, i, 1))
                            src = mb[:, 0:2, :].rearrange("p a n -> p (a n)")
                        act.activation(h_hi[:, :, :].rearrange("p a n -> p (a n)"), src, ACT.Copy).then_inc(hhi_ready, 1)

                    if last:
                        split_hidden(at + 16)
                    for c in range(16 if last else 0, 16 if first else GRP):
                        n = chunk_of(at + c, i)
                        if last:
                            split_ahead(at + c)
                            continue
                        split_hi(chunk_of(at + c + AHEAD, i), at + c + AHEAD, i, 2, W)
                        if c == 0 and not first:
                            split_hidden(n)
                        if c == 7:
                            act.wait_ge(mm_done, n + 1)
                            if which == 0:
                                if not first:
                                    act.wait_ge(gate_turned, grown(gi, i, 1))
                            elif not first:
                                act.wait_ge(panel_out[(base_q + 1) % 2], grown((base_q + 1) // 2 + 1, i, 3))
                            par_q = qq
                            for t in range(TB):
                                ins = act.activation(gate_n[:, t, :], panel_in(t, par_q), ACT.Copy if which == 0 else ACT.Silu)
                            ins.then_inc(panel_out[par_q % 2], 1)
                        if which == 0 and c == 10:
                            act.wait_ge(gate_turned, grown(gi + 1, i, 1))
                            if not first:
                                act.wait_ge(hlo_ready, grown(gi, i, 1))
                            for ft in range(FT):
                                at_f = ft if first else i * FT + (FT + ft)
                                ins = act.activation(cv[:, ft, :], mb[:, ft // 2, T * (ft % 2):T * (ft % 2) + T],
                                                     ACT.Identity, bias=conv[:, 3, bass.ds(at_f, 1)],
                                                     scale=conv[:, 2, bass.ds(at_f, 1)])
                            ins.then_inc(conv_begun, 1)
                        if which == 0 and c == 13:
                            act.wait_ge(conv_done, grown(gi + 1, i, 1))
                            flat = cv[:, :, :].rearrange("p a n -> p (a n)")
                            act.activation(flat, flat, ACT.Gelu_apprx_tanh).then_inc(gelu_done, 1)
                        if which == 0 and c == 15:
                            act.wait_ge(mm_done, n + 1)
                            if not first:
                                act.wait_ge(up_turned, grown(gi, i, 1))
                            for t in range(TB):
                                ins = act.activation(up_n[:, t, :], panel_in(t, qq + 1), ACT.Copy)
                            ins.then_inc(panel_out[(qq + 1) % 2], 1)

                group(None, True, False)
                with act.Fori(0, NG - 1) as i:
                    group(i, False, False)
                group(None, False, True)

            act.dma_start(cf[:, :], const_f[:, 0:3 * P]).then_inc(const_in, 16)
            act.dma_start(masks_f[:, :, :].rearrange("p a n -> p (a n)"), const_m).then_inc(const_in, 16)
            rows = []
            for j, name in enumerate(("attn_norm", "ffn_norm", "ple_norm", "attn_norm_w_2", "ffn_norm_w_2")):
                rows.append((stage[KT * j:KT * (j + 1), 0, :], g[name]))
            rows.append((stage[V0:V0 + 1, 0, :], g["hgrn_onorm"]))
            for j, name in enumerate(("fox_qnorm", "fox_knorm", "moba_qnorm", "moba_knorm")):
                rows.append((stage[V0 + 1 + j:V0 + 2 + j, 0, :], g[name]))
            rows.append((stage[V0 + 5:V0 + 9, 0, :], g["gla_gate_b_fwd_2"]))
            rows.append((stage[V0 + 9:V0 + 13, 0, :], g["gla_gate_b_bwd_2"]))
            rows.append((stage[V0 + 13:V0 + 21, 0, :], g["gla_norm_w_2"]))
            for to, src in rows:
                act.dma_start(to, src.rearrange("a (k p) -> (a k) p", p=P)).then_inc(vec_in, 16)
            taps = g["conv_w"].rearrange("a c (f p) -> (a c f) p", p=P)
            act.dma_start(stage[0:88, 1, :], taps[0:88, :]).then_inc(vec_in, 16)
            act.dma_start(stage[0:44, 2, :], taps[88:132, :]).then_inc(vec_in, 16)
            act.dma_start(stage[44:88, 2, :], g["conv_b"].rearrange("a (f p) -> (a f) p", p=P)).then_inc(vec_in, 16)
            act.dma_start(fbias, g["fox_bf"].to_broadcast([P, HEADS_B])).then_inc(vec_in, 16)
            act.dma_start(causal[:, :], const_f[:, 3 * P:3 * P + 384]).then_inc(vec_in, 16)
            act.dma_start(alibi[:, :], const_f[:, 3 * P + 384:3 * P + 768]).then_inc(vec_in, 16)
            act.dma_start(hot_sb[:, :], hot).then_inc(vec_in, 16)
            act.wait_ge(table_one, 1)
            act.dma_start(table[0:BUCKETS, :], g["rel_bias_table_2"]).then_inc(vec_in, 16)
            act.wait_ge(vec_turned, 1)
            act.activation(vecs[:, :], mb[:, 0, 0:NV], ACT.Copy).then_inc(vec_out, 1)
            act.activation(conv[:, :, :], mb[:, 0, P:P + 2 * P].rearrange("p (a n) -> p a n", a=2)[:, :, 0:88], ACT.Copy)\
                .then_inc(vec_out, 1)
            act.wait_ge(rows_made, 1)
            act.activation(rows_sb[:, :], mb[0:HEADS_2, 1, :], ACT.Copy).then_inc(rows_out, 1)
            act.wait_ge(rows_out, 1)
            act.dma_start(bias_rows, rows_sb[:, :]).then_inc(rows_kept, 16)
            act.wait_ge(x_in, 16)
            act.wait_ge(vec_out, 2)
            norm(0)
            for n in range(AHEAD):
                split_ahead(n - AHEAD)
            straight_part(IN1, FFN1)
            ffn_part(0, FFN1, FFN1_Q)
            beside(PLE - 1)
            straight_part(PLE, FFN2)
            ffn_part(1, FFN2, FFN2_Q)
            norm(5)

        @block.vector
        def _(dve):
            links = [0]

            def link(ins):
                links[0] += 1
                ins.then_inc(dve_link, 1)
                dve.wait_ge(dve_link, links[0])

            def split_lo(n, base, i, per, width):
                dve.wait_ge(hi_ready, n + 1)
                dve.tensor_tensor(cut(w_lo, base % SPL, per, width), cut(raw, base % RAW, per, width),
                                  cut(w_hi, base % SPL, per, width).bitcast(F32), ALU.subtract).then_inc(lo_ready, 1)

            def add_panel(q, col):
                for t in range(TB):
                    to = h[:, t, col:col + W]
                    ins = dve.tensor_tensor(to, panel_in(t, q), to, ALU.add)
                return ins

            def norm(i):
                if i:
                    dve.wait_ge(h_done, i)
                dve.tensor_tensor_reduce(hn[:, 1, :], h[:, 1, :], h[:, 1, :], 1.0, 0.0, ALU.mult, ALU.add,
                                         ssq[:, 1:2]).then_inc(sq_dve, 1)
                dve.wait_ge(rstd_ready, i + 1)
                if i == 5:
                    dve.wait_ge(fin_in, 16)
                    for t in range(TB):
                        dve.scalar_tensor_tensor(hn[:, t, :], h[:, t, :], rstd[:, t:t + 1], fin_g[:, :], ALU.mult,
                                                 ALU.mult).then_inc(fin_done, 1)
                    return
                dve.tensor_scalar(hn[:, 1, :], h[:, 1, :], rstd[:, 1:2], None, ALU.mult).then_inc(hn_dve, 1)
                for j in range(KT // 2):
                    dve.wait_ge(xhi_ready, 8 * i + j + 1)
                    for k in range(2):
                        kt = 2 * j + k
                        ins = dve.scalar_tensor_tensor(x_lo[:, kt, :], mb[:, j % 4, T * k:T * k + T],
                                                       NORM[i][:, kt:kt + 1], x_hi[:, kt, :].bitcast(F32),
                                                       ALU.mult, ALU.subtract)
                    ins.then_inc(xlo_ready, 1)

            def level_parts(blk, j):
                d, hp, lv = (LEVELS1 if blk == 0 else LEVELS2)[j]
                k = j + 16 * blk
                B = (B1 if blk == 0 else (BF2, BB2)[d])[:, 512 * hp:512 * hp + 512]
                X = (X1 if blk == 0 else X2)[:, k % 2, :]
                return d, hp, lv, k, B, X

            def level_expo(blk, j):
                d, hp, lv, k, B, X = level_parts(blk, j)
                if j >= 2:
                    dve.wait_ge(pair_made, (17 if blk else 0) + j)
                edge = -1 if d == 0 else 0
                if lv < 7:
                    size = LEVELS[lv]
                    r = B.rearrange("p (b s l) -> p b s l", s=2, l=size)
                    x = X.rearrange("p (b s l) -> p b s l", s=2, l=size)
                    e0 = size - 1 if d == 0 else 0
                    ref = r[:, :, d, e0:e0 + 1].to_broadcast([P, 512 // (2 * size), size])
                    dve.tensor_tensor(x[:, :, d, :], ref, r[:, :, d, :], ALU.subtract)
                    if size < 64:
                        ins = dve.tensor_tensor(x[:, :, 1 - d, :], r[:, :, 1 - d, :], ref, ALU.subtract)
                    else:
                        ins = dve.tensor_copy(x[:, :, 1 - d, :], r[:, :, 1 - d, :])
                    ins.then_inc(expo_out, 1)
                    return
                r = B.rearrange("p (h c l) -> p h c l", c=4, l=64)
                x = X.rearrange("p (h c l) -> p h c l", c=4, l=64)
                fk, nk, nq, fq = (0, 1, 2, 3) if d == 0 else (3, 2, 1, 0)
                e0 = 63 if d == 0 else 0
                link(dve.tensor_tensor(full01[:, 0:2], r[:, :, nk, e0], r[:, :, fk, e0], ALU.add))

                def whole(c):
                    return r[:, :, c, e0:e0 + 1].to_broadcast([P, 2, 64])

                dve.tensor_tensor(x[:, :, nk, :], whole(nk), r[:, :, nk, :], ALU.subtract)
                dve.tensor_tensor(x[:, :, fk, :], full01[:, 0:2].unsqueeze(2).to_broadcast([P, 2, 64]), r[:, :, fk, :],
                                  ALU.subtract)
                dve.tensor_copy(x[:, :, nq, :], r[:, :, nq, :])
                dve.tensor_tensor(x[:, :, fq, :], r[:, :, fq, :], whole(nq), ALU.add).then_inc(expo_out, 1)

            def level_mult(blk, j):
                d, hp, lv, k, B, X = level_parts(blk, j)
                size = LEVELS[lv] if lv < 7 else P
                q, kk = (a_reg[:, 0, :], a_reg[:, 1, :]) if blk == 0 else (reg2[:, 0, :], reg2[:, 1, :])
                x = X.rearrange("p (b s l) -> p b s l", s=2, l=size)
                dve.wait_ge(exp_out, k + 1)
                for half, src in ((d, kk), (1 - d, q)):
                    s = src[:, 512 * hp:512 * hp + 512].rearrange("p (b s l) -> p b s l", s=2, l=size)
                    ins = dve.tensor_tensor(x[:, :, half, :], x[:, :, half, :], s[:, :, half, :], ALU.mult)
                ins.then_inc(x_out, 1)

            def level_keep(blk, j):
                d, hp, lv, k, _, _ = level_parts(blk, j)
                A = (AT1 if blk == 0 else AT2)[:, :, :, :].rearrange("p h s (a l) -> p h (s a) l", l=P)
                dve.wait_ge(pair_made, (17 if blk else 0) + 1 + j + 1)
                if lv == 7:
                    dve.tensor_copy(A[:, 2 * hp:2 * hp + 2, 1 + d, :], mb[:, k % 2, 0:256].rearrange("p (h l) -> p h l", h=2))\
                        .then_inc(pair_kept, 1)
                    return
                for e in range(2):
                    ins = dve.copy_predicated(A[:, 2 * hp + e, 0:4:3, :],
                                              masks[:, 1 + 7 * d + lv:2 + 7 * d + lv, :].to_broadcast([P, 2, P]),
                                              mb[:, k % 2, 256 * e:256 * e + 256].rearrange("p (b l) -> p b l", b=2))
                ins.then_inc(pair_kept, 1)

            def diagonal_keep(blk):
                A = (AT1 if blk == 0 else AT2)[:, :, :, :].rearrange("p h s (a l) -> p h (s a) l", l=P)
                dve.wait_ge(pair_made, (17 if blk else 0) + 1)
                dve.wait_ge(at_zero, blk + 1)
                for e in range(4):
                    ins = dve.copy_predicated(A[:, e, 0:4:3, :], masks[:, 0:1, :].to_broadcast([P, 2, P]),
                                              mb[:, 2 + e // 2, 256 * (e % 2):256 * (e % 2) + 256].rearrange("p (b l) -> p b l", b=2))
                ins.then_inc(pair_kept, 1)

            def scan(B, src, back):
                for e in range(4):
                    a, z = B[:, T * e:T * e + T], src[:, T * e:T * e + T]
                    if back:
                        a, z = a[:, ::-1], z[:, ::-1]
                    ins = dve.tensor_tensor_scan(a, scanm[:, :], z, 0.0, ALU.mult, ALU.add)
                ins.then_inc(decay_out, 1)

            def head_steps(n, slots, u0):
                for i, s in enumerate(slots):
                    u = u0 + i
                    second = u >= 12
                    L = (L2 if second else L1)[:, u % 2, :]
                    if n == s + 1:
                        S = mb[:, u % 2, :]
                        dve.wait_ge(scores_made, u + 1)
                        if u >= 2:
                            dve.wait_ge(probs_turned, u - 1)
                        if u == 12:
                            dve.wait_ge(z_in, 16)
                        for t, (c, keys) in enumerate(LOGITS[second]):
                            s_t, l_t = S[:, c:c + keys], L[:, c:c + keys]
                            if u < HEADS_B:
                                ins = dve.scalar_tensor_tensor(l_t, s_t, fcum[:, t, u:u + 1], causal[:, c:c + keys],
                                                               ALU.add, ALU.add)
                            elif u < 12:
                                slope = 2.0 ** (-8.0 * (u - HEADS_B + 1) / HEADS_C)
                                ins = dve.scalar_tensor_tensor(l_t, alibi[:, c:c + keys], slope, s_t, ALU.mult, ALU.add)
                            else:
                                a = T - P * (t + 1)
                                z = Z[:, u - 12, P * t:P * t + T]
                                ins = dve.tensor_tensor(l_t, s_t, z[:, ::-1], ALU.add)
                        link(ins)
                        for t, (c, keys) in enumerate(LOGITS[second]):
                            at = 2 * (u % 2) + t
                            ins = dve.tensor_reduce(negmax[:, at:at + 1], L[:, c:c + keys], AX_X, ALU.max, negate=True)
                        ins.then_inc(logits_out, 1)
                    if n == s + 2:
                        dve.wait_ge(exps_out, u + 1)
                        at = 2 * (u % 2)
                        link(dve.reciprocal(rowinv[:, at:at + 2], rowsum[:, at:at + 2]))
                        for t, (c, keys) in enumerate(LOGITS[second]):
                            ins = dve.tensor_scalar(L[:, c:c + keys], L[:, c:c + keys], rowinv[:, at + t:at + t + 1], None,
                                                    ALU.mult)
                        ins.then_inc(probs_out, 1)

            def beside(n):
                if n == 0:
                    dve.wait_ge(panel_out[0], 1)
                    link(dve.tensor_tensor(lf, tail[:, :, :], fbias.unsqueeze(1).to_broadcast([P, TB, HEADS_B]), ALU.add))
                    dve.scalar_tensor_tensor(nlf, lf, -1.0, lf, ALU.mult, ALU.min).then_inc(forget_exp, 1)
                if n == 1:
                    dve.wait_ge(log1p_out, 1)
                    link(dve.scalar_tensor_tensor(lf, lf, 0.0, nlf, ALU.min, ALU.subtract))
                    dve.tensor_scalar(nlf, lf, -1.0, None, ALU.mult).then_inc(forget_out, 1)
                if n == HG["turn_f"] + 1:
                    z = mb[:, 2:4, :].rearrange("p a n -> p (a n)")
                    dve.wait_ge(log1p_out, 2)
                    link(dve.scalar_tensor_tensor(LG1[:, :], z, 0.0, X1[:, :, :].rearrange("p a n -> p (a n)"),
                                                  ALU.min, ALU.subtract))
                    dve.tensor_tensor(a_reg[:, 1, :], LG1[:, :], z, ALU.subtract).then_inc(logf_out, 1)
                    dve.wait_ge(logf_out, 1)
                    link(dve.tensor_scalar(LG1[:, :], LG1[:, :], LN_TINY, None, ALU.max))
                    scan(B1, LG1, False)
                if n == HG["turn_f"] + 2:
                    dve.wait_ge(decay_out, 1)
                if n == HG["levels"]:
                    diagonal_keep(0)
                for j in range(len(LEVELS1)):
                    if n == level_slot(0, j):
                        level_expo(0, j)
                    if n == level_slot(0, j) + 1:
                        level_mult(0, j)
                    if n == level_slot(0, j) + 3:
                        level_keep(0, j)
                if n == HG["make_o"] + 2:
                    X = X1[:, :, :].rearrange("p a n -> p (a n)")
                    dve.wait_ge(o_out, 1)
                    link(dve.tensor_tensor(X, LG1[:, :], LG1[:, :], ALU.mult))
                    dve.tensor_reduce(hsq, X.rearrange("p (g l) -> p g l", l=P), AX_X, ALU.add).then_inc(osq_out, 1)
                if n == HG["make_o"] + 3:
                    dve.wait_ge(orstd, 1)
                    o = LG1[:, :].rearrange("p (g l) -> p g l", l=P)
                    link(dve.tensor_tensor(o, o, hrs.unsqueeze(2).to_broadcast([P, 8, P]), ALU.mult))
                    dve.wait_ge(og_out, 1)
                    dve.tensor_tensor(LG1[:, :], LG1[:, :], a_reg[:, 3, :], ALU.mult).then_inc(o_scaled, 1)
                for j, (panel, s) in enumerate(PREP1.items()):
                    r = bc_reg[:, panel - 5, :]
                    if n == s:
                        dve.wait_ge(panel_out[panel % 2], panel // 2 + 1)
                        if j == 0:
                            dve.wait_ge(o_turned, 1)
                        link(dve.tensor_tensor(LG1[:, 0:768], r, r, ALU.mult))
                        dve.tensor_reduce(hsq[:, 0:6], LG1[:, 0:768].rearrange("p (g l) -> p g l", l=P), AX_X, ALU.add)\
                            .then_inc(prep_sq, 1)
                    if n == s + 1:
                        dve.wait_ge(prep_rstd, j + 1)
                        v = r.rearrange("p (g l) -> p g l", l=P)
                        dve.tensor_tensor(v, v, hrs[:, 0:6].unsqueeze(2).to_broadcast([P, 6, P]), ALU.mult)\
                            .then_inc(prep_scaled, 1)
                head_steps(n, HEAD1, 0)

                if n in (IN2 + 5, IN2 + 7):
                    d = (n - IN2 - 5) // 2
                    B = (BF2, BB2)[d]
                    X = X2[:, :, :].rearrange("p a n -> p (a n)")
                    dve.wait_ge(log1p_out, 3 + d)
                    link(dve.scalar_tensor_tensor(X, B[:, :], 0.0, X, ALU.min, ALU.subtract))
                    link(dve.tensor_scalar(X, X, 1.0 / 16.0, None, ALU.mult))
                    scan(B, X, d == 1)
                if n == IN2 + 19:
                    dve.wait_ge(decay_out, 3)
                    diagonal_keep(1)
                for j in range(len(LEVELS2)):
                    if n == level_slot(1, j):
                        level_expo(1, j)
                    if n == level_slot(1, j) + 1:
                        level_mult(1, j)
                    if n == level_slot(1, j) + 3:
                        level_keep(1, j)
                ob = reg2[:, 0:2, :]
                if n == IN2 + 72:
                    dve.wait_ge(o_out, 2)
                    X = X2[:, :, :].rearrange("p a n -> p (a n)")
                    for t in range(TB):
                        link(dve.tensor_tensor(X, ob[:, t, :], ob[:, t, :], ALU.mult))
                        ins = dve.tensor_reduce(hsq[:, 4 * t:4 * t + 4], X.rearrange("p (g l) -> p g l", l=T), AX_X, ALU.add)
                        if t == 0:
                            link(ins)
                    ins.then_inc(osq_out, 1)
                if n == IN2 + 73:
                    dve.wait_ge(orstd, 2)
                    o = ob.rearrange("p a n -> p (a n)").rearrange("p (g l) -> p g l", l=T)
                    link(dve.tensor_tensor(o, o, hrs.unsqueeze(2).to_broadcast([P, 8, T]), ALU.mult))
                    dve.wait_ge(og_out, 2)
                    for c in range(2):
                        part = ob[:, :, W * c:W * c + W]
                        ins = dve.tensor_tensor(part, part, reg2[:, 4 + c, :].rearrange("p (t n) -> p t n", t=TB), ALU.mult)
                    ins.then_inc(o_scaled, 1)
                head_steps(n, HEAD2, 12)
                if n in OSPLIT:
                    blk = n >= IN2
                    for s in OSPLIT[n]:
                        pair = s if not blk else (s - 4) % 8
                        dve.wait_ge(ohi_ready, s + 1)
                        for kt in (2 * pair, 2 * pair + 1):
                            ins = dve.tensor_tensor(x_lo[:, kt, :], o_turned_at(kt, int(blk)), x_hi[:, kt, :].bitcast(F32),
                                                    ALU.subtract)
                        ins.then_inc(olo_ready, 1)
                if n in ends and (OUT1 <= n < OUT1_END or OUT2 <= n < OUT2_END):
                    q = ends[n]
                    dve.wait_ge(mm_done, n + 1)
                    first_q = OUT1_Q if n < OUT1_END else OUT2_Q
                    add_panel(q, (q - first_q) % 4 * W).then_inc(panel_out[q % 2], 1)
                if n in (OUT1_END - 1, OUT2_END - 1):
                    dve.wait_ge(panel_out[ends[n] % 2], ends[n] // 2 + 1)
                    dve.sem_inc(h_done, 1)
                if PLE <= n < PLE_END and n in ends and (ends[n] - PLE_Q) % 2 == 1:
                    q = ends[n]
                    j = (q - PLE_Q) // 2
                    dve.wait_ge(panel_out[q % 2], q // 2 + 1)
                    dve.wait_ge(panel_out[(q - 1) % 2], (q - 1) // 2 + 1)
                    link(dve.tensor_tensor(gate_n[:, :, :], gate_n[:, :, :], pn[:, :, :], ALU.mult))
                    to = h[:, :, W * j:W * j + W]
                    ins = dve.tensor_tensor(to, to, gate_n[:, :, :], ALU.add)
                    ins.then_inc(ple_sig_out, 1)
                    if n == PLE_END - 1:
                        dve.wait_ge(ple_sig_out, 4)
                        dve.sem_inc(h_done, 1)
                if n in NORM_AT:
                    norm(NORM_AT[n])
                if n == PLE - 1:
                    dve.wait_ge(phi_ready, 1)
                    dve.tensor_tensor(p_lo[:, :, :].rearrange("p a n -> p (a n)"), mb[:, 0, :],
                                      p_hi[:, :, :].rearrange("p a n -> p (a n)").bitcast(F32), ALU.subtract)\
                        .then_inc(plo_ready, 1)

            def split_ahead(n):
                m = n + AHEAD
                if m < TOTAL:
                    per, width = shape_of(m)
                    split_lo(m, m, None, per, width)

            def straight_part(a, z):
                for n in range(a, z):
                    split_ahead(n)
                    beside(n)

            def ffn_part(which, base, base_q):
                groups = NG * which

                def group(i, first, last):
                    at = base if first else base + 16
                    qq = base_q if first else base_q + 2
                    if last:
                        at += (NG - 1) * GRP - 16
                        qq += 6 * (NG - 1) - 2
                    gi = 0 if first else 1

                    def split_hidden():
                        dve.wait_ge(hhi_ready, groups + NG if last else grown(groups + 1, i, 1))
                        src = (cv[:, :, :] if which == 0 else mb[:, 0:2, :]).rearrange("p a n -> p (a n)")
                        dve.tensor_tensor(h_lo[:, :, :].rearrange("p a n -> p (a n)"), src,
                                          h_hi[:, :, :].rearrange("p a n -> p (a n)").bitcast(F32), ALU.subtract)\
                            .then_inc(hlo_ready, 1)

                    if last:
                        split_hidden()
                    for c in range(16 if last else 0, 16 if first else GRP):
                        n = chunk_of(at + c, i)
                        if last:
                            split_ahead(at + c)
                        else:
                            split_lo(chunk_of(at + c + AHEAD, i), at + c + AHEAD, i, 2, W)
                        if c == 0 and not first and not last:
                            split_hidden()
                        if which == 0 and c == 11:
                            dve.wait_ge(conv_begun, grown(gi + 1, i, 1))
                            for back in (1, 2):
                                for ft in range(FT):
                                    at_f = ft if first else i * FT + (FT + ft)
                                    ins = dve.scalar_tensor_tensor(
                                        cv[:, ft, back:T], mb[:, ft // 2, T * (ft % 2):T * (ft % 2) + T - back],
                                        conv[:, 2 - back, bass.ds(at_f, 1)], cv[:, ft, back:T], ALU.mult, ALU.add)
                                if back == 1:
                                    ins.then_inc(conv_first, 1)
                                    dve.wait_ge(conv_first, grown(gi + 1, i, 1))
                            ins.then_inc(conv_done, 1)
                        if which == 1 and c == 15:
                            dve.wait_ge(mm_done, n + 1)
                            dve.wait_ge(panel_out[qq % 2], grown(qq // 2 + 1, i, 3))
                            if not first:
                                dve.wait_ge(up_turned, grown(groups + gi, i, 1))
                            for t in range(TB):
                                ins = dve.tensor_tensor(up_n[:, t, :], panel_in(t, qq + 1), gate_n[:, t, :], ALU.mult)
                            ins.then_inc(panel_out[(qq + 1) % 2], 1)
                        if which == 0 and (c == 18 and not last or c == 15 and first):
                            dve.wait_ge(up_turned, grown(gi + 1, i, 1))
                            dve.wait_ge(gelu_done, grown(gi + 1, i, 1))
                            flat = cv[:, :, :].rearrange("p a n -> p (a n)")
                            dve.tensor_tensor(flat, flat, mb[:, 2:4, :].rearrange("p a n -> p (a n)"), ALU.mult)\
                                .then_inc(prod_done, 1)
                        if c >= 17 and c % 2 == 1:
                            part = (c - 17) // 2
                            dve.wait_ge(mm_done, n + 1)
                            add_panel(qq + 2 + part, part * W).then_inc(panel_out[(qq + part) % 2], 1)

                group(None, True, False)
                with dve.Fori(0, NG - 1) as i:
                    group(i, False, False)
                group(None, False, True)
                last_q = base_q + 6 * NG - 1
                dve.wait_ge(panel_out[last_q % 2], last_q // 2 + 1)
                dve.sem_inc(h_done, 1)

            dve.wait_ge(const_in, 32)
            dve.wait_ge(vec_in, 16 * VEC_DMAS)
            dve.wait_ge(vec_out, 1)
            dve.tensor_copy(masks[:, :, :], masks_f[:, :, :])
            for j in (0, 2):
                dve.tensor_scalar(qk_gain[j], qk_gain[j], float(P) ** -0.5, None, ALU.mult)
            dve.wait_ge(x_in, 16)
            norm(0)
            for n in range(AHEAD):
                split_ahead(n - AHEAD)
            straight_part(IN1, FFN1)
            ffn_part(0, FFN1, FFN1_Q)
            beside(PLE - 1)
            straight_part(PLE, FFN2)
            ffn_part(1, FFN2, FFN2_Q)
            norm(5)


NAMES = ["x", "p", "attn_norm", "w_in", "fox_bf", "lb_logits", "hgrn_onorm", "fox_qnorm", "fox_knorm",
         "moba_qnorm", "moba_knorm", "w_out", "ffn_norm", "w_gate", "w_up", "conv_w", "conv_b", "w_down",
         "ple_norm", "w_ple_gate", "w_ple_proj", "attn_norm_w_2", "w_in_2", "rel_bias_table_2",
         "gla_gate_w_fwd_2", "gla_gate_b_fwd_2", "gla_gate_w_bwd_2", "gla_gate_b_bwd_2", "gla_norm_w_2",
         "w_out_2", "ffn_norm_w_2", "w_gate_2", "w_up_2", "w_down_2", "final_norm_w_2"]


def kernel(**inputs):
    import concourse.bacc as bacc
    from concourse.bass_utils import run_bass_kernel_spmd

    nc = bacc.Bacc("TRN2", target_bir_lowering=False, num_devices=1)
    arrays, aps = {}, {}

    def give(name, a):
        arrays[name] = a
        return nc.dram_tensor(name, a.shape, mybir.dt.from_np(a.dtype), kind="ExternalInput").ap()

    for name in NAMES:
        aps[name] = give(f"in_{name}", np.ascontiguousarray(inputs[name]))
    cf, masks, hot = shape_constants()
    consts = [give("const_f", cf), give("const_m", masks), give("const_hot", hot)]
    out = nc.dram_tensor("out", (1, T, D), F32, kind="ExternalOutput").ap()
    build(nc, aps, out, *consts)
    r = run_bass_kernel_spmd(nc, [arrays], core_ids=[0])
    return r.results[0]["out"]
```

```python
from contextlib import ExitStack
from math import log

import numpy as np

import concourse.bass as bass
from concourse import mybir

ALU = mybir.AluOpType
ACT = mybir.ActivationFunctionType
F32 = mybir.dt.float32
F32R = mybir.dt.float32r
I8 = mybir.dt.int8
AX_X = mybir.AxisListType.X

P = 128
T = 256
TB = T // P
D = 2048
KT = D // P
FF = 5632
W = 512
NG = FF // W
FT = W // P
EPS = 1e-6
NEG = -1e30
FAR = -1e34
LN_TINY = log(1e-30)
RAW = 4
SPL = 6
AHEAD = 5
HEADS_B = HEADS_C = 6
HEADS_2 = 16
LEVELS = (1, 2, 4, 8, 16, 32, 64)
GRP = 24
BUCKETS = 32
ZR = 7
ND = 2 * T - 1


def shape_constants():
    i, j = np.arange(P)[:, None], np.arange(P)[None, :]
    cf = np.zeros((P, 3 * P + 768), np.float32)
    cf[:, 0:P] = i == j
    cf[:, P:2 * P] = i <= j
    cf[:, 2 * P:3 * P] = 1.0
    q = np.arange(P)[:, None]
    k0, k1 = np.arange(P)[None, :], np.arange(T)[None, :]
    dist = np.concatenate([k0 - q, k1 - q - P], axis=1)
    cf[:, 3 * P:3 * P + 384] = np.where(dist <= 0, 0.0, NEG)
    cf[:, 3 * P + 384:3 * P + 768] = np.where(dist <= 0, dist, FAR)
    masks = np.zeros((P, 15, P), np.float32)
    masks[:, 0] = i == j
    for n, size in enumerate(LEVELS):
        pair = (i // (2 * size) == j // (2 * size)) & (i // size % 2 == 0) & (j // size % 2 == 1)
        masks[:, 1 + n] = pair
        masks[:, 8 + n] = pair.T
    rel = T - 1 - np.arange(ND)
    nb = BUCKETS // 2
    n = np.abs(rel)
    exact = nb // 2
    large = exact + (np.log(np.maximum(n, 1) / exact) / log(1024 / exact) * (nb - exact)).astype(np.int64)
    bucket = np.where(rel > 0, nb, 0) + np.where(n < exact, n, np.minimum(large, nb - 1))
    times = (n <= 64) * 1 + (rel % 4 == 0) * 1 + (rel % 16 == 0) * 1
    hot = np.zeros((BUCKETS + 1, 512), np.float32)
    hot[bucket, np.arange(ND)] = 1.0
    hot[BUCKETS, :ND] = np.where(times > 0, np.log(np.maximum(times, 1)), NEG)
    return cf, masks.reshape(P, 15 * P), hot


class Panel:

    def __init__(self, weight, col, width, kts, per=2, row0=0, source="x"):
        self.weight, self.col, self.width, self.kts, self.per = weight, col, width, kts, per
        self.row0, self.source = row0, source
        self.chunks = len(kts) // per


def plan():
    full = list(range(KT))
    a0 = 0
    b0 = 4 * W
    c0 = b0 + 3 * HEADS_B * P + HEADS_B
    first = [Panel("w_in", a0 + W * j, W, full) for j in range(4)]
    first.insert(1, Panel("w_in", b0 + 3 * HEADS_B * P, HEADS_B, full, per=KT))
    for base in (b0, c0):
        first += [Panel("w_in", base + HEADS_B * P * m + 384 * half, 384, full)
                  for half in range(2) for m in range(3)]
    out1 = [Panel("w_out", W * j, W, full[:12]) for j in range(4)]
    out1 += [Panel("w_out", W * j, W, full[12:]) for j in range(4)]
    ple = []
    for j in range(4):
        ple += [Panel("w_ple_proj", W * j, W, [0, 1], source="p"), Panel("w_ple_gate", W * j, W, full)]
    second = [Panel("w_in_2", c, W, full) for c in
              (3072, 3584, 4096, 4608, 5120, 5632, 0, 1024, 2048, 512, 1536, 2560)]
    second.insert(1, Panel("w_in_2", 6144, 32, full, per=KT))
    out2 = [Panel("w_out_2", W * j, W, full[8:] + full[:4]) for j in range(4)]
    out2 += [Panel("w_out_2", W * j, W, full[4:8]) for j in range(4)]
    return first, out1, ple, second, out2


def build(nc, g, out, const_f, const_m, hot):
    first, out1, ple, second, out2 = plan()
    straight = {}
    ends = {}
    n = q = 0

    def lay(panels):
        nonlocal n, q
        begin = n
        for p in panels:
            for j in range(p.chunks):
                straight[n] = (p, q, j)
                n += 1
            ends[n - 1] = q
            q += 1
        return begin, n

    IN1, IN1_END = lay(first)
    OUT1, OUT1_END = lay(out1)
    FFN1, FFN1_Q = n, q
    n += GRP * NG
    q += 6 * NG
    PLE, PLE_END = lay(ple)
    PLE_Q = straight[PLE][1]
    IN2, IN2_END = lay(second)
    IN2_Q = straight[IN2][1]
    OUT2, OUT2_END = lay(out2)
    OUT1_Q, OUT2_Q = straight[OUT1][1], straight[OUT2][1]
    FFN2, FFN2_Q = n, q
    n += GRP * NG
    TOTAL = n

    x_d = g["x"].rearrange("b (t p) d -> p (b t) d", p=P)
    out_d = out.rearrange("b (t p) d -> p (b t) d", p=P)
    wd = {k: (g[k].rearrange("a r c -> (a r) c")) for k in (
        "w_in", "w_out", "w_gate", "w_up", "w_down", "w_ple_gate", "w_ple_proj", "w_in_2", "w_out_2",
        "w_gate_2", "w_up_2", "w_down_2")}
    VEC_DMAS = 21
    bias_rows = nc.dram_tensor("bias_rows", [HEADS_2, 512], F32, kind="Internal").ap()

    with ExitStack() as ctx:
        def sb(name, shape, dt=F32, stack=ctx):
            return stack.enter_context(nc.sbuf_tensor(name, shape, dt))

        def sem(name):
            return ctx.enter_context(nc.semaphore(name))

        acc = ctx.enter_context(nc.psum_tensor("acc", [P, 4, 512], F32))
        mb = ctx.enter_context(nc.psum_tensor("mb", [P, 4, 512], F32))

        raw = sb("raw", [P, RAW, 2 * W])
        w_hi = sb("w_hi", [P, SPL, 2 * W], F32R)
        w_lo = sb("w_lo", [P, SPL, 2 * W], F32R)
        x_hi = sb("x_hi", [P, KT, T], F32R)
        x_lo = sb("x_lo", [P, KT, T], F32R)
        h = sb("h", [P, TB, D])
        cf = sb("cf", [P, 3 * P])
        ident, upto, ones = cf[:, 0:P], cf[:, P:2 * P], cf[:, 2 * P:3 * P]
        masks = sb("masks", [P, 15, P], I8)
        NV = 5 * KT + 1 + 4 + 8 + 8
        vecs = sb("vecs", [P, NV])
        NORM = [vecs[:, KT * j:KT * (j + 1)] for j in range(5)]
        V0 = 5 * KT
        hgrn_gain = vecs[:, V0:V0 + 1]
        qk_gain = [vecs[:, V0 + 1 + j:V0 + 2 + j] for j in range(4)]
        gate_bias = [vecs[:, V0 + 5 + 4 * d:V0 + 9 + 4 * d] for d in range(2)]
        gla_gain = vecs[:, V0 + 13:V0 + 21]
        conv = sb("conv", [P, 4, 44])
        small = sb("small", [P, 128])
        half = small[:, 0:1]
        sums = small[:, 88:104].rearrange("p (m t d) -> p m t d", m=2, t=TB)
        rstd = [small[:, 104 + 2 * i:106 + 2 * i] for i in range(6)]
        hsq, hrs = small[:, 8:16], small[:, 16:24]
        full01 = small[:, 24:32]
        negmax, rowsum, rowinv = small[:, 32:36], small[:, 36:40], small[:, 40:44]
        fbias = small[:, 44:50]
        lf = small[:, 52:64].rearrange("p (t h) -> p t h", t=2)
        nlf = small[:, 64:76].rearrange("p (t h) -> p t h", t=2)
        fcum = small[:, 76:88].rearrange("p (t h) -> p t h", t=2)
        scanm = sb("scanm", [P, T])
        junk = sb("junk", [P, W])


        with ExitStack() as s1:
            tail = sb("tail", [P, TB, HEADS_B], F32, s1)
            a_reg = sb("a_reg", [P, 4, 1024], F32, s1)
            bc_reg = sb("bc_reg", [P, 12, 768], F32, s1)
            AT1 = sb("AT1", [P, 4, TB, T], F32, s1)
            X1 = sb("X1", [P, 2, 512], F32, s1)
            LG1 = sb("LG1", [P, 1024], F32, s1)
            B1 = sb("B1", [P, 1024], F32, s1)
            L1 = sb("L1", [P, 2, 512], F32, s1)
            WT1 = sb("WT1", [P, 2, 512], F32, s1)
            causal = sb("causal", [P, 384], F32, s1)
            alibi = sb("alibi", [P, 384], F32, s1)
            stage = sb("stage", [P, 3, P], F32, s1)
            table = sb("table", [BUCKETS + 1, HEADS_2], F32, s1)
            hot_sb = sb("hot_sb", [BUCKETS + 1, 512], F32, s1)
        rows_sb = LG1[0:HEADS_2, 0:512]
        masks_f = bc_reg[:, 0:3, :].rearrange("p a n -> p (a n)")[:, 0:15 * P]
        with ExitStack() as s2:
            h_hi = sb("h_hi", [P, FT, T], F32R, s2)
            h_lo = sb("h_lo", [P, FT, T], F32R, s2)
            gate_n = sb("gate_n", [P, TB, W], F32, s2)
            up_n = sb("up_n", [P, TB, W], F32, s2)
            cv = sb("cv", [P, FT, T], F32, s2)
            pn = sb("pn", [P, TB, W], F32, s2)
            p_in = sb("p_in", [P, TB, 256], F32, s2)
            p_hi = sb("p_hi", [P, 2, T], F32R, s2)
            p_lo = sb("p_lo", [P, 2, T], F32R, s2)
            fin_g = sb("fin_g", [P, D], F32, s2)
            result = sb("result", [P, TB, D], F32, s2)
        with ExitStack() as s3:
            tail2 = sb("tail2", [P, TB, 32], F32, s3)
            reg2 = sb("reg2", [P, 12, 1024], F32, s3)
            Z = sb("Z", [P, ZR, 384], F32, s3)
            AT2 = sb("AT2", [P, 4, TB, T], F32, s3)
            X2 = sb("X2", [P, 2, 512], F32, s3)
            BF2 = sb("BF2", [P, 1024], F32, s3)
            BB2 = sb("BB2", [P, 1024], F32, s3)
            L2 = sb("L2", [P, 2, 512], F32, s3)
            WT2 = sb("WT2", [P, 2, 512], F32, s3)
            lr_t = L2[0:16, :, 0:T]
            gate_w = WT2[0:16, :, :]

        raw_in = [sem(f"raw_in{s}") for s in range(RAW)]
        hi_ready = sem("hi_ready")
        lo_ready = sem("lo_ready")
        mm_done = sem("mm_done")
        panel_out = [sem("panel_out_even"), sem("panel_out_odd")]
        x_in, const_in, gain_in, vec_in = sem("x_in"), sem("const_in"), sem("gain_in"), sem("vec_in")
        gain_turned, gain_out = sem("gain_turned"), sem("gain_out")
        pool_set, table_one = sem("pool_set"), sem("table_one")
        vec_turned, vec_out, rows_made, rows_out, rows_kept = (
            sem("vec_turned"), sem("vec_out"), sem("rows_made"), sem("rows_out"), sem("rows_kept"))
        squares_out, squares_summed, rstd_ready = sem("squares_out"), sem("squares_summed"), sem("rstd_ready")
        h_turned, xhi_ready, xlo_ready = sem("h_turned"), sem("xhi_ready"), sem("xlo_ready")
        gate_turned, conv_begun, conv_first, conv_done = (
            sem("gate_turned"), sem("conv_begun"), sem("conv_first"), sem("conv_done"))
        gelu_done, up_turned, prod_done = sem("gelu_done"), sem("up_turned"), sem("prod_done")
        hhi_ready, hlo_ready = sem("hhi_ready"), sem("hlo_ready")
        p_landed, p_turned, phi_ready, plo_ready = (
            sem("p_landed"), sem("p_turned"), sem("phi_ready"), sem("plo_ready"))
        ple_added = sem("ple_added")
        dq_turned, dq_out, dk_turned, dk_out = sem("dq_turned"), sem("dq_out"), sem("dk_turned"), sem("dk_out")
        log1p_out, logf_out, decay_out = sem("log1p_out"), sem("logf_out"), sem("decay_out")
        lr_turned, lr_out, gates_made, gate_w_in = sem("lr_turned"), sem("lr_out"), sem("gates_made"), sem("gate_w_in")
        expo_out, exp_out, x_out, pair_made, pair_kept = (
            sem("expo_out"), sem("exp_out"), sem("x_out"), sem("pair_made"), sem("pair_kept"))
        at_zero, o_made, o_out, og_out, osq_out, orstd, o_scaled, o_turned, o_kept = (
            sem("at_zero"), sem("o_made"), sem("o_out"), sem("og_out"), sem("osq_out"), sem("orstd"),
            sem("o_scaled"), sem("o_turned"), sem("o_kept"))
        forget_exp, forget_out, fcum_made, fcum_out = (
            sem("forget_exp"), sem("forget_out"), sem("fcum_made"), sem("fcum_out"))
        prep_sq, prep_rstd, prep_scaled, prep_turned, prep_out = (
            sem("prep_sq"), sem("prep_rstd"), sem("prep_scaled"), sem("prep_turned"), sem("prep_out"))
        scores_made, logits_out, exps_out, probs_out, probs_turned, probs_kept, head_made, head_out = (
            sem("scores_made"), sem("logits_out"), sem("exps_out"), sem("probs_out"),
            sem("probs_turned"), sem("probs_kept"), sem("head_made"), sem("head_out"))
        z_in = [sem(f"z_in{r}") for r in range(ZR)]
        ohi_ready, olo_ready = sem("ohi_ready"), sem("olo_ready")
        fin_in, fin_done, out_stored = sem("fin_in"), sem("fin_done"), sem("out_stored")
        act_link, dve_link, pool_link = sem("act_link"), sem("dve_link"), sem("pool_link")

        HG = dict(turn_q=8, turn_f=17, levels=20, make_o=57)
        PREP1 = {5: 62, 6: 64, 8: 66, 9: 74, 11: 99, 12: 101, 14: 117, 15: 121}
        HEAD1 = [78 + 3 * i for i in range(6)] + [106, 109, 112, 129, 131, 133]
        b = IN2
        PREP2 = {7: b + 76, 8: b + 77, 10: b + 97, 11: b + 98}
        HEAD2 = [b + 79 + 2 * i for i in range(8)] + [b + 100 + 2 * i for i in range(8)]
        OSPLIT = {IN1_END - 8 + s: [s] for s in range(6)} | {OUT1 + 22: [6, 7]}
        OSPLIT |= {IN2_END - 4 + s: [4 + s] for s in range(4)} | {OUT2 + 1: [0, 1], OUT2 + 22: [2, 3]}
        OSPLIT_ORDER = [s for n in sorted(OSPLIT) for s in OSPLIT[n]]
        TAIL1, TAIL2 = FFN1 + 16 + (NG - 1) * GRP, FFN2 + 16 + (NG - 1) * GRP
        TURN = [(-4 + d, 0, d) for d in range(4)]
        TURN += [(OUT1 + 26, 1, 0), (OUT1 + 28, 1, 1), (OUT1 + 30, 1, 2), (FFN1, 1, 3)]
        TURN += [(TAIL1 + 2, 2, 0), (TAIL1 + 4, 2, 1), (TAIL1 + 6, 2, 2), (PLE, 2, 3)]
        TURN += [(PLE_END - 7 + 2 * d, 3, d) for d in range(3)] + [(IN2, 3, 3)]
        TURN += [(OUT2 + 26, 4, 0), (OUT2 + 30, 4, 2), (FFN2, 4, 1), (FFN2 + 1, 4, 3)]
        LEVELS1 = [(0, hp, lv) for hp in range(2) for lv in range(8)]
        LEVELS2 = [(d, hp, lv) for d in range(2) for hp in range(2) for lv in range(8)]

        def level_slot(block, j):
            return HG["levels"] + 2 * j if block == 0 else IN2 + 19 + 3 * j // 2

        def chunk_of(value, i):
            return value if i is None else i * GRP + value

        def grown(value, i, step):
            return value if i is None else i * step + value

        def wait_panel(eng, q):
            eng.wait_ge(panel_out[q % 2], q // 2 + 1)

        def wait_h(eng, i, d):
            if i == 0:
                eng.wait_ge(x_in, 32)
            elif i == 3:
                eng.wait_ge(ple_added, d + 1)
            else:
                wait_panel(eng, {1: OUT1_Q + 4, 2: FFN1_Q + 6 * NG - 4, 4: OUT2_Q + 4, 5: FFN2_Q + 6 * NG - 4}[i] + d)

        def turned_before(i, pair):
            at = [(j, d) for _, j, d in TURN].index((i, pair // 2))
            return 2 * at + pair % 2 + 1

        def norm_of(q):
            return 0 if q < OUT1_Q else 1 if q < PLE_Q else 2 if q < IN2_Q else 3 if q < OUT2_Q else 4

        def cut(buf, slot, per, width):
            return buf[:, slot, 0:per * width].rearrange("p (k n) -> p k n", k=per)

        def shape_of(n):
            if n in straight:
                return straight[n][0].per, straight[n][0].width
            return 2, W

        def panel_in(t, q):
            return acc[:, 2 * (q % 2) + t, :]

        def region(q):
            j = q if q < IN2_Q else q - IN2_Q
            if q < IN2_Q:
                r = a_reg[:, max(j - 1, 0), :] if j <= 4 else bc_reg[:, j - 5, :]
            else:
                r = reg2[:, max(j - 1, 0), :]
            wide = 384 if q < IN2_Q and j > 4 else W
            return r.rearrange("p (t n) -> p t n", t=TB), r.rearrange("p (k t) -> p k t", t=T), wide // P

        def o_turned_at(kt, block):
            if block == 0:
                if kt < 4:
                    return a_reg[:, 3, T * kt:T * kt + T]
                hh = kt - 4
                return bc_reg[:, 6 * (hh // 6) + 3 * (hh % 6 // 3), T * (hh % 3):T * (hh % 3) + T]
            if kt >= 8:
                return reg2[:, 4 + (kt - 8) // 4, T * (kt % 4):T * (kt % 4) + T]
            return reg2[:, 6 + 3 * (kt // 4), T * (kt % 4):T * (kt % 4) + T]

        def head(u):
            if u < 12:
                base, s = 6 * (u // 6) + 3 * (u % 6 // 3), T * (u % 3)
                v = bc_reg[:, base + 2, :].rearrange("p (t n) -> p t n", t=TB)[:, :, P * (u % 3):P * (u % 3) + P]
                return bc_reg[:, base, s:s + T], bc_reg[:, base + 1, s:s + T], v, bc_reg[:, base, s:s + T], P
            e = u - 12
            base, s, lo = 6 + 3 * (e // 8), T * (e % 8 // 2), 64 * (e % 2)
            v = reg2[:, base + 2, :].rearrange("p (t n) -> p t n", t=TB)[:, :, 64 * (e % 8):64 * (e % 8) + 64]
            q = reg2[lo:lo + 64, base, s:s + T]
            return q, reg2[lo:lo + 64, base + 1, s:s + T], v, q, 64

        LOGITS = [((0, 128), (128, 256)), ((0, 256), (256, 256))]

        block = ctx.enter_context(nc.Block())

        @block.sync
        def _(sp):
            sp.dma_start(cf[:, :], const_f[:, 0:3 * P]).then_inc(const_in, 16)
            for t in range(TB):
                sp.dma_start(h[:, t, :], x_d[:, t, :]).then_inc(x_in, 16)

            def load(n, base, i, src, per, width):
                if i is not None or base >= RAW:
                    sp.wait_ge(lo_ready, n - (RAW - 1))
                sp.dma_start(cut(raw, base % RAW, per, width),
                             src.rearrange("(k p) n -> p k n", p=P)).then_inc(raw_in[base % RAW], 16)

            def load_straight(a, z):
                for n in range(a, z):
                    p, _, j = straight[n]
                    rows = p.kts[j * p.per] * P
                    load(n, n, None, wd[p.weight][rows:rows + p.per * P, p.col:p.col + p.width], p.per, p.width)

            def load_ffn(base, gate, up, down):
                def group(i, first, last):
                    at = base + (16 if not first else 0)
                    col = 0 if i is None else i * W + W
                    prev = (NG - 1) * W if last else (i * W if i is not None else None)
                    for c in range(16 if first else GRP):
                        if last and c < 16:
                            continue
                        cc = c
                        b0 = at + c
                        if last:
                            b0 = base + 16 + (NG - 1) * GRP + c - 16
                        n = chunk_of(b0, i)
                        if c < 16:
                            wsrc = wd[gate if c < 8 else up]
                            src = wsrc[(cc % 8) * 2 * P:(cc % 8 + 1) * 2 * P, bass.ds(col, W)]
                        else:
                            row = prev + (c % 2) * 2 * P
                            src = wd[down][bass.ds(row, 2 * P), (c - 16) // 2 * W:((c - 16) // 2 + 1) * W]
                        load(n, b0, i, src, 2, W)

                group(None, True, False)
                with sp.Fori(0, NG - 1) as i:
                    group(i, False, False)
                group(None, False, True)

            load_straight(IN1, FFN1)
            load_ffn(FFN1, "w_gate", "w_up", "w_down")
            load_straight(PLE, FFN2)
            load_ffn(FFN2, "w_gate_2", "w_up_2", "w_down_2")
            for t in range(TB):
                sp.wait_ge(fin_done, t + 1)
                sp.dma_start(out_d[:, t, :], result[:, t, :]).then_inc(out_stored, 16)
            sp.wait_ge(out_stored, 16 * TB)

        @block.gpsimd
        def _(pool):
            links = [0]

            def link(ins):
                links[0] += 1
                ins.then_inc(pool_link, 1)
                pool.wait_ge(pool_link, links[0])

            pool.memset(small[:, 0:1], -0.5).then_inc(pool_set, 1)
            pool.memset(scanm[:, :], 1.0).then_inc(pool_set, 1)
            pool.memset(table[:, :], 1.0).then_inc(table_one, 1)
            pool.wait_ge(pool_set, 2)
            pool.memset(scanm[:, 0:T:64], 0.0).then_inc(pool_set, 1)
            pool.memset(AT1[:, :, :, :], 0.0).then_inc(at_zero, 1)

            def inverse_root(to, sums, count, done):
                link(pool.tensor_scalar(to, sums, 1.0 / count, EPS, ALU.mult, ALU.add))
                pool.tensor_tensor(to, to, small[:, 0:1].to_broadcast([P, to.shape[1]]), ALU.pow).then_inc(done, 1)

            def norm(i):
                pool.wait_ge(squares_summed, i + 1)
                inverse_root(rstd[i], rstd[i], D, rstd_ready)

            norm(0)
            pool.wait_ge(osq_out, 1)
            inverse_root(hrs, hsq, P, orstd)
            for j in range(len(PREP1)):
                pool.wait_ge(prep_sq, j + 1)
                inverse_root(hrs[:, 0:6], hsq[:, 0:6], P, prep_rstd)
            norm(1)
            norm(2)
            norm(3)
            pool.wait_ge(gate_w_in, 32)
            pool.memset(AT2[:, :, :, :], 0.0).then_inc(at_zero, 1)
            pool.wait_ge(osq_out, 2)
            inverse_root(hrs, hsq, T, orstd)
            norm(4)
            norm(5)

        @block.tensor
        def _(pe):
            def turn(out, in_):
                return pe.transpose(out, in_, ident)

            def multiply(n, base, i, per, width, kts, hi, lo, pair, first, last):
                pe.wait_ge(lo_ready, n + 1)
                wh, wl = cut(w_hi, base % SPL, per, width), cut(w_lo, base % SPL, per, width)
                for k in range(per):
                    for t in range(TB):
                        to = acc[:, 2 * pair + t, 0:width]
                        s = slice(P * t, P * t + P)
                        for m, (xx, ww) in enumerate(((hi, wh), (hi, wl), (lo, wh))):
                            mm = pe.matmul(to, xx[:, kts[k], s], ww[:, k, :], start=first and k == 0 and m == 0,
                                           stop=last and k == per - 1 and m == 2)
                mm.then_inc(mm_done, 1)

            def turn_h(k):
                _, i, d = TURN[k]
                wait_h(pe, i, d)
                if k >= 2:
                    pe.wait_ge(xlo_ready, 2 * (k - 1))
                for m in range(4):
                    for t in range(TB):
                        c = P * (4 * d + m)
                        mm = turn(mb[:, 2 * (k % 2) + m // 2, T * (m % 2) + P * t:T * (m % 2) + P * t + P],
                                  h[:, t, c:c + P])
                    if m % 2:
                        mm.then_inc(h_turned, 1)

            def turn_panel(src, banks, tiles, done):
                for k in range(tiles):
                    for t in range(TB):
                        at = T * k + P * t
                        mm = turn(mb[:, banks + at // 512, at % 512:at % 512 + P], src[:, t, P * k:P * k + P])
                mm.then_inc(done, 1)

            def pair_levels(block, j):
                steps = LEVELS1 if block == 0 else LEVELS2
                d, hp, lv = steps[j]
                k = j + (16 if block else 0)
                X = (X1 if block == 0 else X2)[:, k % 2, :].rearrange("p (h t) -> p h t", h=2)
                pe.wait_ge(x_out, k + 1)
                if j >= 2:
                    pe.wait_ge(pair_kept, (17 if block else 0) + j)
                for e in range(2):
                    if lv == 7:
                        ks, qs = (0, P) if d == 0 else (P, 0)
                        mm = pe.matmul(mb[:, k % 2, P * e:P * e + P], X[:, e, ks:ks + P], X[:, e, qs:qs + P],
                                       start=True, stop=True)
                    else:
                        for t in range(TB):
                            s = slice(P * t, P * t + P)
                            mm = pe.matmul(mb[:, k % 2, 256 * e + P * t:256 * e + P * t + P], X[:, e, s], X[:, e, s],
                                           start=True, stop=True)
                mm.then_inc(pair_made, 1)

            def diagonal(block):
                q, k = (a_reg[:, 0, :], a_reg[:, 1, :]) if block == 0 else (reg2[:, 0, :], reg2[:, 1, :])
                for e in range(4):
                    for t in range(TB):
                        s = slice(T * e + P * t, T * e + P * t + P)
                        to = mb[:, 2 + e // 2, 256 * (e % 2) + P * t:256 * (e % 2) + P * t + P]
                        for again in range(block + 1):
                            mm = pe.matmul(to, k[:, s], q[:, s], start=again == 0, stop=again == block)
                mm.then_inc(pair_made, 1)

            def make_o(block):
                AT = AT1 if block == 0 else AT2
                dv = P if block == 0 else T
                pe.wait_ge(pair_kept, 17 if block == 0 else 50)
                for t in range(TB):
                    for e in range(4):
                        to = mb[:, t, P * e:P * e + P] if block == 0 else mb[:, 2 * t + e // 2, T * (e % 2):T * (e % 2) + T]
                        srcs = [s for s in range(TB) if block == 1 or s <= t]
                        for s in srcs:
                            if block == 0:
                                v = a_reg[:, 2, :].rearrange("p (t n) -> p t n", t=TB)[:, s, P * e:P * e + P]
                            else:
                                v = reg2[:, 2 + e // 2, :].rearrange("p (t n) -> p t n", t=TB)[:, s, T * (e % 2):T * (e % 2) + T]
                            mm = pe.matmul(to, AT[:, e, s, P * t:P * t + P], v, start=s == srcs[0], stop=s == srcs[-1])
                mm.then_inc(o_made, 1)

            def scores(u):
                q, k, _, _, rows = head(u)
                to = mb[:, u % 2, :]
                if u >= 2:
                    pe.wait_ge(logits_out, u - 1)
                fox = u < HEADS_B
                second = u >= 12
                for t, (c, keys) in enumerate(LOGITS[second]):
                    mm = pe.matmul(to[:, c:c + keys], q[:, P * t:P * t + P], k[:, 0:keys], start=True, stop=not fox)
                    if fox:
                        for s in range(t + 1):
                            row = nlf[:, s, u:u + 1].to_broadcast([P, P])
                            if s < t:
                                pe.matmul(to[:, c + P:c + 2 * P], row, ones, start=False, stop=False)
                            mm = pe.matmul(to[:, c + P * s:c + P * s + P], row, upto, start=False, stop=s == t)
                return mm

            def turn_probs(u):
                second = u >= 12
                L = (L2 if second else L1)[:, u % 2, :]
                pe.wait_ge(probs_out, u + 1)
                if u >= 2:
                    pe.wait_ge(head_out, u - 1)
                to = mb[:, 2 + u % 2, :]
                if second:
                    spots = [(0, 0), (P, T), (T, P), (T + P, T + P)]
                else:
                    spots = [(0, 0), (P, P), (2 * P, T)]
                for src, dst in spots:
                    mm = turn(to[:, dst:dst + P], L[:, src:src + P])
                mm.then_inc(probs_turned, 1)

            def head_values(u):
                _, _, v, _, rows = head(u)
                second = u >= 12
                WT = (WT2 if second else WT1)[:, u % 2, :]
                lo = 64 * (u % 2) if second else 0
                to = mb[lo:lo + rows, 2 + u % 2, :]
                pe.wait_ge(probs_kept, u + 1)
                pe.matmul(to[:, 0:T], v[:, 0, :], WT[:, 0:T], start=True, stop=False)
                if second:
                    mm = pe.matmul(to[:, 0:T], v[:, 1, :], WT[:, T:2 * T], start=False, stop=True)
                else:
                    mm = pe.matmul(to[:, P:T], v[:, 1, :], WT[:, T:T + P], start=False, stop=True)
                mm.then_inc(head_made, 1)

            def head_steps(n, slots, u0):
                for i, s in enumerate(slots):
                    u = u0 + i
                    if n == s:
                        if u == 0:
                            pe.wait_ge(prep_out, 4)
                            pe.wait_ge(fcum_out, 1)
                        if u == 6:
                            pe.wait_ge(prep_out, 6)
                        if u == 9:
                            pe.wait_ge(prep_out, 8)
                        if u == 12:
                            pe.wait_ge(prep_out, 10)
                        if u == 20:
                            pe.wait_ge(prep_out, 12)
                        scores(u).then_inc(scores_made, 1)
                    if n == s + 2:
                        turn_probs(u)
                    if n == s + 3:
                        head_values(u)

            def beside(n):
                if n == 2:
                    pe.wait_ge(vec_in, 16 * VEC_DMAS)
                    pe.wait_ge(xlo_ready, 8)
                    for k, (s, rows) in enumerate(((0, NV), (1, 88), (2, 88))):
                        mm = pe.transpose(mb[:, 0, P * k:P * k + rows], stage[0:rows, s, :], ident[0:rows, 0:rows])
                    mm.then_inc(vec_turned, 1)
                    pe.matmul(mb[0:HEADS_2, 1, :], table[:, :], hot_sb[:, :], start=True, stop=True).then_inc(rows_made, 1)
                if n == 10:
                    pe.wait_ge(forget_out, 1)
                    pe.matmul(mb[:, 3, 0:6], upto, lf[:, 0, :], start=True, stop=True)
                    pe.matmul(mb[:, 3, 6:12], ones, lf[:, 0, :], start=True, stop=False)
                    pe.matmul(mb[:, 3, 6:12], upto, lf[:, 1, :], start=False, stop=True).then_inc(fcum_made, 1)
                if n == HG["turn_q"]:
                    wait_panel(pe, 0)
                    pe.wait_ge(rows_out, 1)
                    turn_panel(region(0)[0], 0, 4, dq_turned)
                if n == HG["turn_f"]:
                    wait_panel(pe, 2)
                    pe.wait_ge(fcum_out, 1)
                    turn_panel(region(2)[0], 2, 4, dk_turned)
                if n == HG["levels"] - 1:
                    pe.wait_ge(dk_out, 1)
                    diagonal(0)
                for j in range(len(LEVELS1)):
                    if n == level_slot(0, j) + 2:
                        pair_levels(0, j)
                if n == HG["make_o"]:
                    make_o(0)
                if n == HG["make_o"] + 4:
                    pe.wait_ge(o_scaled, 1)
                    turn_panel(LG1[:, :].rearrange("p (t n) -> p t n", t=TB), 2, 4, o_turned)
                for j, (panel, s) in enumerate(PREP1.items()):
                    if n == s + 2:
                        pe.wait_ge(prep_scaled, j + 1)
                        if j:
                            pe.wait_ge(prep_out, j)
                        if j in (4, 6):
                            pe.wait_ge(head_out, 6 if j == 4 else 9)
                        turn_panel(region(panel)[0], 0, 3, prep_turned)
                head_steps(n, HEAD1, 0)

                if n == IN2 + 10:
                    wait_panel(pe, IN2_Q + 1)
                    pe.wait_ge(dq_out, 2)
                    for d in range(2):
                        for t in range(TB):
                            mm = turn(mb[0:16, 0, T * d + P * t:T * d + P * t + P], tail2[:, t, 16 * d:16 * d + 16])
                    mm.then_inc(lr_turned, 1)
                if n == IN2 + 12:
                    pe.wait_ge(lr_out, 1)
                    pe.wait_ge(gate_w_in, 32)
                    for d in range(2):
                        for e in range(4):
                            mm = pe.matmul(mb[:, 2 * d + e // 2, T * (e % 2):T * (e % 2) + T],
                                           gate_w[:, d, P * e:P * e + P], lr_t[:, d, :], start=True, stop=True)
                    mm.then_inc(gates_made, 1)
                if n == IN2 + 8:
                    wait_panel(pe, IN2_Q)
                    turn_panel(region(IN2_Q)[0], 0, 4, dq_turned)
                if n == IN2 + 17:
                    wait_panel(pe, IN2_Q + 2)
                    pe.wait_ge(log1p_out, 4)
                    turn_panel(region(IN2_Q + 2)[0], 2, 4, dk_turned)
                if n == IN2 + 18:
                    pe.wait_ge(dk_out, 2)
                    pe.wait_ge(dq_out, 2)
                    diagonal(1)
                for j in range(len(LEVELS2)):
                    if n == level_slot(1, j) + 2:
                        pair_levels(1, j)
                if n == IN2 + 70:
                    make_o(1)
                if n == IN2 + 74:
                    pe.wait_ge(o_scaled, 2)
                    src = reg2[:, 0:2, :].rearrange("p r n -> p (r n)").rearrange("p (t n) -> p t n", t=TB)
                    turn_panel(src, 0, 8, o_turned)
                for j, (panel, s) in enumerate(PREP2.items()):
                    if n == s:
                        pe.wait_ge(panel_out[(IN2_Q + panel) % 2], (IN2_Q + panel) // 2 + 1)
                        if j == 0:
                            pe.wait_ge(o_kept, 2)
                        if j == 2:
                            pe.wait_ge(head_out, 20)
                        turn_panel(region(IN2_Q + panel)[0], 2 * (j % 2), 4, prep_turned)
                head_steps(n, HEAD2, 12)
                for k, (at, _, _) in enumerate(TURN):
                    if n == at:
                        turn_h(k)
                if n == TAIL1:
                    pe.wait_ge(p_landed, 16)
                    pe.wait_ge(prod_done, NG)
                    turn_panel(p_in, 2, 2, p_turned)

            def straight_part(a, z):
                for n in range(a, z):
                    p, q, j = straight[n]
                    if j == 0 and q >= 2:
                        pe.wait_ge(panel_out[q % 2], q // 2)
                    hi, lo, kts = x_hi, x_lo, [k for k in p.kts[j * p.per:(j + 1) * p.per]]
                    if p.source == "p":
                        hi, lo = p_hi, p_lo
                        pe.wait_ge(plo_ready, 1)
                    elif p.weight.startswith("w_out"):
                        from8 = 8 if p.weight == "w_out_2" else 0
                        pe.wait_ge(olo_ready, OSPLIT_ORDER.index(kts[0] // 2, from8) + 1)
                    elif q in (0, PLE_Q + 1, IN2_Q):
                        pe.wait_ge(xlo_ready, turned_before(norm_of(q), kts[0] // 2))
                    multiply(n, n, None, p.per, p.width, kts, hi, lo, q % 2, j == 0, j == p.chunks - 1)
                    beside(n)

            def ffn_part(which, base, base_q):
                norm_no = 1 if which == 0 else 4
                groups = NG * which

                def group(i, first, last):
                    if not last:
                        at = base if first else base + 16
                        qq = base_q if first else base_q + 2
                    else:
                        at, qq = base + 16 + (NG - 1) * GRP - 16, base_q + 2 + 6 * (NG - 1) - 2
                    number = grown(groups + (0 if first else 1), i, 1)
                    for c in range(16 if last else 0, 16 if first else GRP):
                        par = (qq + (c // 8 if c < 16 else 2 + (c - 16) // 2)) % 2
                        part = c // 8 if c < 16 else 2 + (c - 16) // 2
                        begins = c % 8 == 0 if c < 16 else c % 2 == 0
                        if begins:
                            pe.wait_ge(panel_out[par], grown((qq + part) // 2, i, 3))
                        n = chunk_of(at + c, i)
                        if first and c < 8:
                            pe.wait_ge(xlo_ready, turned_before(norm_no, c))
                        if c == 16:
                            pe.wait_ge(hlo_ready, groups + NG if last else grown(groups + 1, i, 1))
                        if c < 16:
                            multiply(n, at + c, i, 2, W, (2 * (c % 8), 2 * (c % 8) + 1), x_hi, x_lo, par,
                                     c % 8 == 0, c % 8 == 7)
                        else:
                            multiply(n, at + c, i, 2, W, (2 * (c % 2), 2 * (c % 2) + 1), h_hi, h_lo, par,
                                     c % 2 == 0, c % 2 == 1)
                        if first or last:
                            beside(at + c)
                        if last:
                            continue
                        if which == 0 and c == 9:
                            pe.wait_ge(panel_out[qq % 2], grown(qq // 2 + 1, i, 3))
                            if not first:
                                pe.wait_ge(conv_done, grown(1, i, 1))
                            turn_panel(gate_n, 0, FT, gate_turned)
                        if c == 15 and first or c == 17:
                            pe.wait_ge(panel_out[(qq + 1) % 2], grown((qq + 1) // 2 + 1, i, 3))
                            if not first:
                                pe.wait_ge(hlo_ready if which else prod_done, number)
                            turn_panel(up_n, 2 if which == 0 else 0, FT, up_turned)

                group(None, True, False)
                with pe.Fori(0, NG - 1) as i:
                    group(i, False, False)
                group(None, False, True)

            pe.wait_ge(const_in, 16)
            pe.wait_ge(gain_in, 16)
            pe.transpose(acc[:, 0, 0:KT], stage[0:KT, 0, :], ident[0:KT, 0:KT]).then_inc(gain_turned, 1)
            pe.wait_ge(gain_out, 1)
            for n in range(-4, 0):
                beside(n)
            straight_part(IN1, FFN1)
            ffn_part(0, FFN1, FFN1_Q)
            straight_part(PLE, FFN2)
            ffn_part(1, FFN2, FFN2_Q)

        @block.scalar
        def _(act):
            links = [0]

            def link(ins):
                links[0] += 1
                ins.then_inc(act_link, 1)
                act.wait_ge(act_link, links[0])

            def split_hi(n, base, i, per, width):
                act.wait_ge(raw_in[base % RAW], grown(16 * (base // RAW + 1), i, 16 * GRP // RAW))
                if i is not None or base >= SPL:
                    act.wait_ge(mm_done, n - (SPL - 1))
                act.activation(cut(w_hi, base % SPL, per, width), cut(raw, base % RAW, per, width),
                               ACT.Copy).then_inc(hi_ready, 1)

            def copy_panel(q, to, func=ACT.Copy, scaled=True):
                width = to.shape[2]
                if scaled:
                    act.wait_ge(rstd_ready, norm_of(q) + 1)
                for t in range(TB):
                    scale = rstd[norm_of(q)][:, t:t + 1] if scaled else 1.0
                    ins = act.activation(to[:, t, :], panel_in(t, q)[:, 0:width], func, scale=scale)
                ins.then_inc(panel_out[q % 2], 1)

            squares = [0]

            def square(i, d):
                wait_h(act, i, d)
                for t in range(TB):
                    if squares[0]:
                        act.wait_ge(squares_out, squares[0])
                    act.activation(junk[:, :], h[:, t, W * d:W * d + W], ACT.Square,
                                   accum_out=sums[:, i % 2, t, d:d + 1]).then_inc(squares_out, 1)
                    squares[0] += 1

            def turned_hi(k):
                _, i, d = TURN[k]
                for pair in range(2):
                    act.wait_ge(h_turned, 2 * k + pair + 1)
                    if i == 3 and d < 3:
                        act.wait_ge(mm_done, PLE_END - 8 + 2 * d + pair + 1)
                    for m in (2 * pair, 2 * pair + 1):
                        kt = 4 * d + m
                        ins = act.activation(x_hi[:, kt, :], mb[:, 2 * (k % 2) + m // 2, T * (m % 2):T * (m % 2) + T],
                                             ACT.Copy, scale=NORM[i][:, kt:kt + 1])
                    ins.then_inc(xhi_ready, 1)
                square(i, d)

            def load_bias(e):
                act.dma_start(Z[:, e % ZR, :], bass.AP(bias_rows.tensor, 512 * e, [[1, P], [1, 384]])).then_inc(z_in[e % ZR], 16)

            def log1p_exp(d, k):
                X = (X1 if k == 0 else X2)[:, :, :].rearrange("p a n -> p (a n)")
                src = mb[:, 2:4, :].rearrange("p a n -> p (a n)") if k == 0 else (BF2 if d == 0 else BB2)[:, :]
                link(act.activation(X, src, ACT.Abs))
                link(act.activation(X, X, ACT.Exp, scale=-1.0))
                act.activation(X, X, ACT.Ln, bias=1.0).then_inc(log1p_out, 1)

            def level_exp(blk, j):
                k = j + 16 * blk
                X = (X1 if blk == 0 else X2)[:, k % 2, :]
                act.wait_ge(expo_out, k + 1)
                act.activation(X, X, ACT.Exp).then_inc(exp_out, 1)

            def head_steps(n, slots, u0):
                for i, s in enumerate(slots):
                    u = u0 + i
                    second = u >= 12
                    L = (L2 if second else L1)[:, u % 2, :]
                    WT = (WT2 if second else WT1)[:, u % 2, :]
                    if n == s + 1:
                        act.wait_ge(logits_out, u + 1)
                        for t, (c, keys) in enumerate(LOGITS[second]):
                            at = 2 * (u % 2) + t
                            ins = act.activation(L[:, c:c + keys], L[:, c:c + keys], ACT.Exp,
                                                 bias=negmax[:, at:at + 1], accum_out=rowsum[:, at:at + 1])
                        ins.then_inc(exps_out, 1)
                        if second and u - 12 + ZR < HEADS_2:
                            load_bias(u - 12 + ZR)
                    if n == s + 3:
                        act.wait_ge(probs_turned, u + 1)
                        if u >= 2:
                            act.wait_ge(head_made, u - 1)
                        width = 512 if second else 384
                        act.activation(WT[:, 0:width], mb[:, 2 + u % 2, 0:width], ACT.Copy).then_inc(probs_kept, 1)
                    if n == s + 4:
                        _, _, _, o, rows = head(u)
                        lo = 64 * (u % 2) if second else 0
                        act.wait_ge(head_made, u + 1)
                        act.activation(o, mb[lo:lo + rows, 2 + u % 2, 0:T], ACT.Copy).then_inc(head_out, 1)

            def beside(n):
                if n in ends and (n < OUT1 or IN2 <= n < OUT2):
                    q = ends[n]
                    act.wait_ge(mm_done, n + 1)
                    if q == 1:
                        copy_panel(q, tail)
                    elif q == IN2_Q + 1:
                        copy_panel(q, tail2)
                    else:
                        copy_panel(q, region(q)[0])
                if n == 2:
                    act.wait_ge(vec_turned, 1)
                    act.activation(vecs[:, KT:NV], mb[:, 0, KT:NV], ACT.Copy).then_inc(vec_out, 1)
                    act.activation(conv[:, :, :], mb[:, 0, P:P + 2 * P].rearrange("p (a n) -> p a n", a=2)[:, :, 0:88],
                                   ACT.Copy).then_inc(vec_out, 1)
                    act.wait_ge(rows_made, 1)
                    act.activation(rows_sb, mb[0:HEADS_2, 1, :], ACT.Copy).then_inc(rows_out, 1)
                    act.wait_ge(rows_out, 1)
                    act.dma_start(bias_rows, rows_sb).then_inc(rows_kept, 16)
                if n == 8:
                    act.wait_ge(forget_exp, 1)
                    flat = small[:, 64:76]
                    link(act.activation(flat, flat, ACT.Exp))
                    act.activation(flat, flat, ACT.Ln, bias=1.0).then_inc(log1p_out, 1)
                if n == 11:
                    act.wait_ge(fcum_made, 1)
                    act.activation(small[:, 76:88], mb[:, 3, 0:12], ACT.Copy).then_inc(fcum_out, 1)
                if n == HG["turn_q"] + 1:
                    act.wait_ge(dq_turned, 1)
                    act.activation(a_reg[:, 0, :], mb[:, 0:2, :].rearrange("p a n -> p (a n)"), ACT.Silu).then_inc(dq_out, 1)
                if n == HG["turn_f"] + 1:
                    act.wait_ge(dk_turned, 1)
                    log1p_exp(0, 0)
                if n == HG["turn_f"] + 2:
                    act.wait_ge(logf_out, 1)
                    act.activation(a_reg[:, 1, :], a_reg[:, 1, :], ACT.Exp).then_inc(dk_out, 1)
                for j in range(len(LEVELS1)):
                    if n == level_slot(0, j):
                        level_exp(0, j)
                if n == HG["make_o"] + 1:
                    act.wait_ge(o_made, 1)
                    act.activation(LG1[:, :], mb[:, 0:2, :].rearrange("p a n -> p (a n)"), ACT.Copy).then_inc(o_out, 1)
                    wait_panel(act, 4)
                    act.activation(a_reg[:, 3, :], a_reg[:, 3, :], ACT.Silu).then_inc(og_out, 1)
                if n == HG["make_o"] + 5:
                    act.wait_ge(o_turned, 1)
                    act.activation(a_reg[:, 3, :], mb[:, 2:4, :].rearrange("p a n -> p (a n)"), ACT.Copy,
                                   scale=hgrn_gain).then_inc(o_kept, 1)
                for j, (panel, s) in enumerate(PREP1.items()):
                    if n == s + 3:
                        act.wait_ge(prep_turned, j + 1)
                        act.activation(bc_reg[:, panel - 5, :], mb[:, 0:2, :].rearrange("p a n -> p (a n)")[:, 0:768],
                                       ACT.Copy, scale=qk_gain[j // 4 * 2 + j % 2]).then_inc(prep_out, 1)
                head_steps(n, HEAD1, 0)

                if n == IN2 + 11:
                    act.wait_ge(lr_turned, 1)
                    act.activation(lr_t, mb[0:16, 0, :].rearrange("p (d t) -> p d t", d=2), ACT.Copy).then_inc(lr_out, 1)
                if n == IN2 + 20:
                    act.wait_ge(rows_kept, 16)
                    for e in range(ZR):
                        load_bias(e)
                if n in (IN2 + 13, IN2 + 15):
                    d = (n - IN2 - 13) // 2
                    B = (BF2, BB2)[d]
                    if d == 0:
                        act.wait_ge(gates_made, 1)
                    else:
                        act.wait_ge(decay_out, 2)
                    for e in range(4):
                        ins = act.activation(B[:, T * e:T * e + T], mb[:, 2 * d + e // 2, T * (e % 2):T * (e % 2) + T],
                                             ACT.Identity, bias=gate_bias[d][:, e:e + 1])
                    link(ins)
                    log1p_exp(d, 1)
                if n == IN2 + 9:
                    act.wait_ge(dq_turned, 2)
                    act.activation(reg2[:, 0, :], mb[:, 0:2, :].rearrange("p a n -> p (a n)"), ACT.Copy,
                                   scale=float(P) ** -0.5).then_inc(dq_out, 1)
                if n == IN2 + 18:
                    act.wait_ge(dk_turned, 2)
                    act.activation(reg2[:, 1, :], mb[:, 2:4, :].rearrange("p a n -> p (a n)"), ACT.Copy).then_inc(dk_out, 1)
                for j in range(len(LEVELS2)):
                    if n == level_slot(1, j):
                        level_exp(1, j)
                if n == IN2 + 50:
                    wait_panel(act, IN2_Q + 6)
                    wait_panel(act, IN2_Q + 5)
                    gr = reg2[:, 4:6, :].rearrange("p a n -> p (a n)")
                    act.activation(gr, gr, ACT.Silu).then_inc(og_out, 1)
                if n == IN2 + 71:
                    act.wait_ge(o_made, 2)
                    act.activation(reg2[:, 0:2, :].rearrange("p a n -> p (a n)"), mb[:, :, :].rearrange("p a n -> p (a n)"),
                                   ACT.Copy).then_inc(o_out, 1)
                if n == IN2 + 75:
                    act.wait_ge(o_turned, 2)
                    for kt in range(8):
                        ins = act.activation(o_turned_at(8 + kt, 1), mb[:, kt // 2, T * (kt % 2):T * (kt % 2) + T], ACT.Copy,
                                             scale=gla_gain[:, kt:kt + 1])
                    ins.then_inc(o_kept, 1)
                for j, (panel, s) in enumerate(PREP2.items()):
                    if n == s + 1:
                        act.wait_ge(prep_turned, 8 + j + 1)
                        src = mb[:, 2 * (j % 2):2 * (j % 2) + 2, :].rearrange("p a n -> p (a n)")
                        act.activation(reg2[:, panel - 1, :], src, ACT.Copy,
                                       scale=64.0 ** -0.5 if j % 2 == 0 else 1.0).then_inc(prep_out, 1)
                head_steps(n, HEAD2, 12)
                if n in OSPLIT:
                    blk = n >= IN2
                    act.wait_ge(mm_done, n + 1)
                    act.wait_ge(o_kept, blk + 1)
                    if n in (IN1_END - 8 + 2, OUT1 + 22, OUT2 + 1, OUT2 + 22):
                        act.wait_ge(head_out, {IN1_END - 6: 9, OUT1 + 22: 12, OUT2 + 1: 20, OUT2 + 22: 28}[n])
                    for pair in OSPLIT[n]:
                        for kt in (2 * pair, 2 * pair + 1):
                            ins = act.activation(x_hi[:, kt, :], o_turned_at(kt, int(blk)), ACT.Copy)
                        ins.then_inc(ohi_ready, 1)
                if PLE <= n < PLE_END and n in ends:
                    q = ends[n]
                    j = (q - PLE_Q) // 2
                    act.wait_ge(mm_done, n + 1)
                    if (q - PLE_Q) % 2 == 0:
                        if j:
                            act.wait_ge(ple_added, j)
                        copy_panel(q, pn, scaled=False)
                    else:
                        copy_panel(q, gate_n, ACT.Sigmoid)
                for k, (at, _, _) in enumerate(TURN):
                    if n == at:
                        turned_hi(k)
                if n == FFN1:
                    act.dma_start(p_in[:, :, :], g["p"].rearrange("a b (t p) d -> p (a b t) d", p=P)).then_inc(p_landed, 16)
                if n == FFN2:
                    act.dma_start(fin_g[:, :], g["final_norm_w_2"].rearrange("(a d) -> a d", a=1)
                                  .to_broadcast([P, D])).then_inc(fin_in, 16)
                if TAIL2 < n and (n - TAIL2) % 2 == 0:
                    square(5, (n - TAIL2) // 2 - 1)
                if n == IN2 + 1:
                    for d, name in enumerate(("gla_gate_w_fwd_2", "gla_gate_w_bwd_2")):
                        act.dma_start(gate_w[:, d, :], g[name].rearrange("a r c -> (a r) c")).then_inc(gate_w_in, 16)
                if n == TAIL1 + 1:
                    act.wait_ge(p_turned, 1)
                    act.activation(p_hi[:, :, :].rearrange("p a n -> p (a n)"), mb[:, 2, :], ACT.Copy).then_inc(phi_ready, 1)

            def split_ahead(n):
                m = n + AHEAD
                if m < TOTAL:
                    per, width = shape_of(m)
                    split_hi(m, m, None, per, width)

            def straight_part(a, z):
                for n in range(a, z):
                    split_ahead(n)
                    beside(n)

            def ffn_part(which, base, base_q):
                groups = NG * which
                norm_no = 1 if which == 0 else 4

                def group(i, first, last):
                    at = base if first else base + 16
                    qq = base_q if first else base_q + 2
                    if last:
                        at += (NG - 1) * GRP - 16
                    gi = 0 if first else 1

                    def split_hidden(n):
                        act.wait_ge(mm_done, n)
                        if which == 0:
                            act.wait_ge(prod_done, NG if last else grown(1, i, 1))
                            src = cv[:, :, :].rearrange("p a n -> p (a n)")
                        else:
                            act.wait_ge(up_turned, groups + NG if last else grown(groups + 1, i, 1))
                            src = mb[:, 0:2, :].rearrange("p a n -> p (a n)")
                        act.activation(h_hi[:, :, :].rearrange("p a n -> p (a n)"), src, ACT.Copy).then_inc(hhi_ready, 1)

                    if last:
                        split_hidden(at + 16)
                    for c in range(16 if last else 0, 16 if first else GRP):
                        n = chunk_of(at + c, i)
                        if last:
                            split_ahead(at + c)
                            beside(at + c)
                            continue
                        split_hi(chunk_of(at + c + AHEAD, i), at + c + AHEAD, i, 2, W)
                        if c == 0 and not first:
                            split_hidden(n)
                        if first:
                            beside(at + c)
                        if c == 7:
                            act.wait_ge(mm_done, n + 1)
                            act.wait_ge(rstd_ready, norm_no + 1)
                            if which == 0:
                                if not first:
                                    act.wait_ge(gate_turned, grown(gi, i, 1))
                            elif not first:
                                act.wait_ge(panel_out[(base_q + 1) % 2], grown((base_q + 1) // 2 + 1, i, 3))
                            par_q = qq
                            for t in range(TB):
                                ins = act.activation(gate_n[:, t, :], panel_in(t, par_q), ACT.Copy if which == 0 else ACT.Silu,
                                                     scale=rstd[norm_no][:, t:t + 1])
                            ins.then_inc(panel_out[par_q % 2], 1)
                        if which == 0 and c == 10:
                            act.wait_ge(gate_turned, grown(gi + 1, i, 1))
                            if not first:
                                act.wait_ge(hlo_ready, grown(gi, i, 1))
                            for ft in range(FT):
                                at_f = ft if first else i * FT + (FT + ft)
                                ins = act.activation(cv[:, ft, :], mb[:, ft // 2, T * (ft % 2):T * (ft % 2) + T],
                                                     ACT.Identity, bias=conv[:, 3, bass.ds(at_f, 1)],
                                                     scale=conv[:, 2, bass.ds(at_f, 1)])
                            ins.then_inc(conv_begun, 1)
                        if which == 0 and c == 13:
                            act.wait_ge(conv_done, grown(gi + 1, i, 1))
                            flat = cv[:, :, :].rearrange("p a n -> p (a n)")
                            act.activation(flat, flat, ACT.Gelu_apprx_tanh).then_inc(gelu_done, 1)
                        if which == 0 and c == 15:
                            act.wait_ge(mm_done, n + 1)
                            if not first:
                                act.wait_ge(up_turned, grown(gi, i, 1))
                            for t in range(TB):
                                ins = act.activation(up_n[:, t, :], panel_in(t, qq + 1), ACT.Copy,
                                                     scale=rstd[norm_no][:, t:t + 1])
                            ins.then_inc(panel_out[(qq + 1) % 2], 1)

                group(None, True, False)
                with act.Fori(0, NG - 1) as i:
                    group(i, False, False)
                group(None, False, True)

            act.dma_start(stage[0:KT, 0, :], g["attn_norm"].rearrange("a (k p) -> (a k) p", p=P)).then_inc(gain_in, 16)
            rows = []
            for j, name in enumerate(("ffn_norm", "ple_norm", "attn_norm_w_2", "ffn_norm_w_2")):
                rows.append((stage[KT * (j + 1):KT * (j + 2), 0, :], g[name]))
            rows.append((stage[V0:V0 + 1, 0, :], g["hgrn_onorm"]))
            for j, name in enumerate(("fox_qnorm", "fox_knorm", "moba_qnorm", "moba_knorm")):
                rows.append((stage[V0 + 1 + j:V0 + 2 + j, 0, :], g[name]))
            rows.append((stage[V0 + 5:V0 + 9, 0, :], g["gla_gate_b_fwd_2"]))
            rows.append((stage[V0 + 9:V0 + 13, 0, :], g["gla_gate_b_bwd_2"]))
            rows.append((stage[V0 + 13:V0 + 21, 0, :], g["gla_norm_w_2"]))
            act.wait_ge(gain_turned, 1)
            act.activation(vecs[:, 0:KT], acc[:, 0, 0:KT], ACT.Copy).then_inc(gain_out, 1)
            act.wait_ge(gain_out, 1)
            for n in range(-4, 0):
                beside(n)
            for n in range(AHEAD):
                split_ahead(n - AHEAD)
            for to, src in rows:
                act.dma_start(to, src.rearrange("a (k p) -> (a k) p", p=P)).then_inc(vec_in, 16)
            taps = g["conv_w"].rearrange("a c (f p) -> (a c f) p", p=P)
            act.dma_start(stage[0:88, 1, :], taps[0:88, :]).then_inc(vec_in, 16)
            act.dma_start(stage[0:44, 2, :], taps[88:132, :]).then_inc(vec_in, 16)
            act.dma_start(stage[44:88, 2, :], g["conv_b"].rearrange("a (f p) -> (a f) p", p=P)).then_inc(vec_in, 16)
            act.dma_start(fbias, g["fox_bf"].to_broadcast([P, HEADS_B])).then_inc(vec_in, 16)
            act.dma_start(causal[:, :], const_f[:, 3 * P:3 * P + 384]).then_inc(vec_in, 16)
            act.dma_start(alibi[:, :], const_f[:, 3 * P + 384:3 * P + 768]).then_inc(vec_in, 16)
            act.dma_start(masks_f, const_m).then_inc(vec_in, 16)
            act.dma_start(hot_sb[:, :], hot).then_inc(vec_in, 16)
            act.wait_ge(table_one, 1)
            act.dma_start(table[0:BUCKETS, :], g["rel_bias_table_2"]).then_inc(vec_in, 16)
            straight_part(IN1, FFN1)
            ffn_part(0, FFN1, FFN1_Q)
            straight_part(PLE, FFN2)
            ffn_part(1, FFN2, FFN2_Q)
            square(5, 3)

        @block.vector
        def _(dve):
            links = [0]

            def link(ins):
                links[0] += 1
                ins.then_inc(dve_link, 1)
                dve.wait_ge(dve_link, links[0])

            def split_lo(n, base, i, per, width):
                dve.wait_ge(hi_ready, n + 1)
                dve.tensor_tensor(cut(w_lo, base % SPL, per, width), cut(raw, base % RAW, per, width),
                                  cut(w_hi, base % SPL, per, width).bitcast(F32), ALU.subtract).then_inc(lo_ready, 1)

            def add_panel(q, col):
                for t in range(TB):
                    to = h[:, t, col:col + W]
                    ins = dve.tensor_tensor(to, panel_in(t, q), to, ALU.add)
                return ins

            def sum_squares(i):
                dve.wait_ge(squares_out, 4 * TB * (i + 1))
                dve.tensor_reduce(rstd[i], sums[:, i % 2, :, :], AX_X, ALU.add).then_inc(squares_summed, 1)

            def turned_lo(k):
                _, i, d = TURN[k]
                for pair in range(2):
                    dve.wait_ge(xhi_ready, 2 * k + pair + 1)
                    for m in (2 * pair, 2 * pair + 1):
                        kt = 4 * d + m
                        ins = dve.scalar_tensor_tensor(x_lo[:, kt, :], mb[:, 2 * (k % 2) + m // 2, T * (m % 2):T * (m % 2) + T],
                                                       NORM[i][:, kt:kt + 1], x_hi[:, kt, :].bitcast(F32),
                                                       ALU.mult, ALU.subtract)
                    ins.then_inc(xlo_ready, 1)
                if k % 4 == 3:
                    sum_squares(i)

            def level_parts(blk, j):
                d, hp, lv = (LEVELS1 if blk == 0 else LEVELS2)[j]
                k = j + 16 * blk
                B = (B1 if blk == 0 else (BF2, BB2)[d])[:, 512 * hp:512 * hp + 512]
                X = (X1 if blk == 0 else X2)[:, k % 2, :]
                return d, hp, lv, k, B, X

            def level_expo(blk, j):
                d, hp, lv, k, B, X = level_parts(blk, j)
                if j >= 2:
                    dve.wait_ge(pair_made, (17 if blk else 0) + j)
                edge = -1 if d == 0 else 0
                if lv < 7:
                    size = LEVELS[lv]
                    r = B.rearrange("p (b s l) -> p b s l", s=2, l=size)
                    x = X.rearrange("p (b s l) -> p b s l", s=2, l=size)
                    e0 = size - 1 if d == 0 else 0
                    ref = r[:, :, d, e0:e0 + 1].to_broadcast([P, 512 // (2 * size), size])
                    dve.tensor_tensor(x[:, :, d, :], ref, r[:, :, d, :], ALU.subtract)
                    if size < 64:
                        ins = dve.tensor_tensor(x[:, :, 1 - d, :], r[:, :, 1 - d, :], ref, ALU.subtract)
                    else:
                        ins = dve.tensor_copy(x[:, :, 1 - d, :], r[:, :, 1 - d, :])
                    ins.then_inc(expo_out, 1)
                    return
                r = B.rearrange("p (h c l) -> p h c l", c=4, l=64)
                x = X.rearrange("p (h c l) -> p h c l", c=4, l=64)
                fk, nk, nq, fq = (0, 1, 2, 3) if d == 0 else (3, 2, 1, 0)
                e0 = 63 if d == 0 else 0
                link(dve.tensor_tensor(full01[:, 0:2], r[:, :, nk, e0], r[:, :, fk, e0], ALU.add))

                def whole(c):
                    return r[:, :, c, e0:e0 + 1].to_broadcast([P, 2, 64])

                dve.tensor_tensor(x[:, :, nk, :], whole(nk), r[:, :, nk, :], ALU.subtract)
                dve.tensor_tensor(x[:, :, fk, :], full01[:, 0:2].unsqueeze(2).to_broadcast([P, 2, 64]), r[:, :, fk, :],
                                  ALU.subtract)
                dve.tensor_copy(x[:, :, nq, :], r[:, :, nq, :])
                dve.tensor_tensor(x[:, :, fq, :], r[:, :, fq, :], whole(nq), ALU.add).then_inc(expo_out, 1)

            def level_mult(blk, j):
                d, hp, lv, k, B, X = level_parts(blk, j)
                size = LEVELS[lv] if lv < 7 else P
                q, kk = (a_reg[:, 0, :], a_reg[:, 1, :]) if blk == 0 else (reg2[:, 0, :], reg2[:, 1, :])
                x = X.rearrange("p (b s l) -> p b s l", s=2, l=size)
                dve.wait_ge(exp_out, k + 1)
                for half, src in ((d, kk), (1 - d, q)):
                    s = src[:, 512 * hp:512 * hp + 512].rearrange("p (b s l) -> p b s l", s=2, l=size)
                    ins = dve.tensor_tensor(x[:, :, half, :], x[:, :, half, :], s[:, :, half, :], ALU.mult)
                ins.then_inc(x_out, 1)

            def level_keep(blk, j):
                d, hp, lv, k, _, _ = level_parts(blk, j)
                A = (AT1 if blk == 0 else AT2)[:, :, :, :].rearrange("p h s (a l) -> p h (s a) l", l=P)
                dve.wait_ge(pair_made, (17 if blk else 0) + 1 + j + 1)
                if lv == 7:
                    dve.tensor_copy(A[:, 2 * hp:2 * hp + 2, 1 + d, :], mb[:, k % 2, 0:256].rearrange("p (h l) -> p h l", h=2))\
                        .then_inc(pair_kept, 1)
                    return
                for e in range(2):
                    ins = dve.copy_predicated(A[:, 2 * hp + e, 0:4:3, :],
                                              masks[:, 1 + 7 * d + lv:2 + 7 * d + lv, :].to_broadcast([P, 2, P]),
                                              mb[:, k % 2, 256 * e:256 * e + 256].rearrange("p (b l) -> p b l", b=2))
                ins.then_inc(pair_kept, 1)

            def diagonal_keep(blk):
                A = (AT1 if blk == 0 else AT2)[:, :, :, :].rearrange("p h s (a l) -> p h (s a) l", l=P)
                dve.wait_ge(pair_made, (17 if blk else 0) + 1)
                dve.wait_ge(at_zero, blk + 1)
                for e in range(4):
                    ins = dve.copy_predicated(A[:, e, 0:4:3, :], masks[:, 0:1, :].to_broadcast([P, 2, P]),
                                              mb[:, 2 + e // 2, 256 * (e % 2):256 * (e % 2) + 256].rearrange("p (b l) -> p b l", b=2))
                ins.then_inc(pair_kept, 1)

            def scan(B, src, back):
                for e in range(4):
                    a, z = B[:, T * e:T * e + T], src[:, T * e:T * e + T]
                    if back:
                        a, z = a[:, ::-1], z[:, ::-1]
                    ins = dve.tensor_tensor_scan(a, scanm[:, :], z, 0.0, ALU.mult, ALU.add)
                ins.then_inc(decay_out, 1)

            def head_steps(n, slots, u0):
                for i, s in enumerate(slots):
                    u = u0 + i
                    second = u >= 12
                    L = (L2 if second else L1)[:, u % 2, :]
                    if n == s + 1:
                        S = mb[:, u % 2, :]
                        dve.wait_ge(scores_made, u + 1)
                        if u >= 2:
                            dve.wait_ge(probs_turned, u - 1)
                        if second:
                            dve.wait_ge(z_in[(u - 12) % ZR], 16 * ((u - 12) // ZR + 1))
                        for t, (c, keys) in enumerate(LOGITS[second]):
                            s_t, l_t = S[:, c:c + keys], L[:, c:c + keys]
                            if u < HEADS_B:
                                ins = dve.scalar_tensor_tensor(l_t, s_t, fcum[:, t, u:u + 1], causal[:, c:c + keys],
                                                               ALU.add, ALU.add)
                            elif u < 12:
                                slope = 2.0 ** (-8.0 * (u - HEADS_B + 1) / HEADS_C)
                                ins = dve.scalar_tensor_tensor(l_t, alibi[:, c:c + keys], slope, s_t, ALU.mult, ALU.add)
                            else:
                                z = Z[:, (u - 12) % ZR, P * t:P * t + T]
                                ins = dve.tensor_tensor(l_t, s_t, z[:, ::-1], ALU.add)
                        link(ins)
                        for t, (c, keys) in enumerate(LOGITS[second]):
                            at = 2 * (u % 2) + t
                            ins = dve.tensor_reduce(negmax[:, at:at + 1], L[:, c:c + keys], AX_X, ALU.max, negate=True)
                        ins.then_inc(logits_out, 1)
                    if n == s + 2:
                        dve.wait_ge(exps_out, u + 1)
                        at = 2 * (u % 2)
                        link(dve.reciprocal(rowinv[:, at:at + 2], rowsum[:, at:at + 2]))
                        for t, (c, keys) in enumerate(LOGITS[second]):
                            ins = dve.tensor_scalar(L[:, c:c + keys], L[:, c:c + keys], rowinv[:, at + t:at + t + 1], None,
                                                    ALU.mult)
                        ins.then_inc(probs_out, 1)

            def beside(n):
                if n == 3:
                    dve.wait_ge(vec_in, 16 * VEC_DMAS)
                    dve.wait_ge(vec_out, 1)
                    dve.tensor_copy(masks[:, :, :].rearrange("p a n -> p (a n)"), masks_f)
                    for j in (0, 2):
                        dve.tensor_scalar(qk_gain[j], qk_gain[j], float(P) ** -0.5, None, ALU.mult)
                if n == 8:
                    wait_panel(dve, 1)
                    link(dve.tensor_tensor(lf, tail[:, :, :], fbias.unsqueeze(1).to_broadcast([P, TB, HEADS_B]), ALU.add))
                    dve.scalar_tensor_tensor(nlf, lf, -1.0, lf, ALU.mult, ALU.min).then_inc(forget_exp, 1)
                if n == 9:
                    dve.wait_ge(log1p_out, 1)
                    link(dve.scalar_tensor_tensor(lf, lf, 0.0, nlf, ALU.min, ALU.subtract))
                    dve.tensor_scalar(nlf, lf, -1.0, None, ALU.mult).then_inc(forget_out, 1)
                if n == HG["turn_f"] + 1:
                    z = mb[:, 2:4, :].rearrange("p a n -> p (a n)")
                    dve.wait_ge(log1p_out, 2)
                    dve.wait_ge(rows_kept, 16)
                    link(dve.scalar_tensor_tensor(LG1[:, :], z, 0.0, X1[:, :, :].rearrange("p a n -> p (a n)"),
                                                  ALU.min, ALU.subtract))
                    dve.tensor_tensor(a_reg[:, 1, :], LG1[:, :], z, ALU.subtract).then_inc(logf_out, 1)
                    dve.wait_ge(logf_out, 1)
                    link(dve.tensor_scalar(LG1[:, :], LG1[:, :], LN_TINY, None, ALU.max))
                    scan(B1, LG1, False)
                if n == HG["turn_f"] + 2:
                    dve.wait_ge(decay_out, 1)
                if n == HG["levels"]:
                    diagonal_keep(0)
                for j in range(len(LEVELS1)):
                    if n == level_slot(0, j):
                        level_expo(0, j)
                    if n == level_slot(0, j) + 1:
                        level_mult(0, j)
                    if n == level_slot(0, j) + 3:
                        level_keep(0, j)
                if n == HG["make_o"] + 2:
                    X = X1[:, :, :].rearrange("p a n -> p (a n)")
                    dve.wait_ge(o_out, 1)
                    link(dve.tensor_tensor(X, LG1[:, :], LG1[:, :], ALU.mult))
                    dve.tensor_reduce(hsq, X.rearrange("p (g l) -> p g l", l=P), AX_X, ALU.add).then_inc(osq_out, 1)
                if n == HG["make_o"] + 3:
                    dve.wait_ge(orstd, 1)
                    o = LG1[:, :].rearrange("p (g l) -> p g l", l=P)
                    link(dve.tensor_tensor(o, o, hrs.unsqueeze(2).to_broadcast([P, 8, P]), ALU.mult))
                    dve.wait_ge(og_out, 1)
                    dve.tensor_tensor(LG1[:, :], LG1[:, :], a_reg[:, 3, :], ALU.mult).then_inc(o_scaled, 1)
                for j, (panel, s) in enumerate(PREP1.items()):
                    r = bc_reg[:, panel - 5, :]
                    if n == s:
                        dve.wait_ge(panel_out[panel % 2], panel // 2 + 1)
                        if j == 0:
                            dve.wait_ge(o_turned, 1)
                        link(dve.tensor_tensor(LG1[:, 0:768], r, r, ALU.mult))
                        dve.tensor_reduce(hsq[:, 0:6], LG1[:, 0:768].rearrange("p (g l) -> p g l", l=P), AX_X, ALU.add)\
                            .then_inc(prep_sq, 1)
                    if n == s + 1:
                        dve.wait_ge(prep_rstd, j + 1)
                        v = r.rearrange("p (g l) -> p g l", l=P)
                        dve.tensor_tensor(v, v, hrs[:, 0:6].unsqueeze(2).to_broadcast([P, 6, P]), ALU.mult)\
                            .then_inc(prep_scaled, 1)
                head_steps(n, HEAD1, 0)

                if n in (IN2 + 14, IN2 + 16):
                    d = (n - IN2 - 14) // 2
                    B = (BF2, BB2)[d]
                    X = X2[:, :, :].rearrange("p a n -> p (a n)")
                    dve.wait_ge(log1p_out, 3 + d)
                    link(dve.scalar_tensor_tensor(X, B[:, :], 0.0, X, ALU.min, ALU.subtract))
                    link(dve.tensor_scalar(X, X, 1.0 / 16.0, None, ALU.mult))
                    scan(B, X, d == 1)
                if n == IN2 + 19:
                    dve.wait_ge(decay_out, 3)
                    diagonal_keep(1)
                for j in range(len(LEVELS2)):
                    if n == level_slot(1, j):
                        level_expo(1, j)
                    if n == level_slot(1, j) + 1:
                        level_mult(1, j)
                    if n == level_slot(1, j) + 3:
                        level_keep(1, j)
                ob = reg2[:, 0:2, :]
                if n == IN2 + 72:
                    dve.wait_ge(o_out, 2)
                    X = X2[:, :, :].rearrange("p a n -> p (a n)")
                    for t in range(TB):
                        link(dve.tensor_tensor(X, ob[:, t, :], ob[:, t, :], ALU.mult))
                        ins = dve.tensor_reduce(hsq[:, 4 * t:4 * t + 4], X.rearrange("p (g l) -> p g l", l=T), AX_X, ALU.add)
                        if t == 0:
                            link(ins)
                    ins.then_inc(osq_out, 1)
                if n == IN2 + 73:
                    dve.wait_ge(orstd, 2)
                    o = ob.rearrange("p a n -> p (a n)").rearrange("p (g l) -> p g l", l=T)
                    link(dve.tensor_tensor(o, o, hrs.unsqueeze(2).to_broadcast([P, 8, T]), ALU.mult))
                    dve.wait_ge(og_out, 2)
                    for c in range(2):
                        part = ob[:, :, W * c:W * c + W]
                        ins = dve.tensor_tensor(part, part, reg2[:, 4 + c, :].rearrange("p (t n) -> p t n", t=TB), ALU.mult)
                    ins.then_inc(o_scaled, 1)
                head_steps(n, HEAD2, 12)
                if n in OSPLIT:
                    blk = n >= IN2
                    for pair in OSPLIT[n]:
                        dve.wait_ge(ohi_ready, OSPLIT_ORDER.index(pair, 8 * blk) + 1)
                        for kt in (2 * pair, 2 * pair + 1):
                            ins = dve.tensor_tensor(x_lo[:, kt, :], o_turned_at(kt, int(blk)), x_hi[:, kt, :].bitcast(F32),
                                                    ALU.subtract)
                        ins.then_inc(olo_ready, 1)
                if n in ends and (OUT1 <= n < OUT1_END or OUT2 <= n < OUT2_END):
                    q = ends[n]
                    dve.wait_ge(mm_done, n + 1)
                    first_q = OUT1_Q if n < OUT1_END else OUT2_Q
                    add_panel(q, (q - first_q) % 4 * W).then_inc(panel_out[q % 2], 1)
                if PLE <= n < PLE_END and n in ends and (ends[n] - PLE_Q) % 2 == 1:
                    q = ends[n]
                    j = (q - PLE_Q) // 2
                    dve.wait_ge(panel_out[q % 2], q // 2 + 1)
                    dve.wait_ge(panel_out[(q - 1) % 2], (q - 1) // 2 + 1)
                    link(dve.tensor_tensor(gate_n[:, :, :], gate_n[:, :, :], pn[:, :, :], ALU.mult))
                    to = h[:, :, W * j:W * j + W]
                    ins = dve.tensor_tensor(to, to, gate_n[:, :, :], ALU.add)
                    ins.then_inc(ple_added, 1)
                for k, (at, _, _) in enumerate(TURN):
                    if n == at:
                        turned_lo(k)
                if n == TAIL1 + 1:
                    dve.wait_ge(phi_ready, 1)
                    dve.tensor_tensor(p_lo[:, :, :].rearrange("p a n -> p (a n)"), mb[:, 2, :],
                                      p_hi[:, :, :].rearrange("p a n -> p (a n)").bitcast(F32), ALU.subtract)\
                        .then_inc(plo_ready, 1)

            def split_ahead(n):
                m = n + AHEAD
                if m < TOTAL:
                    per, width = shape_of(m)
                    split_lo(m, m, None, per, width)

            def straight_part(a, z):
                for n in range(a, z):
                    split_ahead(n)
                    beside(n)

            def ffn_part(which, base, base_q):
                groups = NG * which

                def group(i, first, last):
                    at = base if first else base + 16
                    qq = base_q if first else base_q + 2
                    if last:
                        at += (NG - 1) * GRP - 16
                        qq += 6 * (NG - 1) - 2
                    gi = 0 if first else 1

                    def split_hidden():
                        dve.wait_ge(hhi_ready, groups + NG if last else grown(groups + 1, i, 1))
                        src = (cv[:, :, :] if which == 0 else mb[:, 0:2, :]).rearrange("p a n -> p (a n)")
                        dve.tensor_tensor(h_lo[:, :, :].rearrange("p a n -> p (a n)"), src,
                                          h_hi[:, :, :].rearrange("p a n -> p (a n)").bitcast(F32), ALU.subtract)\
                            .then_inc(hlo_ready, 1)

                    if last:
                        split_hidden()
                    for c in range(16 if last else 0, 16 if first else GRP):
                        n = chunk_of(at + c, i)
                        if last:
                            split_ahead(at + c)
                        else:
                            split_lo(chunk_of(at + c + AHEAD, i), at + c + AHEAD, i, 2, W)
                        if c == 0 and not first and not last:
                            split_hidden()
                        if which == 0 and c == 11:
                            dve.wait_ge(conv_begun, grown(gi + 1, i, 1))
                            for back in (1, 2):
                                for ft in range(FT):
                                    at_f = ft if first else i * FT + (FT + ft)
                                    ins = dve.scalar_tensor_tensor(
                                        cv[:, ft, back:T], mb[:, ft // 2, T * (ft % 2):T * (ft % 2) + T - back],
                                        conv[:, 2 - back, bass.ds(at_f, 1)], cv[:, ft, back:T], ALU.mult, ALU.add)
                                if back == 1:
                                    ins.then_inc(conv_first, 1)
                                    dve.wait_ge(conv_first, grown(gi + 1, i, 1))
                            ins.then_inc(conv_done, 1)
                        if which == 1 and c == 15:
                            dve.wait_ge(mm_done, n + 1)
                            dve.wait_ge(panel_out[qq % 2], grown(qq // 2 + 1, i, 3))
                            if not first:
                                dve.wait_ge(up_turned, grown(groups + gi, i, 1))
                            for t in range(TB):
                                ins = dve.scalar_tensor_tensor(up_n[:, t, :], panel_in(t, qq + 1), rstd[4][:, t:t + 1],
                                                               gate_n[:, t, :], ALU.mult, ALU.mult)
                            ins.then_inc(panel_out[(qq + 1) % 2], 1)
                        if which == 0 and (c == 18 and not last or c == 15 and first):
                            dve.wait_ge(up_turned, grown(gi + 1, i, 1))
                            dve.wait_ge(gelu_done, grown(gi + 1, i, 1))
                            flat = cv[:, :, :].rearrange("p a n -> p (a n)")
                            dve.tensor_tensor(flat, flat, mb[:, 2:4, :].rearrange("p a n -> p (a n)"), ALU.mult)\
                                .then_inc(prod_done, 1)
                        if c >= 17 and c % 2 == 1:
                            part = (c - 17) // 2
                            dve.wait_ge(mm_done, n + 1)
                            add_panel(qq + 2 + part, part * W).then_inc(panel_out[(qq + part) % 2], 1)
                        if first or last:
                            beside(at + c)

                group(None, True, False)
                with dve.Fori(0, NG - 1) as i:
                    group(i, False, False)
                group(None, False, True)

            dve.wait_ge(gain_out, 1)
            for n in range(-4, 0):
                beside(n)
            for n in range(AHEAD):
                split_ahead(n - AHEAD)
            straight_part(IN1, FFN1)
            ffn_part(0, FFN1, FFN1_Q)
            straight_part(PLE, FFN2)
            ffn_part(1, FFN2, FFN2_Q)
            sum_squares(5)
            dve.wait_ge(fin_in, 16)
            dve.wait_ge(rstd_ready, 6)
            for t in range(TB):
                dve.scalar_tensor_tensor(result[:, t, :], h[:, t, :], rstd[5][:, t:t + 1], fin_g[:, :], ALU.mult,
                                         ALU.mult).then_inc(fin_done, 1)


NAMES = ["x", "p", "attn_norm", "w_in", "fox_bf", "lb_logits", "hgrn_onorm", "fox_qnorm", "fox_knorm",
         "moba_qnorm", "moba_knorm", "w_out", "ffn_norm", "w_gate", "w_up", "conv_w", "conv_b", "w_down",
         "ple_norm", "w_ple_gate", "w_ple_proj", "attn_norm_w_2", "w_in_2", "rel_bias_table_2",
         "gla_gate_w_fwd_2", "gla_gate_b_fwd_2", "gla_gate_w_bwd_2", "gla_gate_b_bwd_2", "gla_norm_w_2",
         "w_out_2", "ffn_norm_w_2", "w_gate_2", "w_up_2", "w_down_2", "final_norm_w_2"]


def kernel(**inputs):
    import concourse.bacc as bacc
    from concourse.bass_utils import run_bass_kernel_spmd

    nc = bacc.Bacc("TRN2", target_bir_lowering=False, num_devices=1)
    arrays, aps = {}, {}

    def give(name, a):
        arrays[name] = a
        return nc.dram_tensor(name, a.shape, mybir.dt.from_np(a.dtype), kind="ExternalInput").ap()

    for name in NAMES:
        aps[name] = give(f"in_{name}", np.ascontiguousarray(inputs[name]))
    cf, masks, hot = shape_constants()
    consts = [give("const_f", cf), give("const_m", masks), give("const_hot", hot)]
    out = nc.dram_tensor("out", (1, T, D), F32, kind="ExternalOutput").ap()
    build(nc, aps, out, *consts)
    r = run_bass_kernel_spmd(nc, [arrays], core_ids=[0])
    return r.results[0]["out"]
```

```python
from contextlib import ExitStack
from math import log

import numpy as np

import concourse.bass as bass
from concourse import mybir

ALU = mybir.AluOpType
ACT = mybir.ActivationFunctionType
F32 = mybir.dt.float32
F32R = mybir.dt.float32r
I8 = mybir.dt.int8
AX_X = mybir.AxisListType.X

P = 128
T = 256
TB = T // P
D = 2048
KT = D // P
FF = 5632
W = 512
NG = FF // W
FT = W // P
EPS = 1e-6
NEG = -1e30
FAR = -1e34
LN_TINY = log(1e-30)
RAW = 4
SPL = 6
AHEAD = 5
HEADS_B = HEADS_C = 6
HEADS_2 = 16
LEVELS = (1, 2, 4, 8, 16, 32, 64)
GRP = 24
BUCKETS = 32
GRW = (1024 + 32) // 3
ZR = 4
ND = 2 * T - 1


def shape_constants():
    i, j = np.arange(P)[:, None], np.arange(P)[None, :]
    cf = np.zeros((P, 3 * P + 768), np.float32)
    cf[:, 0:P] = i == j
    cf[:, P:2 * P] = i <= j
    cf[:, 2 * P:3 * P] = 1.0
    q = np.arange(P)[:, None]
    k0, k1 = np.arange(P)[None, :], np.arange(T)[None, :]
    dist = np.concatenate([k0 - q, k1 - q - P], axis=1)
    cf[:, 3 * P:3 * P + 384] = np.where(dist <= 0, 0.0, NEG)
    cf[:, 3 * P + 384:3 * P + 768] = np.where(dist <= 0, dist, FAR)
    masks = np.zeros((P, 15, P), np.float32)
    masks[:, 0] = i == j
    for n, size in enumerate(LEVELS):
        pair = (i // (2 * size) == j // (2 * size)) & (i // size % 2 == 0) & (j // size % 2 == 1)
        masks[:, 1 + n] = pair
        masks[:, 8 + n] = pair | pair.T
    rel = T - 1 - np.arange(ND)
    nb = BUCKETS // 2
    n = np.abs(rel)
    exact = nb // 2
    large = exact + (np.log(np.maximum(n, 1) / exact) / log(1024 / exact) * (nb - exact)).astype(np.int64)
    bucket = np.where(rel > 0, nb, 0) + np.where(n < exact, n, np.minimum(large, nb - 1))
    times = (n <= 64) * 1 + (rel % 4 == 0) * 1 + (rel % 16 == 0) * 1
    hot = np.zeros((BUCKETS + 1, 512), np.float32)
    hot[bucket, np.arange(ND)] = 1.0
    hot[BUCKETS, :ND] = np.where(times > 0, np.log(np.maximum(times, 1)), NEG)
    return cf, masks.reshape(P, 15 * P), hot


class Panel:

    def __init__(self, weight, col, width, kts, per=2, row0=0, source="x"):
        self.weight, self.col, self.width, self.kts, self.per = weight, col, width, kts, per
        self.row0, self.source = row0, source
        self.chunks = len(kts) // per


def plan():
    full = list(range(KT))
    a0 = 0
    b0 = 4 * W
    c0 = b0 + 3 * HEADS_B * P + HEADS_B
    first = [Panel("w_in", a0 + W * j, W, full) for j in range(4)]
    for base, halves in ((b0, (1, 0)), (c0, (0, 1))):
        first += [Panel("w_in", base + HEADS_B * P * m + 384 * half,
                        384 + (HEADS_B if (base, half, m) == (b0, 1, 2) else 0), full)
                  for half in halves for m in range(3)]
    out1 = [Panel("w_out", W * j, W, full[:12]) for j in range(4)]
    out1 += [Panel("w_out", W * j, W, full[12:]) for j in range(4)]
    ple = []
    for j in range(4):
        ple += [Panel("w_ple_proj", W * j, W, [0, 1], source="p"), Panel("w_ple_gate", W * j, W, full)]
    second = [Panel("w_in_2", c, width, full) for c, width in
              ((3072, W), (5120 + 2 * GRW, GRW), (3584, W), (4096, W), (4608, W), (5120, GRW), (5120 + GRW, GRW),
               (0, W), (1024, W), (2048, W), (512, W), (1536, W), (2560, W))]
    out2 = [Panel("w_out_2", W * j, W, full[8:] + full[:4]) for j in range(4)]
    out2 += [Panel("w_out_2", W * j, W, full[4:8]) for j in range(4)]
    return first, out1, ple, second, out2


def build(nc, g, out, const_f, const_m, hot):
    first, out1, ple, second, out2 = plan()
    straight = {}
    ends = {}
    n = q = 0

    def lay(panels):
        nonlocal n, q
        begin = n
        for p in panels:
            for j in range(p.chunks):
                straight[n] = (p, q, j)
                n += 1
            ends[n - 1] = q
            q += 1
        return begin, n

    IN1, IN1_END = lay(first)
    OUT1, OUT1_END = lay(out1)
    FFN1, FFN1_Q = n, q
    n += GRP * NG
    q += 6 * NG
    PLE, PLE_END = lay(ple)
    PLE_Q = straight[PLE][1]
    IN2, IN2_END = lay(second)
    IN2_Q = straight[IN2][1]
    OUT2, OUT2_END = lay(out2)
    OUT1_Q, OUT2_Q = straight[OUT1][1], straight[OUT2][1]
    FFN2, FFN2_Q = n, q
    n += GRP * NG
    TOTAL = n

    x_d = g["x"].rearrange("b (t p) d -> p (b t) d", p=P)
    out_d = out.rearrange("b (t p) d -> p (b t) d", p=P)
    wd = {k: (g[k].rearrange("a r c -> (a r) c")) for k in (
        "w_in", "w_out", "w_gate", "w_up", "w_down", "w_ple_gate", "w_ple_proj", "w_in_2", "w_out_2",
        "w_gate_2", "w_up_2", "w_down_2")}
    VEC_DMAS = 21
    bias_rows = nc.dram_tensor("bias_rows", [HEADS_2, 512], F32, kind="Internal").ap()

    with ExitStack() as ctx:
        def sb(name, shape, dt=F32, stack=ctx):
            return stack.enter_context(nc.sbuf_tensor(name, shape, dt))

        def sem(name):
            return ctx.enter_context(nc.semaphore(name))

        acc = ctx.enter_context(nc.psum_tensor("acc", [P, 4, 512], F32))
        mb = ctx.enter_context(nc.psum_tensor("mb", [P, 4, 512], F32))

        raw = sb("raw", [P, RAW, 2 * W])
        w_hi = sb("w_hi", [P, SPL, 2 * W], F32R)
        w_lo = sb("w_lo", [P, SPL, 2 * W], F32R)
        x_hi = sb("x_hi", [P, KT, T], F32R)
        x_lo = sb("x_lo", [P, KT, T], F32R)
        h = sb("h", [P, TB, D])
        cf = sb("cf", [P, 3 * P])
        ident, upto, ones = cf[:, 0:P], cf[:, P:2 * P], cf[:, 2 * P:3 * P]
        masks = sb("masks", [P, 15, P], I8)
        NV = 5 * KT + 1 + 4 + 8 + 8
        vecs = sb("vecs", [P, NV])
        NORM = [vecs[:, KT * j:KT * (j + 1)] for j in range(5)]
        V0 = 5 * KT
        hgrn_gain = vecs[:, V0:V0 + 1]
        qk_gain = [vecs[:, V0 + 1 + j:V0 + 2 + j] for j in range(4)]
        gate_bias = [vecs[:, V0 + 5 + 4 * d:V0 + 9 + 4 * d] for d in range(2)]
        gla_gain = vecs[:, V0 + 13:V0 + 21]
        conv = sb("conv", [P, 4, 44])
        small = sb("small", [P, 128])
        minus_half = small[:, 0:1]
        sums = small[:, 88:104].rearrange("p (m t d) -> p m t d", m=2, t=TB)
        rstd = [small[:, 104 + 2 * i:106 + 2 * i] for i in range(6)]
        hsq, hrs = small[:, 8:16], small[:, 16:24]
        full01 = small[:, 24:32]
        negmax, rowsum, rowinv = small[:, 32:36], small[:, 36:40], small[:, 40:44]
        fbias = small[:, 44:50]
        lf = small[:, 52:64].rearrange("p (t h) -> p t h", t=2)
        nlf = small[:, 64:76].rearrange("p (t h) -> p t h", t=2)
        fcum = small[:, 76:88].rearrange("p (t h) -> p t h", t=2)
        scanm = sb("scanm", [P, T])
        junk = sb("junk", [P, W])

        with ExitStack() as s1:
            tail = sb("tail", [P, TB, HEADS_B], F32, s1)
            a_reg = sb("a_reg", [P, 4, 1024], F32, s1)
            bc_reg = sb("bc_reg", [P, 12, 768], F32, s1)
            AT1 = sb("AT1", [P, 4, TB, T], F32, s1)
            X1 = sb("X1", [P, 2, 512], F32, s1)
            LG1 = sb("LG1", [P, 1024], F32, s1)
            B1 = sb("B1", [P, 1024], F32, s1)
            L1 = sb("L1", [P, 2, 512], F32, s1)
            WT1 = sb("WT1", [P, 2, 512], F32, s1)
            causal = sb("causal", [P, 384], F32, s1)
            alibi = sb("alibi", [P, 384], F32, s1)
            stage = sb("stage", [P, 3, P], F32, s1)
            table = sb("table", [BUCKETS + 1, HEADS_2], F32, s1)
            hot_sb = sb("hot_sb", [BUCKETS + 1, 512], F32, s1)
        rows_sb = LG1[0:HEADS_2, 0:512]
        masks_f = bc_reg[:, 0:3, :].rearrange("p a n -> p (a n)")[:, 0:15 * P]
        with ExitStack() as s2:
            h_hi = sb("h_hi", [P, FT, T], F32R, s2)
            h_lo = sb("h_lo", [P, FT, T], F32R, s2)
            gate_n = sb("gate_n", [P, TB, W], F32, s2)
            up_n = sb("up_n", [P, TB, W], F32, s2)
            cv = sb("cv", [P, FT, T], F32, s2)
            pn = sb("pn", [P, TB, W], F32, s2)
            p_in = sb("p_in", [P, TB, 256], F32, s2)
            p_hi = sb("p_hi", [P, 2, T], F32R, s2)
            p_lo = sb("p_lo", [P, 2, T], F32R, s2)
            fin_g = sb("fin_g", [P, D], F32, s2)
            result = sb("result", [P, TB, D], F32, s2)
        with ExitStack() as s3:
            tail2 = sb("tail2", [P, TB, 32], F32, s3)
            reg2 = sb("reg2", [P, 12, 1024], F32, s3)
            Z = sb("Z", [P, ZR, 384], F32, s3)
            AT2 = sb("AT2", [P, 4, TB, T], F32, s3)
            X2 = sb("X2", [P, 2, 2, 512], F32, s3)
            BF2 = sb("BF2", [P, 1024], F32, s3)
            BB2 = sb("BB2", [P, 1024], F32, s3)
            L2 = sb("L2", [P, 2, 512], F32, s3)
            WT2 = sb("WT2", [P, 2, 512], F32, s3)
            gr = reg2[:, 4:6, :].rearrange("p r n -> p (r n)").rearrange("p (t n) -> p t n", t=TB)
            lr_t = L2[0:16, :, 0:T]
            gate_w = WT2[0:16, :, :]
            gate_abs = [B[:, :, :].rearrange("p a n -> p (a n)") for B in (X2[:, 0, :, :], WT2)]

        raw_in = [sem(f"raw_in{s}") for s in range(RAW)]
        hi_ready = sem("hi_ready")
        lo_ready = sem("lo_ready")
        mm_done = sem("mm_done")
        panel_out = [sem("panel_out_even"), sem("panel_out_odd")]
        x_in = [sem(f"x_in{d}") for d in range(4)]
        const_in, gain_in, vec_in = sem("const_in"), sem("gain_in"), sem("vec_in")
        gain_turned, gain_out = sem("gain_turned"), sem("gain_out")
        junk_set, pool_set, table_one = sem("junk_set"), sem("pool_set"), sem("table_one")
        vec_turned, vec_out, rows_made, rows_out, rows_kept = (
            sem("vec_turned"), sem("vec_out"), sem("rows_made"), sem("rows_out"), sem("rows_kept"))
        squares_out, squares_summed, rstd_ready = sem("squares_out"), sem("squares_summed"), sem("rstd_ready")
        h_turned, xhi_ready, xlo_ready = sem("h_turned"), sem("xhi_ready"), sem("xlo_ready")
        gate_turned, conv_begun, conv_first, conv_done = (
            sem("gate_turned"), sem("conv_begun"), sem("conv_first"), sem("conv_done"))
        gelu_done, up_turned, prod_done = sem("gelu_done"), sem("up_turned"), sem("prod_done")
        hhi_ready, hlo_ready = sem("hhi_ready"), sem("hlo_ready")
        p_landed, p_turned, phi_ready, plo_ready = (
            sem("p_landed"), sem("p_turned"), sem("phi_ready"), sem("plo_ready"))
        ple_added = sem("ple_added")
        dq_turned, dq_out, dk_turned, dk_out = sem("dq_turned"), sem("dq_out"), sem("dk_turned"), sem("dk_out")
        neg_abs, log1p_out, logf_out, decay_out = sem("neg_abs"), sem("log1p_out"), sem("logf_out"), sem("decay_out")
        gates_out, exp_abs = sem("gates_out"), sem("exp_abs")
        lr_turned, lr_out, gates_made, gate_w_in = sem("lr_turned"), sem("lr_out"), sem("gates_made"), sem("gate_w_in")
        expo_out, exp_out, x_out, pair_made, pair_kept = (
            sem("expo_out"), sem("exp_out"), sem("x_out"), sem("pair_made"), sem("pair_kept"))
        at_zero, o_made, o_out, og_out, osq_out, orstd, o_scaled, o_turned, o_kept = (
            sem("at_zero"), sem("o_made"), sem("o_out"), sem("og_out"), sem("osq_out"), sem("orstd"),
            sem("o_scaled"), sem("o_turned"), sem("o_kept"))
        forget_exp, forget_out, fcum_made, fcum_out = (
            sem("forget_exp"), sem("forget_out"), sem("fcum_made"), sem("fcum_out"))
        prep_squared, prep_sq, prep_rstd, prep_scaled, prep_turned, prep_out = (
            sem("prep_squared"), sem("prep_sq"), sem("prep_rstd"), sem("prep_scaled"), sem("prep_turned"), sem("prep_out"))
        scores_made, logits_out, exps_out, probs_out, probs_turned, probs_kept, head_made, head_out = (
            sem("scores_made"), sem("logits_out"), sem("exps_out"), sem("probs_out"),
            sem("probs_turned"), sem("probs_kept"), sem("head_made"), sem("head_out"))
        z_in = [sem(f"z_in{r}") for r in range(ZR)]
        ohi_ready, olo_ready = sem("ohi_ready"), sem("olo_ready")
        fin_in, fin_done, out_stored = sem("fin_in"), sem("fin_done"), sem("out_stored")
        fin_gained, fin_done_act = sem("fin_gained"), sem("fin_done_act")
        act_link, dve_link, pool_link = sem("act_link"), sem("dve_link"), sem("pool_link")

        HG = dict(turn_q=9, turn_f=17, levels=23, forget=55, make_o=57)
        PREP1 = {4: 60, 5: 62, 7: 64, 8: 72, 10: 88, 11: 96, 13: 112, 14: 120}
        HEAD1 = [69, 72, 77, 80, 83, 86, 101, 104, 107, 125, 128, 131]
        b = IN2
        PREP2 = {7: b + 80, 8: b + 81, 10: b + 103, 11: b + 104}
        HEAD2 = [b + 83 + 2 * i for i in range(8)] + [b + 106 + 2 * i for i in range(8)]
        OSPLIT = {IN1_END - 8 + s: [s] for s in range(6)} | {OUT1 + 22: [6, 7]}
        OSPLIT |= {IN2_END - 4 + s: [4 + s] for s in range(4)} | {OUT2 + 1: [0, 1], OUT2 + 22: [2, 3]}
        OSPLIT_ORDER = [s for n in sorted(OSPLIT) for s in OSPLIT[n]]
        TAIL1, TAIL2 = FFN1 + 16 + (NG - 1) * GRP, FFN2 + 16 + (NG - 1) * GRP
        TURN = [(-2, 0, 0), (-1, 0, 1), (0, 0, 2), (2, 0, 3)]
        TURN += [(OUT1 + 26, 1, 0), (OUT1 + 28, 1, 1), (OUT1 + 30, 1, 2), (FFN1, 1, 3)]
        TURN += [(TAIL1 + 2, 2, 0), (TAIL1 + 4, 2, 1), (TAIL1 + 6, 2, 2), (PLE, 2, 3)]
        TURN += [(PLE_END - 7 + 2 * d, 3, d) for d in range(3)] + [(IN2, 3, 3)]
        TURN += [(OUT2 + 26, 4, 0), (OUT2 + 30, 4, 2), (FFN2, 4, 1), (FFN2 + 1, 4, 3)]
        LEVELS1 = [(hp, lv) for hp in range(2) for lv in range(8)]
        LEVELS2 = [(hp, lv) for hp in range(2) for lv in range(8)]

        VEC = 11

        def level_slot(block, j):
            return HG["levels"] + 2 * j if block == 0 else IN2 + 26 + 11 * j // 4

        def split_slot(k):
            at = TURN[k][0]
            return at + (at > 3 and at not in (FFN1, PLE, IN2, FFN2, FFN2 + 1))

        def chunk_of(value, i):
            return value if i is None else i * GRP + value

        def grown(value, i, step):
            return value if i is None else i * step + value

        def wait_panel(eng, q):
            eng.wait_ge(panel_out[q % 2], q // 2 + 1)

        def wait_h(eng, i, d):
            if i == 0:
                eng.wait_ge(x_in[d], 16)
            elif i == 3:
                eng.wait_ge(ple_added, d + 1)
            else:
                wait_panel(eng, {1: OUT1_Q + 4, 2: FFN1_Q + 6 * NG - 4, 4: OUT2_Q + 4, 5: FFN2_Q + 6 * NG - 4}[i] + d)

        def turned_before(i, pair):
            at = [(j, d) for _, j, d in TURN].index((i, pair // 2))
            return 2 * at + pair % 2 + 1

        def norm_of(q):
            return 0 if q < OUT1_Q else 1 if q < PLE_Q else 2 if q < IN2_Q else 3 if q < OUT2_Q else 4

        def cut(buf, slot, per, width):
            return buf[:, slot, 0:per * width].rearrange("p (k n) -> p k n", k=per)

        def shape_of(n):
            if n in straight:
                return straight[n][0].per, straight[n][0].width
            return 2, W

        def panel_in(t, q):
            return acc[:, 2 * (q % 2) + t, :]

        def region(q):
            j = q if q < IN2_Q else q - IN2_Q
            if q < IN2_Q:
                r = a_reg[:, j, :] if j < 4 else bc_reg[:, j - 4, :]
            else:
                r = reg2[:, max(j - 1, 0), :]
            wide = 384 if q < IN2_Q and j >= 4 else W
            return r.rearrange("p (t n) -> p t n", t=TB), r.rearrange("p (k t) -> p k t", t=T), wide // P

        def o_turned_at(kt, block):
            if block == 0:
                if kt < 4:
                    return a_reg[:, 3, T * kt:T * kt + T]
                hh = kt - 4
                base = 3 * (1 - hh // 3) if hh < HEADS_B else 3 * (hh // 3)
                return bc_reg[:, base, T * (hh % 3):T * (hh % 3) + T]
            if kt >= 8:
                return reg2[:, 4 + (kt - 8) // 4, T * (kt % 4):T * (kt % 4) + T]
            return reg2[:, 6 + 3 * (kt // 4), T * (kt % 4):T * (kt % 4) + T]

        def head(u):
            if u < 12:
                base, s = 6 * (u // 6) + 3 * (u % 6 // 3), T * (u % 3)
                v = bc_reg[:, base + 2, :].rearrange("p (t n) -> p t n", t=TB)[:, :, P * (u % 3):P * (u % 3) + P]
                return bc_reg[:, base, s:s + T], bc_reg[:, base + 1, s:s + T], v, bc_reg[:, base, s:s + T], P
            e = u - 12
            base, s, lo = 6 + 3 * (e // 8), T * (e % 8 // 2), 64 * (e % 2)
            v = reg2[:, base + 2, :].rearrange("p (t n) -> p t n", t=TB)[:, :, 64 * (e % 8):64 * (e % 8) + 64]
            q = reg2[lo:lo + 64, base, s:s + T]
            return q, reg2[lo:lo + 64, base + 1, s:s + T], v, q, 64

        LOGITS = [((0, 128), (128, 256)), ((0, 256), (256, 256))]

        block = ctx.enter_context(nc.Block())

        @block.sync
        def _(sp):
            sp.dma_start(cf[:, :], const_f[:, 0:3 * P]).then_inc(const_in, 16)

            def load_x(d):
                sp.dma_start(h[:, :, W * d:W * d + W], x_d[:, :, W * d:W * d + W]).then_inc(x_in[d], 16)

            def load(n, base, i, src, per, width):
                if i is not None or base >= RAW:
                    sp.wait_ge(lo_ready, n - (RAW - 1))
                sp.dma_start(cut(raw, base % RAW, per, width),
                             src.rearrange("(k p) n -> p k n", p=P)).then_inc(raw_in[base % RAW], 16)

            def small_inputs():
                rows = []
                for j, name in enumerate(("ffn_norm", "ple_norm", "attn_norm_w_2", "ffn_norm_w_2")):
                    rows.append((stage[KT * (j + 1):KT * (j + 2), 0, :], g[name]))
                rows.append((stage[V0:V0 + 1, 0, :], g["hgrn_onorm"]))
                for j, name in enumerate(("fox_qnorm", "fox_knorm", "moba_qnorm", "moba_knorm")):
                    rows.append((stage[V0 + 1 + j:V0 + 2 + j, 0, :], g[name]))
                rows.append((stage[V0 + 5:V0 + 9, 0, :], g["gla_gate_b_fwd_2"]))
                rows.append((stage[V0 + 9:V0 + 13, 0, :], g["gla_gate_b_bwd_2"]))
                rows.append((stage[V0 + 13:V0 + 21, 0, :], g["gla_norm_w_2"]))
                rows = [(to, src.rearrange("a (k p) -> (a k) p", p=P)) for to, src in rows]
                taps = g["conv_w"].rearrange("a c (f p) -> (a c f) p", p=P)
                rows.append((stage[0:88, 1, :], taps[0:88, :]))
                rows.append((stage[0:44, 2, :], taps[88:132, :]))
                rows.append((stage[44:88, 2, :], g["conv_b"].rearrange("a (f p) -> (a f) p", p=P)))
                rows.append((fbias, g["fox_bf"].to_broadcast([P, HEADS_B])))
                rows.append((causal[:, :], const_f[:, 3 * P:3 * P + 384]))
                rows.append((alibi[:, :], const_f[:, 3 * P + 384:3 * P + 768]))
                rows.append((masks_f, const_m))
                rows.append((hot_sb[:, :], hot))
                rows.append((table[0:BUCKETS, :], g["rel_bias_table_2"]))
                return rows

            def load_straight(a, z):
                for n in range(a, z):
                    p, _, j = straight[n]
                    rows = p.kts[j * p.per] * P
                    load(n, n, None, wd[p.weight][rows:rows + p.per * P, p.col:p.col + p.width], p.per, p.width)

            def load_ffn(base, gate, up, down):
                def group(i, first, last):
                    at = base + (16 if not first else 0)
                    col = 0 if i is None else i * W + W
                    prev = (NG - 1) * W if last else (i * W if i is not None else None)
                    for c in range(16 if first else GRP):
                        if last and c < 16:
                            continue
                        cc = c
                        b0 = at + c
                        if last:
                            b0 = base + 16 + (NG - 1) * GRP + c - 16
                        n = chunk_of(b0, i)
                        if c < 16:
                            wsrc = wd[gate if c < 8 else up]
                            src = wsrc[(cc % 8) * 2 * P:(cc % 8 + 1) * 2 * P, bass.ds(col, W)]
                        else:
                            row = prev + (c % 2) * 2 * P
                            src = wd[down][bass.ds(row, 2 * P), (c - 16) // 2 * W:((c - 16) // 2 + 1) * W]
                        load(n, b0, i, src, 2, W)

                group(None, True, False)
                with sp.Fori(0, NG - 1) as i:
                    group(i, False, False)
                group(None, False, True)

            load_x(0)
            load_straight(0, 1)
            load_x(1)
            load_straight(1, RAW)
            load_x(2)
            load_x(3)
            small_ones = small_inputs()
            assert len(small_ones) == VEC_DMAS
            sp.wait_ge(table_one, 1)
            for n in range(VEC_DMAS // 3):
                load_straight(RAW + n, RAW + n + 1)
                for to, src in small_ones[3 * n:3 * n + 3]:
                    sp.dma_start(to, src).then_inc(vec_in, 16)
            load_straight(RAW + VEC_DMAS // 3, FFN1)
            load_ffn(FFN1, "w_gate", "w_up", "w_down")
            load_straight(PLE, FFN2)
            load_ffn(FFN2, "w_gate_2", "w_up_2", "w_down_2")
            for c in (0, D // 2):
                for t, done in enumerate((fin_done, fin_done_act)):
                    sp.wait_ge(done, 1 + (c > 0))
                    sp.dma_start(out_d[:, t, c:c + D // 2], result[:, t, c:c + D // 2]).then_inc(out_stored, 16)
            sp.wait_ge(out_stored, 16 * 2 * TB)

        @block.gpsimd
        def _(pool):
            links = [0]

            def link(ins):
                links[0] += 1
                ins.then_inc(pool_link, 1)
                pool.wait_ge(pool_link, links[0])

            pool.memset(junk[:, 0:T], 1.0).then_inc(junk_set, 1)
            pool.memset(minus_half, -0.5).then_inc(pool_set, 1)
            pool.memset(scanm[:, :], 1.0).then_inc(pool_set, 1)
            pool.memset(table[:, :], 1.0).then_inc(table_one, 1)
            pool.wait_ge(pool_set, 2)
            pool.memset(scanm[:, 0:T:64], 0.0).then_inc(pool_set, 1)
            pool.memset(AT1[:, :, :, :], 0.0).then_inc(at_zero, 1)

            def inverse_root(to, sums, count, done):
                link(pool.tensor_scalar(to, sums, 1.0 / count, EPS, ALU.mult, ALU.add))
                pool.tensor_tensor(to, to, minus_half.to_broadcast([P, to.shape[1]]), ALU.pow).then_inc(done, 1)

            def norm(i):
                pool.wait_ge(squares_summed, i + 1)
                inverse_root(rstd[i], rstd[i], D, rstd_ready)

            def load_bias(e):
                pool.dma_start(Z[:, e % ZR, :], bass.AP(bias_rows.tensor, 512 * e, [[1, P], [1, 384]])).then_inc(z_in[e % ZR], 16)

            norm(0)
            pool.wait_ge(osq_out, 8)
            inverse_root(hrs, hsq, P, orstd)
            for j in range(len(PREP1)):
                pool.wait_ge(prep_sq, j + 1)
                inverse_root(hrs[:, 0:6], hsq[:, 0:6], P, prep_rstd)
            norm(1)
            norm(2)
            norm(3)
            pool.wait_ge(gate_w_in, 32)
            pool.memset(AT2[:, :, :, :], 0.0).then_inc(at_zero, 1)
            pool.wait_ge(rows_kept, 16)
            for e in range(ZR):
                load_bias(e)
            pool.wait_ge(osq_out, 16)
            inverse_root(hrs, hsq, T, orstd)
            for e in range(ZR, HEADS_2):
                pool.wait_ge(logits_out, 12 + e - ZR + 1)
                load_bias(e)
            norm(4)
            norm(5)

        @block.tensor
        def _(pe):
            def turn(out, in_):
                return pe.transpose(out, in_, ident)

            def multiply(n, base, i, per, width, kts, hi, lo, pair, first, last):
                if base < 8:
                    pe.wait_ge(lo_ready, base + 1)
                elif base % 2 == 0:
                    pe.wait_ge(lo_ready, n + 2)
                wh, wl = cut(w_hi, base % SPL, per, width), cut(w_lo, base % SPL, per, width)
                for k in range(per):
                    for t in range(TB):
                        to = acc[:, 2 * pair + t, 0:width]
                        s = slice(P * t, P * t + P)
                        for m, (xx, ww) in enumerate(((hi, wh), (hi, wl), (lo, wh))):
                            mm = pe.matmul(to, xx[:, kts[k], s], ww[:, k, :], start=first and k == 0 and m == 0,
                                           stop=last and k == per - 1 and m == 2)
                mm.then_inc(mm_done, 1)

            def turn_h(k):
                _, i, d = TURN[k]
                wait_h(pe, i, d)
                if k >= 2:
                    pe.wait_ge(xlo_ready, 2 * (k - 1))
                for m in range(4):
                    for t in range(TB):
                        c = P * (4 * d + m)
                        mm = turn(mb[:, 2 * (k % 2) + m // 2, T * (m % 2) + P * t:T * (m % 2) + P * t + P],
                                  h[:, t, c:c + P])
                    if m % 2:
                        mm.then_inc(h_turned, 1)

            def turn_panel(src, banks, tiles, done):
                for k in range(tiles):
                    for t in range(TB):
                        at = T * k + P * t
                        mm = turn(mb[:, banks + at // 512, at % 512:at % 512 + P], src[:, t, P * k:P * k + P])
                mm.then_inc(done, 1)

            def pair_levels(block, j):
                hp, lv = (LEVELS1 if block == 0 else LEVELS2)[j]
                k = j + 16 * block
                keys = queries = X1[:, k % 2, :].rearrange("p (h t) -> p h t", h=2)
                if block:
                    keys, queries = (X2[:, k % 2, m, :].rearrange("p (h t) -> p h t", h=2) for m in range(2))
                pe.wait_ge(x_out, k + 1)
                if j >= 2:
                    pe.wait_ge(pair_kept, (17 if block else 0) + j)
                for e in range(2):
                    if lv == 7:
                        for d in range(block + 1):
                            c = (256 if block else P) * e + P * d
                            mm = pe.matmul(mb[:, k % 2, c:c + P], keys[:, e, P * d:P * d + P],
                                           queries[:, e, P - P * d:2 * P - P * d], start=True, stop=True)
                        continue
                    for t in range(TB):
                        s = slice(P * t, P * t + P)
                        if block:
                            c = 256 * e + P * t
                            mm = pe.matmul(mb[:, k % 2, c:c + P], keys[:, e, s], queries[:, e, s], start=True, stop=True)
                            continue
                        size, c = LEVELS[lv], P * e + 64 * t
                        xq = queries[:, e, s].rearrange("p (b s l) -> p b s l", s=2, l=size)[:, :, 1, :]
                        to = mb[:, k % 2, c:c + 64].rearrange("p (b l) -> p b l", l=size)
                        mm = pe.matmul(to, keys[:, e, s], xq, start=True, stop=True)
                mm.then_inc(pair_made, 1)

            def diagonal(block):
                q, k = (a_reg[:, 0, :], a_reg[:, 1, :]) if block == 0 else (reg2[:, 0, :], reg2[:, 1, :])
                for e in range(4):
                    for t in range(TB):
                        s = slice(T * e + P * t, T * e + P * t + P)
                        to = mb[:, 2 + e // 2, 256 * (e % 2) + P * t:256 * (e % 2) + P * t + P]
                        for again in range(block + 1):
                            mm = pe.matmul(to, k[:, s], q[:, s], start=again == 0, stop=again == block)
                mm.then_inc(pair_made, 1)

            def make_o(block):
                AT = AT1 if block == 0 else AT2
                dv = P if block == 0 else T
                pe.wait_ge(pair_kept, 17 if block == 0 else 34)
                for t in range(TB):
                    for e in range(4):
                        to = mb[:, t, P * e:P * e + P] if block == 0 else mb[:, 2 * t + e // 2, T * (e % 2):T * (e % 2) + T]
                        srcs = [s for s in range(TB) if block == 1 or s <= t]
                        for s in srcs:
                            if block == 0:
                                v = a_reg[:, 2, :].rearrange("p (t n) -> p t n", t=TB)[:, s, P * e:P * e + P]
                            else:
                                v = reg2[:, 2 + e // 2, :].rearrange("p (t n) -> p t n", t=TB)[:, s, T * (e % 2):T * (e % 2) + T]
                            mm = pe.matmul(to, AT[:, e, s, P * t:P * t + P], v, start=s == srcs[0], stop=s == srcs[-1])
                mm.then_inc(o_made, 1)

            def scores(u):
                q, k, _, _, rows = head(u)
                to = mb[:, u % 2, :]
                if u >= 2:
                    pe.wait_ge(logits_out, u - 1)
                fox = u < HEADS_B
                fh = (u + 3) % HEADS_B
                second = u >= 12
                for t, (c, keys) in enumerate(LOGITS[second]):
                    mm = pe.matmul(to[:, c:c + keys], q[:, P * t:P * t + P], k[:, 0:keys], start=True, stop=not fox)
                    if fox:
                        for s in range(t + 1):
                            row = nlf[:, s, fh:fh + 1].to_broadcast([P, P])
                            if s < t:
                                pe.matmul(to[:, c + P:c + 2 * P], row, ones, start=False, stop=False)
                            mm = pe.matmul(to[:, c + P * s:c + P * s + P], row, upto, start=False, stop=s == t)
                return mm

            def turn_probs(u):
                second = u >= 12
                L = (L2 if second else L1)[:, u % 2, :]
                pe.wait_ge(probs_out, u + 1)
                if u >= 2:
                    pe.wait_ge(head_out, u - 1)
                to = mb[:, 2 + u % 2, :]
                if second:
                    spots = [(0, 0), (P, T), (T, P), (T + P, T + P)]
                else:
                    spots = [(0, 0), (P, P), (2 * P, T)]
                for src, dst in spots:
                    mm = turn(to[:, dst:dst + P], L[:, src:src + P])
                mm.then_inc(probs_turned, 1)

            def head_values(u):
                _, _, v, _, rows = head(u)
                second = u >= 12
                WT = (WT2 if second else WT1)[:, u % 2, :]
                lo = 64 * (u % 2) if second else 0
                to = mb[lo:lo + rows, 2 + u % 2, :]
                pe.wait_ge(probs_kept, u + 1)
                pe.matmul(to[:, 0:T], v[:, 0, :], WT[:, 0:T], start=True, stop=False)
                if second:
                    mm = pe.matmul(to[:, 0:T], v[:, 1, :], WT[:, T:2 * T], start=False, stop=True)
                else:
                    mm = pe.matmul(to[:, P:T], v[:, 1, :], WT[:, T:T + P], start=False, stop=True)
                mm.then_inc(head_made, 1)

            def head_steps(n, slots, u0):
                for i, s in enumerate(slots):
                    u = u0 + i
                    if n == s:
                        if u == 0:
                            pe.wait_ge(prep_out, 3)
                            pe.wait_ge(fcum_out, 1)
                        if u == 2:
                            pe.wait_ge(prep_out, 4)
                        if u == 6:
                            pe.wait_ge(prep_out, 6)
                        if u == 9:
                            pe.wait_ge(prep_out, 8)
                        if u == 12:
                            pe.wait_ge(prep_out, 10)
                        if u == 20:
                            pe.wait_ge(prep_out, 12)
                        scores(u).then_inc(scores_made, 1)
                    if n == s + 3:
                        turn_probs(u)
                    if n == s + 4:
                        head_values(u)

            def beside(n):
                if n == VEC:
                    pe.wait_ge(vec_in, 16 * VEC_DMAS)
                    pe.wait_ge(dq_out, 1)
                    for k, (s, rows) in enumerate(((0, NV), (1, 88), (2, 88))):
                        mm = pe.transpose(mb[:, 0, P * k:P * k + rows], stage[0:rows, s, :], ident[0:rows, 0:rows])
                    mm.then_inc(vec_turned, 1)
                    pe.matmul(mb[0:HEADS_2, 1, :], table[:, :], hot_sb[:, :], start=True, stop=True).then_inc(rows_made, 1)
                if n == HG["forget"] + 3:
                    pe.wait_ge(forget_out, 1)
                    pe.matmul(mb[:, 3, 0:6], upto, lf[:, 0, :], start=True, stop=True)
                    pe.matmul(mb[:, 3, 6:12], ones, lf[:, 0, :], start=True, stop=False)
                    pe.matmul(mb[:, 3, 6:12], upto, lf[:, 1, :], start=False, stop=True).then_inc(fcum_made, 1)
                if n == HG["turn_q"]:
                    wait_panel(pe, 0)
                    turn_panel(region(0)[0], 0, 4, dq_turned)
                if n == HG["turn_f"]:
                    wait_panel(pe, 1)
                    turn_panel(region(1)[0], 2, 4, dk_turned)
                if n == HG["levels"]:
                    pe.wait_ge(dk_out, 1)
                    pe.wait_ge(rows_out, 1)
                    diagonal(0)
                for j in range(len(LEVELS1)):
                    if n == level_slot(0, j) + 2:
                        pair_levels(0, j)
                if n == HG["make_o"]:
                    make_o(0)
                if n == HG["make_o"] + 4:
                    pe.wait_ge(o_scaled, 1)
                    pe.wait_ge(fcum_out, 1)
                    turn_panel(LG1[:, :].rearrange("p (t n) -> p t n", t=TB), 2, 4, o_turned)
                for j, (panel, s) in enumerate(PREP1.items()):
                    if n == s + 3:
                        pe.wait_ge(prep_scaled, j + 1)
                        if j:
                            pe.wait_ge(prep_out, j)
                        if j > 2:
                            pe.wait_ge(logits_out, sum(h0 < n for h0 in HEAD1))
                        turn_panel(region(panel)[0], 0, 3, prep_turned)
                head_steps(n, HEAD1, 0)

                if n == IN2 + 16:
                    wait_panel(pe, IN2_Q + 1)
                    pe.wait_ge(dq_out, 2)
                    for d in range(2):
                        for t in range(TB):
                            mm = turn(mb[0:16, 0, T * d + P * t:T * d + P * t + P], tail2[:, t, 16 * d:16 * d + 16])
                    mm.then_inc(lr_turned, 1)
                if n == IN2 + 18:
                    pe.wait_ge(lr_out, 1)
                    pe.wait_ge(gate_w_in, 32)
                    for d in range(2):
                        for e in range(4):
                            mm = pe.matmul(mb[:, 2 * d + e // 2, T * (e % 2):T * (e % 2) + T],
                                           gate_w[:, d, P * e:P * e + P], lr_t[:, d, :], start=True, stop=True)
                    mm.then_inc(gates_made, 1)
                if n == IN2 + 9:
                    wait_panel(pe, IN2_Q)
                    turn_panel(region(IN2_Q)[0], 0, 4, dq_turned)
                if n == IN2 + 25:
                    wait_panel(pe, IN2_Q + 2)
                    pe.wait_ge(gates_out, 2)
                    turn_panel(region(IN2_Q + 2)[0], 2, 4, dk_turned)
                if n == IN2 + 26:
                    pe.wait_ge(dk_out, 2)
                    pe.wait_ge(dq_out, 2)
                    diagonal(1)
                for j in range(len(LEVELS2)):
                    if n == level_slot(1, j) + 2:
                        pair_levels(1, j)
                if n == IN2 + 73:
                    make_o(1)
                if n == IN2 + 78:
                    pe.wait_ge(o_scaled, 3)
                    src = reg2[:, 0:2, :].rearrange("p r n -> p (r n)").rearrange("p (t n) -> p t n", t=TB)
                    turn_panel(src, 0, 8, o_turned)
                for j, (panel, s) in enumerate(PREP2.items()):
                    if n == s:
                        pe.wait_ge(panel_out[(IN2_Q + panel) % 2], (IN2_Q + panel) // 2 + 1)
                        if j == 0:
                            pe.wait_ge(o_kept, 2)
                        if j == 2:
                            pe.wait_ge(head_out, 20)
                        turn_panel(region(IN2_Q + panel)[0], 2 * (j % 2), 4, prep_turned)
                head_steps(n, HEAD2, 12)
                for k, (at, _, _) in enumerate(TURN):
                    if n == at:
                        turn_h(k)
                if n == TAIL1:
                    pe.wait_ge(p_landed, 16)
                    pe.wait_ge(prod_done, NG)
                    turn_panel(p_in, 2, 2, p_turned)

            def straight_part(a, z):
                for n in range(a, z):
                    p, q, j = straight[n]
                    if j == 0 and q >= 2:
                        pe.wait_ge(panel_out[q % 2], q // 2)
                    hi, lo, kts = x_hi, x_lo, [k for k in p.kts[j * p.per:(j + 1) * p.per]]
                    if p.source == "p":
                        hi, lo = p_hi, p_lo
                        pe.wait_ge(plo_ready, 1)
                    elif p.weight.startswith("w_out"):
                        from8 = 8 if p.weight == "w_out_2" else 0
                        pe.wait_ge(olo_ready, OSPLIT_ORDER.index(kts[0] // 2, from8) + 1)
                    elif q in (0, PLE_Q + 1, IN2_Q):
                        pe.wait_ge(xlo_ready, turned_before(norm_of(q), kts[0] // 2))
                    multiply(n, n, None, p.per, p.width, kts, hi, lo, q % 2, j == 0, j == p.chunks - 1)
                    beside(n)

            def ffn_part(which, base, base_q):
                norm_no = 1 if which == 0 else 4
                groups = NG * which

                def group(i, first, last):
                    if not last:
                        at = base if first else base + 16
                        qq = base_q if first else base_q + 2
                    else:
                        at, qq = base + 16 + (NG - 1) * GRP - 16, base_q + 2 + 6 * (NG - 1) - 2
                    number = grown(groups + (0 if first else 1), i, 1)
                    for c in range(16 if last else 0, 16 if first else GRP):
                        par = (qq + (c // 8 if c < 16 else 2 + (c - 16) // 2)) % 2
                        part = c // 8 if c < 16 else 2 + (c - 16) // 2
                        begins = c % 8 == 0 if c < 16 else c % 2 == 0
                        if begins:
                            pe.wait_ge(panel_out[par], grown((qq + part) // 2, i, 3))
                        n = chunk_of(at + c, i)
                        if first and c < 8:
                            pe.wait_ge(xlo_ready, turned_before(norm_no, c))
                        if c == 16:
                            pe.wait_ge(hlo_ready, groups + NG if last else grown(groups + 1, i, 1))
                        if c < 16:
                            multiply(n, at + c, i, 2, W, (2 * (c % 8), 2 * (c % 8) + 1), x_hi, x_lo, par,
                                     c % 8 == 0, c % 8 == 7)
                        else:
                            multiply(n, at + c, i, 2, W, (2 * (c % 2), 2 * (c % 2) + 1), h_hi, h_lo, par,
                                     c % 2 == 0, c % 2 == 1)
                        if first or last:
                            beside(at + c)
                        if last:
                            continue
                        if which == 0 and c == 9:
                            pe.wait_ge(panel_out[qq % 2], grown(qq // 2 + 1, i, 3))
                            if not first:
                                pe.wait_ge(conv_done, grown(1, i, 1))
                            turn_panel(gate_n, 0, FT, gate_turned)
                        if c == 15 and first or c == 17:
                            pe.wait_ge(panel_out[(qq + 1) % 2], grown((qq + 1) // 2 + 1, i, 3))
                            if not first:
                                pe.wait_ge(hlo_ready if which else prod_done, number)
                            turn_panel(up_n, 2 if which == 0 else 0, FT, up_turned)

                group(None, True, False)
                with pe.Fori(0, NG - 1) as i:
                    group(i, False, False)
                group(None, False, True)

            def keep_busy(times):
                for _ in range(times):
                    pe.matmul(acc[:, 3, 0:T], junk[:, 0:P], junk[:, 0:T], start=True, stop=True)

            pe.wait_ge(junk_set, 1)
            keep_busy(3)
            pe.wait_ge(const_in, 16)
            pe.wait_ge(gain_in, 16)
            pe.transpose(acc[:, 0, 0:KT], stage[0:KT, 0, :], ident[0:KT, 0:KT]).then_inc(gain_turned, 1)
            pe.wait_ge(gain_out, 1)
            keep_busy(1)
            beside(-2)
            keep_busy(4)
            beside(-1)
            straight_part(IN1, FFN1)
            ffn_part(0, FFN1, FFN1_Q)
            straight_part(PLE, FFN2)
            ffn_part(1, FFN2, FFN2_Q)

        @block.scalar
        def _(act):
            links = [0]

            def link(ins):
                links[0] += 1
                ins.then_inc(act_link, 1)
                act.wait_ge(act_link, links[0])

            def split_hi(n, base, i, per, width):
                act.wait_ge(raw_in[base % RAW], grown(16 * (base // RAW + 1), i, 16 * GRP // RAW))
                if i is not None or base >= SPL:
                    act.wait_ge(mm_done, n - (SPL - 1))
                act.activation(cut(w_hi, base % SPL, per, width), cut(raw, base % RAW, per, width),
                               ACT.Copy).then_inc(hi_ready, 1)

            def copy_panel(q, to, func=ACT.Copy, scaled=True, rest=None):
                width = to.shape[2]
                if scaled:
                    act.wait_ge(rstd_ready, norm_of(q) + 1)
                for t in range(TB):
                    scale = rstd[norm_of(q)][:, t:t + 1] if scaled else 1.0
                    ins = act.activation(to[:, t, :], panel_in(t, q)[:, 0:width], func, scale=scale)
                    if rest is not None:
                        ins = act.activation(rest[:, t, :], panel_in(t, q)[:, width:width + rest.shape[2]], func,
                                             scale=scale)
                ins.then_inc(panel_out[q % 2], 1)

            squares = [0]

            def square(i, d):
                wait_h(act, i, d)
                for t in range(TB):
                    if squares[0]:
                        act.wait_ge(squares_out, squares[0])
                    act.activation(junk[:, :], h[:, t, W * d:W * d + W], ACT.Square,
                                   accum_out=sums[:, i % 2, t, d:d + 1]).then_inc(squares_out, 1)
                    squares[0] += 1

            def turned_hi(k):
                _, i, d = TURN[k]
                for pair in range(2):
                    act.wait_ge(h_turned, 2 * k + pair + 1)
                    if i == 3 and d < 3:
                        act.wait_ge(mm_done, PLE_END - 8 + 2 * d + pair + 1)
                    for m in (2 * pair, 2 * pair + 1):
                        kt = 4 * d + m
                        ins = act.activation(x_hi[:, kt, :], mb[:, 2 * (k % 2) + m // 2, T * (m % 2):T * (m % 2) + T],
                                             ACT.Copy, scale=NORM[i][:, kt:kt + 1])
                    ins.then_inc(xhi_ready, 1)
                if i:
                    square(i, d)

            def square_o(block):
                act.wait_ge(pair_made, 17 if block == 0 else 34)
                dv, o_psum = (P, mb[:, 0:2, :]) if block == 0 else (T, mb[:, :, :])
                o_flat = o_psum.rearrange("p a n -> p (a n)")
                X = (X1[:, :, :] if block == 0 else X2[:, 0, :, :]).rearrange("p a n -> p (a n)")
                for g8 in range(8):
                    if g8 >= 4 and dv == T:
                        act.wait_ge(osq_out, 8 + g8 - 3)
                    act.activation(X[:, dv * g8 % 1024:dv * g8 % 1024 + dv], o_flat[:, dv * g8:dv * g8 + dv], ACT.Square,
                                   accum_out=hsq[:, g8:g8 + 1]).then_inc(osq_out, 1)

            def gate_part(x, k, log):
                act.wait_ge(exp_abs if log else neg_abs, k + 1)
                if log:
                    act.activation(x, x, ACT.Ln, bias=1.0).then_inc(log1p_out, 1)
                else:
                    act.activation(x, x, ACT.Exp, scale=1.0 if k else -1.0).then_inc(exp_abs, 1)

            def level_exp(blk, j):
                k = j + 16 * blk
                X = X1[:, k % 2, :] if blk == 0 else X2[:, k % 2, :, :].rearrange("p a n -> p (a n)")
                act.wait_ge(expo_out, k + 1)
                act.activation(X, X, ACT.Exp).then_inc(exp_out, 1)

            def head_steps(n, slots, u0):
                for i, s in enumerate(slots):
                    u = u0 + i
                    second = u >= 12
                    L = (L2 if second else L1)[:, u % 2, :]
                    WT = (WT2 if second else WT1)[:, u % 2, :]
                    if n == s + 2:
                        act.wait_ge(logits_out, u + 1)
                        for t, (c, keys) in enumerate(LOGITS[second]):
                            at = 2 * (u % 2) + t
                            ins = act.activation(L[:, c:c + keys], L[:, c:c + keys], ACT.Exp,
                                                 bias=negmax[:, at:at + 1], accum_out=rowsum[:, at:at + 1])
                        ins.then_inc(exps_out, 1)
                    if n == s + 4:
                        act.wait_ge(probs_turned, u + 1)
                        if u >= 2:
                            act.wait_ge(head_made, u - 1)
                        width = 512 if second else 384
                        act.activation(WT[:, 0:width], mb[:, 2 + u % 2, 0:width], ACT.Copy).then_inc(probs_kept, 1)
                    if n == s + 5:
                        _, _, _, o, rows = head(u)
                        lo = 64 * (u % 2) if second else 0
                        act.wait_ge(head_made, u + 1)
                        act.activation(o, mb[lo:lo + rows, 2 + u % 2, 0:T], ACT.Copy).then_inc(head_out, 1)

            def beside(n):
                if n - 1 in ends and (n <= OUT1 or IN2 < n <= OUT2):
                    q = ends[n - 1]
                    act.wait_ge(mm_done, n)
                    if q == 6:
                        copy_panel(q, region(q)[0], rest=tail)
                    elif q in (IN2_Q + 5, IN2_Q + 6):
                        c = GRW * (q - IN2_Q - 5)
                        copy_panel(q, gr[:, :, c:c + GRW])
                    elif q == IN2_Q + 1:
                        copy_panel(q, gr[:, :, 2 * GRW:1024], rest=tail2)
                    else:
                        copy_panel(q, region(q)[0])
                if n in (1, 2, 3, 4):
                    square(0, n - 1)
                if n == VEC:
                    act.wait_ge(vec_turned, 1)
                    act.activation(vecs[:, KT:NV], mb[:, 0, KT:NV], ACT.Copy).then_inc(vec_out, 1)
                    act.activation(conv[:, :, :], mb[:, 0, P:P + 2 * P].rearrange("p (a n) -> p a n", a=2)[:, :, 0:88],
                                   ACT.Copy).then_inc(vec_out, 1)
                    act.wait_ge(rows_made, 1)
                    act.activation(rows_sb, mb[0:HEADS_2, 1, :], ACT.Copy).then_inc(rows_out, 1)
                    act.wait_ge(rows_out, 1)
                    act.dma_start(bias_rows, rows_sb).then_inc(rows_kept, 16)
                if n == HG["forget"] + 2:
                    act.wait_ge(forget_exp, 1)
                    flat = small[:, 64:76]
                    link(act.activation(flat, flat, ACT.Exp))
                    act.activation(flat, flat, ACT.Ln, bias=1.0).then_inc(log1p_out, 1)
                if n == HG["forget"] + 4:
                    act.wait_ge(fcum_made, 1)
                    act.activation(small[:, 76:88], mb[:, 3, 0:12], ACT.Copy).then_inc(fcum_out, 1)
                if n == HG["turn_q"] + 1:
                    act.wait_ge(dq_turned, 1)
                    act.activation(a_reg[:, 0, :], mb[:, 0:2, :].rearrange("p a n -> p (a n)"), ACT.Silu).then_inc(dq_out, 1)
                if n == HG["turn_f"] + 1:
                    act.wait_ge(dk_turned, 1)
                    act.activation(X1[:, :, :].rearrange("p a n -> p (a n)"), mb[:, 2:4, :].rearrange("p a n -> p (a n)"),
                                   ACT.Abs).then_inc(neg_abs, 1)
                if n in (HG["turn_f"] + 2, HG["turn_f"] + 3):
                    gate_part(X1[:, :, :].rearrange("p a n -> p (a n)"), 0, n == HG["turn_f"] + 3)
                if n == HG["turn_f"] + 5:
                    act.wait_ge(logf_out, 1)
                    act.activation(a_reg[:, 1, :], a_reg[:, 1, :], ACT.Exp).then_inc(dk_out, 1)
                for j in range(len(LEVELS1)):
                    if n == level_slot(0, j) + 1:
                        level_exp(0, j)
                if n == HG["make_o"] + 1:
                    act.wait_ge(o_made, 1)
                    act.activation(LG1[:, :], mb[:, 0:2, :].rearrange("p a n -> p (a n)"), ACT.Copy).then_inc(o_out, 1)
                    square_o(0)
                if n == HG["make_o"] - 3:
                    wait_panel(act, 3)
                    act.activation(a_reg[:, 3, :], a_reg[:, 3, :], ACT.Silu).then_inc(og_out, 1)
                if n == HG["make_o"] + 5:
                    act.wait_ge(o_turned, 1)
                    act.activation(a_reg[:, 3, :], mb[:, 2:4, :].rearrange("p a n -> p (a n)"), ACT.Copy,
                                   scale=hgrn_gain).then_inc(o_kept, 1)
                for j, (panel, s) in enumerate(PREP1.items()):
                    if n == s:
                        wait_panel(act, panel)
                        act.wait_ge(pair_made, 17)
                        if j:
                            act.wait_ge(prep_sq, j)
                        act.activation(B1[:, 0:768], bc_reg[:, panel - 4, :], ACT.Square).then_inc(prep_squared, 1)
                    if n == s + 4:
                        act.wait_ge(prep_turned, j + 1)
                        act.activation(bc_reg[:, panel - 4, :], mb[:, 0:2, :].rearrange("p a n -> p (a n)")[:, 0:768],
                                       ACT.Copy, scale=qk_gain[j // 4 * 2 + j % 2]).then_inc(prep_out, 1)
                head_steps(n, HEAD1, 0)

                if n == IN2 + 17:
                    act.wait_ge(lr_turned, 1)
                    act.activation(lr_t, mb[0:16, 0, :].rearrange("p (d t) -> p d t", d=2), ACT.Copy).then_inc(lr_out, 1)
                if n in (IN2 + 19, IN2 + 20):
                    d = n - IN2 - 19
                    act.wait_ge(gates_made, 1)
                    for e in range(4):
                        ins = act.activation((BF2, BB2)[d][:, T * e:T * e + T],
                                             mb[:, 2 * d + e // 2, T * (e % 2):T * (e % 2) + T],
                                             ACT.Identity, bias=gate_bias[d][:, e:e + 1])
                    ins.then_inc(gates_out, 1)
                if n in (IN2 + 21, IN2 + 22):
                    gate_part(gate_abs[n - IN2 - 21], n - IN2 - 20, False)
                if n == IN2 + 23:
                    for d in range(2):
                        gate_part(gate_abs[d], d + 1, True)
                if n == IN2 + 10:
                    act.wait_ge(dq_turned, 2)
                    act.activation(reg2[:, 0, :], mb[:, 0:2, :].rearrange("p a n -> p (a n)"), ACT.Copy,
                                   scale=float(P) ** -0.5).then_inc(dq_out, 1)
                if n == IN2 + 26:
                    act.wait_ge(dk_turned, 2)
                    act.activation(reg2[:, 1, :], mb[:, 2:4, :].rearrange("p a n -> p (a n)"), ACT.Copy).then_inc(dk_out, 1)
                for j in range(len(LEVELS2)):
                    if n == level_slot(1, j) + 1:
                        level_exp(1, j)
                if n == IN2 + 57:
                    wait_panel(act, IN2_Q + 6)
                    wait_panel(act, IN2_Q + 5)
                    act.activation(gr, gr, ACT.Silu).then_inc(og_out, 1)
                if n == IN2 + 74:
                    act.wait_ge(o_made, 2)
                    act.activation(reg2[:, 0:2, :].rearrange("p a n -> p (a n)"), mb[:, :, :].rearrange("p a n -> p (a n)"),
                                   ACT.Copy).then_inc(o_out, 1)
                if n == IN2 + 75:
                    square_o(1)
                if n == IN2 + 79:
                    act.wait_ge(o_turned, 2)
                    for kt in range(8):
                        ins = act.activation(o_turned_at(8 + kt, 1), mb[:, kt // 2, T * (kt % 2):T * (kt % 2) + T], ACT.Copy,
                                             scale=gla_gain[:, kt:kt + 1])
                    ins.then_inc(o_kept, 1)
                for j, (panel, s) in enumerate(PREP2.items()):
                    if n == s + 1:
                        act.wait_ge(prep_turned, 8 + j + 1)
                        src = mb[:, 2 * (j % 2):2 * (j % 2) + 2, :].rearrange("p a n -> p (a n)")
                        act.activation(reg2[:, panel - 1, :], src, ACT.Copy,
                                       scale=64.0 ** -0.5 if j % 2 == 0 else 1.0).then_inc(prep_out, 1)
                head_steps(n, HEAD2, 12)
                if n in OSPLIT:
                    blk = n >= IN2
                    act.wait_ge(mm_done, n + 1)
                    act.wait_ge(o_kept, blk + 1)
                    if n in (IN1_END - 8 + 2, OUT1 + 22, OUT2 + 1, OUT2 + 22):
                        act.wait_ge(head_out, {IN1_END - 6: 9, OUT1 + 22: 12, OUT2 + 1: 20, OUT2 + 22: 28}[n])
                    for pair in OSPLIT[n]:
                        for kt in (2 * pair, 2 * pair + 1):
                            ins = act.activation(x_hi[:, kt, :], o_turned_at(kt, int(blk)), ACT.Copy)
                        ins.then_inc(ohi_ready, 1)
                if PLE <= n < PLE_END and n in ends:
                    q = ends[n]
                    j = (q - PLE_Q) // 2
                    act.wait_ge(mm_done, n + 1)
                    if (q - PLE_Q) % 2 == 0:
                        if j:
                            act.wait_ge(ple_added, j)
                        copy_panel(q, pn, scaled=False)
                    else:
                        copy_panel(q, gate_n, ACT.Sigmoid)
                for k in range(len(TURN)):
                    if n == split_slot(k):
                        turned_hi(k)
                if n == FFN1:
                    act.dma_start(p_in[:, :, :], g["p"].rearrange("a b (t p) d -> p (a b t) d", p=P)).then_inc(p_landed, 16)
                if n == FFN2:
                    act.dma_start(fin_g[:, :], g["final_norm_w_2"].rearrange("(a d) -> a d", a=1)
                                  .to_broadcast([P, D])).then_inc(fin_in, 16)
                if TAIL2 < n and (n - TAIL2) % 2 == 0:
                    square(5, (n - TAIL2) // 2 - 1)
                if n == IN2 + 1:
                    for d, name in enumerate(("gla_gate_w_fwd_2", "gla_gate_w_bwd_2")):
                        act.dma_start(gate_w[:, d, :], g[name].rearrange("a r c -> (a r) c")).then_inc(gate_w_in, 16)
                if n == TAIL1 + 1:
                    act.wait_ge(p_turned, 1)
                    act.activation(p_hi[:, :, :].rearrange("p a n -> p (a n)"), mb[:, 2, :], ACT.Copy).then_inc(phi_ready, 1)

            def split_ahead(n):
                m = n + AHEAD
                if m < TOTAL:
                    per, width = shape_of(m)
                    split_hi(m, m, None, per, width)

            def straight_part(a, z):
                for n in range(a, z):
                    split_ahead(n)
                    beside(n)

            def ffn_part(which, base, base_q):
                groups = NG * which
                norm_no = 1 if which == 0 else 4

                def group(i, first, last):
                    at = base if first else base + 16
                    qq = base_q if first else base_q + 2
                    if last:
                        at += (NG - 1) * GRP - 16
                    gi = 0 if first else 1

                    def split_hidden(n):
                        act.wait_ge(mm_done, n)
                        if which == 0:
                            act.wait_ge(prod_done, NG if last else grown(1, i, 1))
                            src = cv[:, :, :].rearrange("p a n -> p (a n)")
                        else:
                            act.wait_ge(up_turned, groups + NG if last else grown(groups + 1, i, 1))
                            src = mb[:, 0:2, :].rearrange("p a n -> p (a n)")
                        act.activation(h_hi[:, :, :].rearrange("p a n -> p (a n)"), src, ACT.Copy).then_inc(hhi_ready, 1)

                    if last:
                        split_hidden(at + 16)
                    for c in range(16 if last else 0, 16 if first else GRP):
                        n = chunk_of(at + c, i)
                        if last:
                            split_ahead(at + c)
                            beside(at + c)
                            continue
                        split_hi(chunk_of(at + c + AHEAD, i), at + c + AHEAD, i, 2, W)
                        if c == 0 and not first:
                            split_hidden(n)
                        if first:
                            beside(at + c)
                        if c == 7:
                            act.wait_ge(mm_done, n + 1)
                            act.wait_ge(rstd_ready, norm_no + 1)
                            if which == 0:
                                if not first:
                                    act.wait_ge(gate_turned, grown(gi, i, 1))
                            elif not first:
                                act.wait_ge(panel_out[(base_q + 1) % 2], grown((base_q + 1) // 2 + 1, i, 3))
                            for t in range(TB):
                                ins = act.activation(gate_n[:, t, :], panel_in(t, qq), ACT.Copy if which == 0 else ACT.Silu,
                                                     scale=rstd[norm_no][:, t:t + 1])
                            ins.then_inc(panel_out[qq % 2], 1)
                        if which == 0 and c == 10:
                            act.wait_ge(gate_turned, grown(gi + 1, i, 1))
                            if not first:
                                act.wait_ge(hlo_ready, grown(gi, i, 1))
                            for ft in range(FT):
                                at_f = ft if first else i * FT + (FT + ft)
                                ins = act.activation(cv[:, ft, :], mb[:, ft // 2, T * (ft % 2):T * (ft % 2) + T],
                                                     ACT.Identity, bias=conv[:, 3, bass.ds(at_f, 1)],
                                                     scale=conv[:, 2, bass.ds(at_f, 1)])
                            ins.then_inc(conv_begun, 1)
                        if which == 0 and c == 13:
                            act.wait_ge(conv_done, grown(gi + 1, i, 1))
                            flat = cv[:, :, :].rearrange("p a n -> p (a n)")
                            act.activation(flat, flat, ACT.Gelu_apprx_tanh).then_inc(gelu_done, 1)
                        if which == 0 and c == 15:
                            act.wait_ge(mm_done, n + 1)
                            if not first:
                                act.wait_ge(up_turned, grown(gi, i, 1))
                            for t in range(TB):
                                ins = act.activation(up_n[:, t, :], panel_in(t, qq + 1), ACT.Copy,
                                                     scale=rstd[norm_no][:, t:t + 1])
                            ins.then_inc(panel_out[(qq + 1) % 2], 1)

                group(None, True, False)
                with act.Fori(0, NG - 1) as i:
                    group(i, False, False)
                group(None, False, True)

            act.dma_start(stage[0:KT, 0, :], g["attn_norm"].rearrange("a (k p) -> (a k) p", p=P)).then_inc(gain_in, 16)
            act.wait_ge(gain_turned, 1)
            act.activation(vecs[:, 0:KT], acc[:, 0, 0:KT], ACT.Copy).then_inc(gain_out, 1)
            act.wait_ge(gain_out, 1)
            beside(-2)
            split_ahead(0 - AHEAD)
            beside(-1)
            for n in range(1, AHEAD):
                split_ahead(n - AHEAD)
            straight_part(IN1, FFN1)
            ffn_part(0, FFN1, FFN1_Q)
            straight_part(PLE, FFN2)
            ffn_part(1, FFN2, FFN2_Q)
            square(5, 3)
            act.wait_ge(fin_gained, 4)
            act.wait_ge(rstd_ready, 6)
            for c in (0, D // 2):
                part = result[:, 1, c:c + D // 2]
                act.activation(part, part, ACT.Copy, scale=rstd[5][:, 1:2]).then_inc(fin_done_act, 1)

        @block.vector
        def _(dve):
            links = [0]

            def link(ins):
                links[0] += 1
                ins.then_inc(dve_link, 1)
                dve.wait_ge(dve_link, links[0])

            def split_lo(n, base, i, per, width):
                dve.wait_ge(hi_ready, n + 1)
                dve.tensor_tensor(cut(w_lo, base % SPL, per, width), cut(raw, base % RAW, per, width),
                                  cut(w_hi, base % SPL, per, width).bitcast(F32), ALU.subtract).then_inc(lo_ready, 1)

            def add_panel(q, col):
                for t in range(TB):
                    to = h[:, t, col:col + W]
                    ins = dve.tensor_tensor(to, panel_in(t, q), to, ALU.add)
                return ins

            def sum_squares(i):
                dve.wait_ge(squares_out, 4 * TB * (i + 1))
                dve.tensor_reduce(rstd[i], sums[:, i % 2, :, :], AX_X, ALU.add).then_inc(squares_summed, 1)

            def gain_final(d):
                dve.wait_ge(fin_in, 16)
                wait_h(dve, 5, d)
                for t in range(TB):
                    ins = dve.tensor_tensor(result[:, t, W * d:W * d + W], h[:, t, W * d:W * d + W],
                                            fin_g[:, W * d:W * d + W], ALU.mult)
                ins.then_inc(fin_gained, 1)

            def turned_lo(k):
                _, i, d = TURN[k]
                for pair in range(2):
                    dve.wait_ge(xhi_ready, 2 * k + pair + 1)
                    for m in (2 * pair, 2 * pair + 1):
                        kt = 4 * d + m
                        ins = dve.scalar_tensor_tensor(x_lo[:, kt, :], mb[:, 2 * (k % 2) + m // 2, T * (m % 2):T * (m % 2) + T],
                                                       NORM[i][:, kt:kt + 1], x_hi[:, kt, :].bitcast(F32),
                                                       ALU.mult, ALU.subtract)
                    ins.then_inc(xlo_ready, 1)
                if i and k % 4 == 3:
                    sum_squares(i)

            def level_expo(blk, j):
                hp, lv = (LEVELS1 if blk == 0 else LEVELS2)[j]
                k = j + 16 * blk
                if j >= 2:
                    dve.wait_ge(pair_made, (17 if blk else 0) + j)
                for d in range(blk + 1):
                    B = ((B1,) if blk == 0 else (BF2, BB2))[d][:, 512 * hp:512 * hp + 512]
                    keys = queries = X1[:, k % 2, :]
                    if blk:
                        keys, queries = X2[:, k % 2, 0, :], X2[:, k % 2, 1, :]
                    if lv < 7:
                        size = LEVELS[lv]
                        form = dict(rearrange_str="p (b s l) -> p b s l", s=2, l=size)
                        r, xk, xq = B.rearrange(**form), keys.rearrange(**form), queries.rearrange(**form)
                        e0 = size - 1 if d == 0 else 0
                        ref = r[:, :, d, e0:e0 + 1].to_broadcast([P, 512 // (2 * size), size])
                        dve.tensor_tensor(xk[:, :, d, :], ref, r[:, :, d, :], ALU.subtract)
                        if size < 64:
                            ins = dve.tensor_tensor(xq[:, :, 1 - d, :], r[:, :, 1 - d, :], ref, ALU.subtract)
                        else:
                            ins = dve.tensor_copy(xq[:, :, 1 - d, :], r[:, :, 1 - d, :])
                        continue
                    r, xk, xq = (y.rearrange("p (h c l) -> p h c l", c=4, l=64) for y in (B, keys, queries))
                    fk, nk, nq, fq = (0, 1, 2, 3) if d == 0 else (3, 2, 1, 0)
                    e0 = 63 if d == 0 else 0
                    both = full01[:, 2 * d:2 * d + 2]
                    link(dve.tensor_tensor(both, r[:, :, nk, e0], r[:, :, fk, e0], ALU.add))

                    def whole(c):
                        return r[:, :, c, e0:e0 + 1].to_broadcast([P, 2, 64])

                    dve.tensor_tensor(xk[:, :, nk, :], whole(nk), r[:, :, nk, :], ALU.subtract)
                    dve.tensor_tensor(xk[:, :, fk, :], both.unsqueeze(2).to_broadcast([P, 2, 64]), r[:, :, fk, :],
                                      ALU.subtract)
                    dve.tensor_copy(xq[:, :, nq, :], r[:, :, nq, :])
                    ins = dve.tensor_tensor(xq[:, :, fq, :], r[:, :, fq, :], whole(nq), ALU.add)
                ins.then_inc(expo_out, 1)

            def level_mult(blk, j):
                hp, lv = (LEVELS1 if blk == 0 else LEVELS2)[j]
                k = j + 16 * blk
                dve.wait_ge(exp_out, k + 1)
                if blk:
                    for m in range(2):
                        x = X2[:, k % 2, m, :]
                        ins = dve.tensor_tensor(x, x, reg2[:, 1 - m, 512 * hp:512 * hp + 512], ALU.mult)
                else:
                    size = LEVELS[lv] if lv < 7 else P
                    x = X1[:, k % 2, :].rearrange("p (b s l) -> p b s l", s=2, l=size)
                    for half, src in ((0, a_reg[:, 1, :]), (1, a_reg[:, 0, :])):
                        s = src[:, 512 * hp:512 * hp + 512].rearrange("p (b s l) -> p b s l", s=2, l=size)
                        ins = dve.tensor_tensor(x[:, :, half, :], x[:, :, half, :], s[:, :, half, :], ALU.mult)
                ins.then_inc(x_out, 1)

            def level_keep(blk, j):
                hp, lv = (LEVELS1 if blk == 0 else LEVELS2)[j]
                k = j + 16 * blk
                A = (AT1 if blk == 0 else AT2)[:, :, :, :].rearrange("p h s (a l) -> p h (s a) l", l=P)
                dve.wait_ge(pair_made, (17 if blk else 0) + 1 + j + 1)
                dve.wait_ge(pair_kept, (17 if blk else 0) + 1 + j)
                if lv == 7:
                    for d in range(blk + 1):
                        src = mb[:, k % 2, 0:256 * (blk + 1)].rearrange("p (h l) -> p h l", h=2)[:, :, P * d:P * d + P]
                        ins = dve.tensor_copy(A[:, 2 * hp:2 * hp + 2, 1 + d, :], src)
                    ins.then_inc(pair_kept, 1)
                    return
                size = LEVELS[lv]
                for e in range(2):
                    to = A[:, 2 * hp + e, 0:4:3, :]
                    if blk:
                        src = mb[:, k % 2, 256 * e:256 * e + 256].rearrange("p (t l) -> p t l", t=TB)
                        mask = masks[:, 8 + lv:9 + lv, :].to_broadcast([P, TB, P])
                    else:
                        to = to.rearrange("p t (b s l) -> p t b s l", s=2, l=size)[:, :, :, 1, :]
                        src = mb[:, k % 2, P * e:P * e + P].rearrange("p (t b l) -> p t b l", t=TB, l=size)
                        mask = masks[:, 1 + lv, :].rearrange("p (b s l) -> p b s l", s=2, l=size)[:, :, 1, :]\
                            .unsqueeze(1).to_broadcast([P, TB, 64 // size, size])
                    ins = dve.copy_predicated(to, mask, src)
                ins.then_inc(pair_kept, 1)

            def diagonal_keep(blk):
                A = (AT1 if blk == 0 else AT2)[:, :, :, :].rearrange("p h s (a l) -> p h (s a) l", l=P)
                dve.wait_ge(pair_made, (17 if blk else 0) + 1)
                dve.wait_ge(at_zero, blk + 1)
                for e in range(4):
                    ins = dve.copy_predicated(A[:, e, 0:4:3, :], masks[:, 0:1, :].to_broadcast([P, 2, P]),
                                              mb[:, 2 + e // 2, 256 * (e % 2):256 * (e % 2) + 256].rearrange("p (b l) -> p b l", b=2))
                ins.then_inc(pair_kept, 1)

            def scan(B, src, back):
                for e in range(4):
                    a, z = B[:, T * e:T * e + T], src[:, T * e:T * e + T]
                    if back:
                        a, z = a[:, ::-1], z[:, ::-1]
                    ins = dve.tensor_tensor_scan(a, scanm[:, :], z, 0.0, ALU.mult, ALU.add)
                ins.then_inc(decay_out, 1)

            def head_steps(n, slots, u0):
                for i, s in enumerate(slots):
                    u = u0 + i
                    second = u >= 12
                    L = (L2 if second else L1)[:, u % 2, :]
                    if n == s + 1:
                        S = mb[:, u % 2, :]
                        dve.wait_ge(scores_made, u + 1)
                        if u >= 2:
                            dve.wait_ge(probs_turned, u - 1)
                        if second:
                            dve.wait_ge(z_in[(u - 12) % ZR], 16 * ((u - 12) // ZR + 1))
                        for t, (c, keys) in enumerate(LOGITS[second]):
                            s_t, l_t = S[:, c:c + keys], L[:, c:c + keys]
                            if u < HEADS_B:
                                ins = dve.scalar_tensor_tensor(l_t, s_t, fcum[:, t, (u + 3) % HEADS_B:(u + 3) % HEADS_B + 1], causal[:, c:c + keys],
                                                               ALU.add, ALU.add)
                            elif u < 12:
                                slope = 2.0 ** (-8.0 * (u - HEADS_B + 1) / HEADS_C)
                                ins = dve.scalar_tensor_tensor(l_t, alibi[:, c:c + keys], slope, s_t, ALU.mult, ALU.add)
                            else:
                                z = Z[:, (u - 12) % ZR, P * t:P * t + T]
                                ins = dve.tensor_tensor(l_t, s_t, z[:, ::-1], ALU.add)
                        link(ins)
                        for t, (c, keys) in enumerate(LOGITS[second]):
                            at = 2 * (u % 2) + t
                            ins = dve.tensor_reduce(negmax[:, at:at + 1], L[:, c:c + keys], AX_X, ALU.max, negate=True)
                        ins.then_inc(logits_out, 1)
                    if n == s + 2:
                        dve.wait_ge(exps_out, u + 1)
                        at = 2 * (u % 2)
                        link(dve.reciprocal(rowinv[:, at:at + 2], rowsum[:, at:at + 2]))
                        for t, (c, keys) in enumerate(LOGITS[second]):
                            ins = dve.tensor_scalar(L[:, c:c + keys], L[:, c:c + keys], rowinv[:, at + t:at + t + 1], None,
                                                    ALU.mult)
                        ins.then_inc(probs_out, 1)

            def beside(n):
                if n == 4:
                    sum_squares(0)
                if n == VEC + 1:
                    dve.wait_ge(vec_in, 16 * VEC_DMAS)
                    dve.wait_ge(vec_out, 1)
                    dve.tensor_copy(masks[:, :, :].rearrange("p a n -> p (a n)"), masks_f)
                    for j in (0, 2):
                        dve.tensor_scalar(qk_gain[j], qk_gain[j], float(P) ** -0.5, None, ALU.mult)
                if n == HG["forget"] + 1:
                    wait_panel(dve, 6)
                    link(dve.tensor_tensor(lf, tail[:, :, :], fbias.unsqueeze(1).to_broadcast([P, TB, HEADS_B]), ALU.add))
                    dve.scalar_tensor_tensor(nlf, lf, -1.0, lf, ALU.mult, ALU.min).then_inc(forget_exp, 1)
                if n == HG["forget"] + 2:
                    dve.wait_ge(log1p_out, 2)
                    link(dve.scalar_tensor_tensor(lf, lf, 0.0, nlf, ALU.min, ALU.subtract))
                    dve.tensor_scalar(nlf, lf, -1.0, None, ALU.mult).then_inc(forget_out, 1)
                if n == HG["turn_f"] + 4:
                    z = mb[:, 2:4, :].rearrange("p a n -> p (a n)")
                    dve.wait_ge(log1p_out, 1)
                    dve.wait_ge(rows_kept, 16)
                    link(dve.scalar_tensor_tensor(LG1[:, :], z, 0.0, X1[:, :, :].rearrange("p a n -> p (a n)"),
                                                  ALU.min, ALU.subtract))
                    dve.tensor_tensor(a_reg[:, 1, :], LG1[:, :], z, ALU.subtract).then_inc(logf_out, 1)
                    dve.wait_ge(logf_out, 1)
                    link(dve.tensor_scalar(LG1[:, :], LG1[:, :], LN_TINY, None, ALU.max))
                    scan(B1, LG1, False)
                if n == HG["levels"]:
                    dve.wait_ge(decay_out, 1)
                if n == HG["levels"] + 1:
                    diagonal_keep(0)
                for j in range(len(LEVELS1)):
                    if n == level_slot(0, j):
                        level_expo(0, j)
                    if n == level_slot(0, j) + 1:
                        level_mult(0, j)
                    if n == level_slot(0, j) + 3:
                        level_keep(0, j)
                if n == HG["make_o"] + 3:
                    dve.wait_ge(orstd, 1)
                    dve.wait_ge(o_out, 1)
                    dve.wait_ge(og_out, 1)
                    for g8 in range(8):
                        o = LG1[:, P * g8:P * g8 + P]
                        ins = dve.scalar_tensor_tensor(o, o, hrs[:, g8:g8 + 1], a_reg[:, 3, P * g8:P * g8 + P],
                                                       ALU.mult, ALU.mult)
                    ins.then_inc(o_scaled, 1)
                for j, (panel, s) in enumerate(PREP1.items()):
                    r = bc_reg[:, panel - 4, :]
                    if n == s + 1:
                        dve.wait_ge(prep_squared, j + 1)
                        dve.tensor_reduce(hsq[:, 0:6], B1[:, 0:768].rearrange("p (g l) -> p g l", l=P), AX_X, ALU.add)\
                            .then_inc(prep_sq, 1)
                    if n == s + 2:
                        dve.wait_ge(prep_rstd, j + 1)
                        v = r.rearrange("p (g l) -> p g l", l=P)
                        dve.tensor_tensor(v, v, hrs[:, 0:6].unsqueeze(2).to_broadcast([P, 6, P]), ALU.mult)\
                            .then_inc(prep_scaled, 1)
                head_steps(n, HEAD1, 0)

                if n in (IN2 + 20, IN2 + 21):
                    d = n - IN2 - 20
                    B = (BF2, BB2)[d][:, :]
                    dve.wait_ge(gates_out, d + 1)
                    dve.scalar_tensor_tensor(gate_abs[d], B, -1.0, B, ALU.mult, ALU.min).then_inc(neg_abs, 1)
                if n in (IN2 + 24, IN2 + 25):
                    d = n - IN2 - 24
                    B, X = (BF2, BB2)[d][:, :], gate_abs[d]
                    dve.wait_ge(log1p_out, 3 + d)
                    link(dve.scalar_tensor_tensor(X, B, 0.0, X, ALU.min, ALU.subtract))
                    link(dve.tensor_scalar(X, X, 1.0 / 16.0, None, ALU.mult))
                    scan((BF2, BB2)[d], X, d == 1)
                if n == IN2 + 26:
                    dve.wait_ge(decay_out, 3)
                if n == IN2 + 27:
                    diagonal_keep(1)
                for j in range(len(LEVELS2)):
                    if n == level_slot(1, j):
                        level_expo(1, j)
                    if n == level_slot(1, j) + 1:
                        level_mult(1, j)
                    if n == level_slot(1, j) + 3:
                        level_keep(1, j)
                if n in (IN2 + 76, IN2 + 77):
                    dve.wait_ge(orstd, 2)
                    dve.wait_ge(o_out, 2)
                    dve.wait_ge(og_out, 2)
                    t = n - IN2 - 76
                    for e in range(4):
                        o = reg2[:, t, T * e:T * e + T]
                        ins = dve.scalar_tensor_tensor(o, o, hrs[:, 4 * t + e:4 * t + e + 1], gr[:, t, T * e:T * e + T],
                                                       ALU.mult, ALU.mult)
                    ins.then_inc(o_scaled, 1)
                head_steps(n, HEAD2, 12)
                if n in OSPLIT:
                    blk = n >= IN2
                    for pair in OSPLIT[n]:
                        dve.wait_ge(ohi_ready, OSPLIT_ORDER.index(pair, 8 * blk) + 1)
                        for kt in (2 * pair, 2 * pair + 1):
                            ins = dve.tensor_tensor(x_lo[:, kt, :], o_turned_at(kt, int(blk)), x_hi[:, kt, :].bitcast(F32),
                                                    ALU.subtract)
                        ins.then_inc(olo_ready, 1)
                if n in ends and (OUT1 <= n < OUT1_END or OUT2 <= n < OUT2_END):
                    q = ends[n]
                    dve.wait_ge(mm_done, n + 1)
                    first_q = OUT1_Q if n < OUT1_END else OUT2_Q
                    add_panel(q, (q - first_q) % 4 * W).then_inc(panel_out[q % 2], 1)
                if PLE <= n < PLE_END and n in ends and (ends[n] - PLE_Q) % 2 == 1:
                    q = ends[n]
                    j = (q - PLE_Q) // 2
                    dve.wait_ge(panel_out[q % 2], q // 2 + 1)
                    dve.wait_ge(panel_out[(q - 1) % 2], (q - 1) // 2 + 1)
                    link(dve.tensor_tensor(gate_n[:, :, :], gate_n[:, :, :], pn[:, :, :], ALU.mult))
                    to = h[:, :, W * j:W * j + W]
                    ins = dve.tensor_tensor(to, to, gate_n[:, :, :], ALU.add)
                    ins.then_inc(ple_added, 1)
                for k in range(len(TURN)):
                    if n == split_slot(k):
                        turned_lo(k)
                if TAIL2 < n and (n - TAIL2) % 2 == 0:
                    gain_final((n - TAIL2) // 2 - 1)
                if n == TAIL1 + 1:
                    dve.wait_ge(phi_ready, 1)
                    dve.tensor_tensor(p_lo[:, :, :].rearrange("p a n -> p (a n)"), mb[:, 2, :],
                                      p_hi[:, :, :].rearrange("p a n -> p (a n)").bitcast(F32), ALU.subtract)\
                        .then_inc(plo_ready, 1)

            def split_ahead(n):
                m = n + AHEAD
                if m < TOTAL:
                    per, width = shape_of(m)
                    split_lo(m, m, None, per, width)

            def straight_part(a, z):
                for n in range(a, z):
                    split_ahead(n)
                    beside(n)

            def ffn_part(which, base, base_q):
                groups = NG * which

                def group(i, first, last):
                    at = base if first else base + 16
                    qq = base_q if first else base_q + 2
                    if last:
                        at += (NG - 1) * GRP - 16
                        qq += 6 * (NG - 1) - 2
                    gi = 0 if first else 1

                    def split_hidden():
                        dve.wait_ge(hhi_ready, groups + NG if last else grown(groups + 1, i, 1))
                        src = (cv[:, :, :] if which == 0 else mb[:, 0:2, :]).rearrange("p a n -> p (a n)")
                        dve.tensor_tensor(h_lo[:, :, :].rearrange("p a n -> p (a n)"), src,
                                          h_hi[:, :, :].rearrange("p a n -> p (a n)").bitcast(F32), ALU.subtract)\
                            .then_inc(hlo_ready, 1)

                    if last:
                        split_hidden()
                    for c in range(16 if last else 0, 16 if first else GRP):
                        n = chunk_of(at + c, i)
                        if last:
                            split_ahead(at + c)
                        else:
                            split_lo(chunk_of(at + c + AHEAD, i), at + c + AHEAD, i, 2, W)
                        if c == 0 and not first and not last:
                            split_hidden()
                        if which == 0 and c == 11:
                            dve.wait_ge(conv_begun, grown(gi + 1, i, 1))
                            for back in (1, 2):
                                for ft in range(FT):
                                    at_f = ft if first else i * FT + (FT + ft)
                                    ins = dve.scalar_tensor_tensor(
                                        cv[:, ft, back:T], mb[:, ft // 2, T * (ft % 2):T * (ft % 2) + T - back],
                                        conv[:, 2 - back, bass.ds(at_f, 1)], cv[:, ft, back:T], ALU.mult, ALU.add)
                                if back == 1:
                                    ins.then_inc(conv_first, 1)
                                    dve.wait_ge(conv_first, grown(gi + 1, i, 1))
                            ins.then_inc(conv_done, 1)
                        if which == 1 and c == 15:
                            dve.wait_ge(mm_done, n + 1)
                            dve.wait_ge(panel_out[qq % 2], grown(qq // 2 + 1, i, 3))
                            if not first:
                                dve.wait_ge(up_turned, grown(groups + gi, i, 1))
                            for t in range(TB):
                                ins = dve.scalar_tensor_tensor(up_n[:, t, :], panel_in(t, qq + 1), rstd[4][:, t:t + 1],
                                                               gate_n[:, t, :], ALU.mult, ALU.mult)
                            ins.then_inc(panel_out[(qq + 1) % 2], 1)
                        if which == 0 and (c == 18 and not last or c == 15 and first):
                            dve.wait_ge(up_turned, grown(gi + 1, i, 1))
                            dve.wait_ge(gelu_done, grown(gi + 1, i, 1))
                            flat = cv[:, :, :].rearrange("p a n -> p (a n)")
                            dve.tensor_tensor(flat, flat, mb[:, 2:4, :].rearrange("p a n -> p (a n)"), ALU.mult)\
                                .then_inc(prod_done, 1)
                        if c >= 17 and c % 2 == 1:
                            part = (c - 17) // 2
                            dve.wait_ge(mm_done, n + 1)
                            add_panel(qq + 2 + part, part * W).then_inc(panel_out[(qq + part) % 2], 1)
                        if first or last:
                            beside(at + c)

                group(None, True, False)
                with dve.Fori(0, NG - 1) as i:
                    group(i, False, False)
                group(None, False, True)

            dve.wait_ge(gain_out, 1)
            beside(-2)
            split_ahead(0 - AHEAD)
            beside(-1)
            for n in range(1, AHEAD):
                split_ahead(n - AHEAD)
            straight_part(IN1, FFN1)
            ffn_part(0, FFN1, FFN1_Q)
            straight_part(PLE, FFN2)
            ffn_part(1, FFN2, FFN2_Q)
            gain_final(3)
            sum_squares(5)
            dve.wait_ge(rstd_ready, 6)
            for c in (0, D // 2):
                part = result[:, 0, c:c + D // 2]
                dve.tensor_scalar(part, part, rstd[5][:, 0:1], None, ALU.mult).then_inc(fin_done, 1)


NAMES = ["x", "p", "attn_norm", "w_in", "fox_bf", "lb_logits", "hgrn_onorm", "fox_qnorm", "fox_knorm",
         "moba_qnorm", "moba_knorm", "w_out", "ffn_norm", "w_gate", "w_up", "conv_w", "conv_b", "w_down",
         "ple_norm", "w_ple_gate", "w_ple_proj", "attn_norm_w_2", "w_in_2", "rel_bias_table_2",
         "gla_gate_w_fwd_2", "gla_gate_b_fwd_2", "gla_gate_w_bwd_2", "gla_gate_b_bwd_2", "gla_norm_w_2",
         "w_out_2", "ffn_norm_w_2", "w_gate_2", "w_up_2", "w_down_2", "final_norm_w_2"]


def kernel(**inputs):
    import concourse.bacc as bacc
    from concourse.bass_utils import run_bass_kernel_spmd

    nc = bacc.Bacc("TRN2", target_bir_lowering=False, num_devices=1)
    arrays, aps = {}, {}

    def give(name, a):
        arrays[name] = a
        return nc.dram_tensor(name, a.shape, mybir.dt.from_np(a.dtype), kind="ExternalInput").ap()

    for name in NAMES:
        aps[name] = give(f"in_{name}", np.ascontiguousarray(inputs[name]))
    cf, masks, hot = shape_constants()
    consts = [give("const_f", cf), give("const_m", masks), give("const_hot", hot)]
    out = nc.dram_tensor("out", (1, T, D), F32, kind="ExternalOutput").ap()
    build(nc, aps, out, *consts)
    r = run_bass_kernel_spmd(nc, [arrays], core_ids=[0])
    return r.results[0]["out"]
```
